# Optimizing a Trainium2 kernel written in Bass

```python
import jax, jax.numpy as jnp
from jax import lax
import numpy as np

D_MODEL = 1024
BATCH = 1
SEQ = 256
DEPTH = 2

N_A_LAYERS = DEPTH // 2
N_B_LAYERS = DEPTH - N_A_LAYERS
FOX_HEADS = 16
FOX_HEAD_DIM = D_MODEL // FOX_HEADS
FOX_WIDTH = FOX_HEADS * FOX_HEAD_DIM
FOX_IN_COLS = 3 * FOX_WIDTH + FOX_HEADS
MLA_HEADS = 8
QK_NOPE_DIM = 128
QK_ROPE_DIM = 64
V_HEAD_DIM = 128
Q_LORA_RANK = 384
KV_LORA_RANK = 256
ROPE_BASE = 10000.0
D_FF = 4 * D_MODEL
Q_BLOCK = 128
EPS = 1e-6


def rms_norm(x, g):
    xf = x.astype(jnp.float32)
    y = xf * lax.rsqrt(jnp.mean(xf * xf, axis=-1, keepdims=True) + EPS)
    return (y * g.astype(jnp.float32)).astype(x.dtype)

def sq_relu_mlp(h, w_up, w_down):
    return jnp.square(jax.nn.relu(h @ w_up)) @ w_down

def rope_tables(seq_len, dim):
    inv = 1.0 / (ROPE_BASE ** (jnp.arange(0, dim, 2, dtype=jnp.float32) / dim))
    ang = jnp.arange(seq_len, dtype=jnp.float32)[:, None] * inv[None, :]
    return jnp.cos(ang), jnp.sin(ang)

def apply_rope(t, cos, sin):
    cos = cos.astype(t.dtype)
    sin = sin.astype(t.dtype)
    half = t.shape[-1] // 2
    t1, t2 = t[..., :half], t[..., half:]
    return jnp.concatenate([t1 * cos - t2 * sin, t2 * cos + t1 * sin], axis=-1)

def causal_block_attention(logits_fn, q_parts, v):
    B, S = v.shape[0], v.shape[1]
    nb = S // Q_BLOCK
    blocks = tuple(jnp.moveaxis(t.reshape((B, nb, Q_BLOCK) + t.shape[2:]), 1, 0) for t in q_parts)
    kpos = jnp.arange(S)

    def one_block(args):
        i, qb = args
        logits = logits_fn(qb)
        qpos = i * Q_BLOCK + jnp.arange(Q_BLOCK)
        logits = jnp.where(kpos[None, :] <= qpos[:, None], logits, -jnp.inf)
        p = jax.nn.softmax(logits, axis=-1).astype(v.dtype)
        return jnp.einsum('bhqk,bkhd->bqhd', p, v)

    out = lax.map(one_block, (jnp.arange(nb), blocks))
    return jnp.moveaxis(out, 0, 1).reshape((B, S) + out.shape[3:])

def fox_mixer(h, w_in, b_f, w_out):
    B, S, _ = h.shape
    proj = h @ w_in
    q = proj[..., :FOX_WIDTH].reshape(B, S, FOX_HEADS, FOX_HEAD_DIM)
    k = proj[..., FOX_WIDTH:2 * FOX_WIDTH].reshape(B, S, FOX_HEADS, FOX_HEAD_DIM)
    v = proj[..., 2 * FOX_WIDTH:3 * FOX_WIDTH].reshape(B, S, FOX_HEADS, FOX_HEAD_DIM)
    f_logit = proj[..., 3 * FOX_WIDTH:].astype(jnp.float32) + b_f.astype(jnp.float32)
    cum = jnp.cumsum(jax.nn.log_sigmoid(f_logit), axis=1)
    c_keys = jnp.transpose(cum, (0, 2, 1))
    scale = FOX_HEAD_DIM ** -0.5

    def logits_fn(qb):
        q_blk, c_blk = qb
        s = jnp.einsum('bqhd,bkhd->bhqk', q_blk, k, preferred_element_type=jnp.float32) * scale
        return s + jnp.transpose(c_blk, (0, 2, 1))[..., None] - c_keys[:, :, None, :]

    ctx = causal_block_attention(logits_fn, (q, cum), v)
    return ctx.reshape(B, S, FOX_WIDTH) @ w_out

def mla_shared_kv(stream, kv_norm_g, w_kv_a, kv_a_norm_g, w_kv_b, cos, sin):
    B, S, _ = stream.shape
    src = rms_norm(stream, kv_norm_g)
    kv_a = src @ w_kv_a
    c_kv = rms_norm(kv_a[..., :KV_LORA_RANK], kv_a_norm_g)
    k_rope = apply_rope(kv_a[..., KV_LORA_RANK:], cos, sin)
    kv_b = (c_kv @ w_kv_b).reshape(B, S, MLA_HEADS, QK_NOPE_DIM + V_HEAD_DIM)
    k_nope = kv_b[..., :QK_NOPE_DIM]
    v = kv_b[..., QK_NOPE_DIM:]
    return k_nope, k_rope, v

def mla_mixer(h, w_q_a, q_a_norm_g, w_q_b, w_out, k_nope, k_rope, v, cos, sin):
    B, S, _ = h.shape
    c_q = rms_norm(h @ w_q_a, q_a_norm_g)
    q = (c_q @ w_q_b).reshape(B, S, MLA_HEADS, QK_NOPE_DIM + QK_ROPE_DIM)
    q_nope = q[..., :QK_NOPE_DIM]
    q_rope = apply_rope(q[..., QK_NOPE_DIM:], cos[:, None, :], sin[:, None, :])
    scale = (QK_NOPE_DIM + QK_ROPE_DIM) ** -0.5

    def logits_fn(qb):
        qn, qr = qb
        s = jnp.einsum('bqhd,bkhd->bhqk', qn, k_nope, preferred_element_type=jnp.float32)
        s = s + jnp.einsum('bqhr,bkr->bhqk', qr, k_rope, preferred_element_type=jnp.float32)
        return s * scale

    ctx = causal_block_attention(logits_fn, (q_nope, q_rope), v)
    return ctx.reshape(B, S, MLA_HEADS * V_HEAD_DIM) @ w_out

def first_inputs(seed: int = 0) -> dict:
    key = jax.random.key(seed)
    ks = jax.random.split(key, 24)

    def w(k, shape, fan_in):
        return jax.random.normal(k, shape, jnp.float32) * (fan_in ** -0.5)

    def gain(k, shape):
        return 1.0 + 0.02 * jax.random.normal(k, shape, jnp.float32)

    return {
        "x": jax.random.normal(ks[0], (BATCH, SEQ, D_MODEL), jnp.float32),
        "norm_mix_g": gain(ks[1], (DEPTH, D_MODEL)),
        "norm_ffn_g": gain(ks[2], (DEPTH, D_MODEL)),
        "fox_w_in": w(ks[3], (N_A_LAYERS, D_MODEL, FOX_IN_COLS), D_MODEL),
        "fox_b_f": 1.0 + 0.1 * jax.random.normal(ks[4], (N_A_LAYERS, FOX_HEADS), jnp.float32),
        "fox_w_out": w(ks[5], (N_A_LAYERS, FOX_WIDTH, D_MODEL), FOX_WIDTH),
        "kv_norm_g": gain(ks[6], (D_MODEL,)),
        "mla_w_kv_a": w(ks[7], (D_MODEL, KV_LORA_RANK + QK_ROPE_DIM), D_MODEL),
        "mla_kv_a_norm_g": gain(ks[8], (KV_LORA_RANK,)),
        "mla_w_kv_b": w(ks[9], (KV_LORA_RANK, MLA_HEADS * (QK_NOPE_DIM + V_HEAD_DIM)), KV_LORA_RANK),
        "mla_w_q_a": w(ks[10], (N_B_LAYERS, D_MODEL, Q_LORA_RANK), D_MODEL),
        "mla_q_a_norm_g": gain(ks[11], (N_B_LAYERS, Q_LORA_RANK)),
        "mla_w_q_b": w(ks[12], (N_B_LAYERS, Q_LORA_RANK, MLA_HEADS * (QK_NOPE_DIM + QK_ROPE_DIM)), Q_LORA_RANK),
        "mla_w_out": w(ks[13], (N_B_LAYERS, MLA_HEADS * V_HEAD_DIM, D_MODEL), MLA_HEADS * V_HEAD_DIM),
        "ffn_w_up": w(ks[14], (DEPTH, D_MODEL, D_FF), D_MODEL),
        "ffn_w_down": w(ks[15], (DEPTH, D_FF, D_MODEL), D_FF),
        "final_norm_g": gain(ks[16], (D_MODEL,)),
    }

def first_block(x, norm_mix_g, norm_ffn_g, fox_w_in, fox_b_f, fox_w_out, kv_norm_g,
              mla_w_kv_a, mla_kv_a_norm_g, mla_w_kv_b, mla_w_q_a, mla_q_a_norm_g,
              mla_w_q_b, mla_w_out, ffn_w_up, ffn_w_down, final_norm_g):
    S = x.shape[1]
    cos, sin = rope_tables(S, QK_ROPE_DIM)
    k_nope = k_rope = v_shared = None
    for layer in range(DEPTH):
        h = rms_norm(x, norm_mix_g[layer])
        if layer < N_A_LAYERS:
            x = x + fox_mixer(h, fox_w_in[layer], fox_b_f[layer], fox_w_out[layer])
        else:
            b = layer - N_A_LAYERS
            x = x + mla_mixer(h, mla_w_q_a[b], mla_q_a_norm_g[b], mla_w_q_b[b], mla_w_out[b],
                              k_nope, k_rope, v_shared, cos, sin)
        x = x + sq_relu_mlp(rms_norm(x, norm_ffn_g[layer]), ffn_w_up[layer], ffn_w_down[layer])
        if layer == N_A_LAYERS - 1:
            k_nope, k_rope, v_shared = mla_shared_kv(x, kv_norm_g, mla_w_kv_a, mla_kv_a_norm_g,
                                                     mla_w_kv_b, cos, sin)
    return rms_norm(x, final_norm_g)


N_MIXERS = 2
GLA_HEADS = 4
GLA_KEY_DIM = D_MODEL // 2
GLA_VAL_DIM = D_MODEL
GLA_HEAD_K = GLA_KEY_DIM // GLA_HEADS
GLA_HEAD_V = GLA_VAL_DIM // GLA_HEADS
GLA_GATE_RANK = 16
GLA_GATE_TAU = 16.0
GLA_CHUNK = 64
GLA_IN_DIM = 2 * GLA_KEY_DIM + 2 * GLA_VAL_DIM + GLA_GATE_RANK
SC_WIDTH = D_MODEL
CONV_WIDTH = 3
D_FF_2 = ((8 * D_MODEL // 3 + 255) // 256) * 256
N_GLA = (DEPTH + 1) // 2
N_SC = DEPTH // 2
RMS_EPS = 1e-6


def rmsnorm(x, g):
    x32 = x.astype(jnp.float32)
    y = x32 * lax.rsqrt(jnp.mean(x32 * x32, axis=-1, keepdims=True) + RMS_EPS)
    return y.astype(x.dtype) * g

def causal_dwconv(x, w):
    T = x.shape[1]
    K = w.shape[1]
    xp = jnp.pad(x, ((0, 0), (K - 1, 0), (0, 0)))
    y = xp[:, 0:T] * w[:, 0]
    for j in range(1, K):
        y = y + xp[:, j:j + T] * w[:, j]
    return y

def to_chunks(t, n_heads, head_dim):
    B, T, _ = t.shape
    n = T // GLA_CHUNK
    return t.reshape(B, n, GLA_CHUNK, n_heads, head_dim).transpose(0, 3, 1, 2, 4)

def gla_mixer(h, w_in, w_gate_up, b_gate, head_norm_g, w_out):
    B, T, _ = h.shape
    proj = h @ w_in
    s1 = GLA_KEY_DIM
    s2 = 2 * GLA_KEY_DIM
    s3 = s2 + GLA_VAL_DIM
    s4 = s3 + GLA_VAL_DIM
    q, k, v, g, a_low = proj[..., :s1], proj[..., s1:s2], proj[..., s2:s3], proj[..., s3:s4], proj[..., s4:]
    log_a = jax.nn.log_sigmoid((a_low @ w_gate_up + b_gate).astype(jnp.float32)) / GLA_GATE_TAU

    qc = to_chunks(q.astype(jnp.float32) * (GLA_HEAD_K ** -0.5), GLA_HEADS, GLA_HEAD_K)
    kc = to_chunks(k.astype(jnp.float32), GLA_HEADS, GLA_HEAD_K)
    vc = to_chunks(v.astype(jnp.float32), GLA_HEADS, GLA_HEAD_V)
    lc = to_chunks(log_a, GLA_HEADS, GLA_HEAD_K)

    bcum = jnp.cumsum(lc, axis=3)
    b_last = bcum[..., -1, :]
    q_in = qc * jnp.exp(bcum)
    k_in = kc * jnp.exp(-bcum)
    mask = jnp.tril(jnp.ones((GLA_CHUNK, GLA_CHUNK), dtype=bool))
    scores = jnp.where(mask, jnp.einsum('bhncd,bhnsd->bhncs', q_in, k_in), 0.0)
    o_intra = jnp.einsum('bhncs,bhnse->bhnce', scores, vc)
    k_dec = kc * jnp.exp(b_last[..., None, :] - bcum)
    chunk_kv = jnp.einsum('bhncd,bhnce->bhnde', k_dec, vc)

    def step(S, inp):
        q_n, kv_n, dec_n = inp
        o_n = jnp.einsum('bhcd,bhde->bhce', q_n, S)
        S = dec_n[..., None] * S + kv_n
        return S, o_n

    S0 = jnp.zeros((B, GLA_HEADS, GLA_HEAD_K, GLA_HEAD_V), jnp.float32)
    xs = (q_in.transpose(2, 0, 1, 3, 4), chunk_kv.transpose(2, 0, 1, 3, 4), jnp.exp(b_last).transpose(2, 0, 1, 3))
    _, o_inter = lax.scan(step, S0, xs)
    o = o_intra + o_inter.transpose(1, 2, 0, 3, 4)
    o = o.transpose(0, 2, 3, 1, 4).reshape(B, T, GLA_HEADS, GLA_HEAD_V)
    o = o * lax.rsqrt(jnp.mean(o * o, axis=-1, keepdims=True) + RMS_EPS)
    o = o.astype(h.dtype) * head_norm_g
    o = o.reshape(B, T, GLA_VAL_DIM) * jax.nn.silu(g)
    return o @ w_out

def short_conv_mixer(h, w_in, conv_w, w_out):
    proj = h @ w_in
    b, c, u = proj[..., :SC_WIDTH], proj[..., SC_WIDTH:2 * SC_WIDTH], proj[..., 2 * SC_WIDTH:]
    y = b * causal_dwconv(c * u, conv_w)
    return y @ w_out

def conv_ffn(h, w_up, conv_w, w_down):
    up = causal_dwconv(h @ w_up, conv_w)
    a, u = up[..., :D_FF_2], up[..., D_FF_2:]
    return (jax.nn.silu(a) * u) @ w_down

def second_inputs(seed: int = 0) -> dict:
    key = jax.random.key(seed)
    ks = jax.random.split(key, 16)
    f32 = jnp.float32
    out_scale = (2.0 * DEPTH) ** -0.5
    nrm = lambda k, shape, s: jax.random.normal(k, shape, f32) * s
    return {
        "x": nrm(ks[0], (BATCH, SEQ, D_MODEL), 1.0),
        "norm_mix_g": 1.0 + nrm(ks[1], (DEPTH, D_MODEL), 0.02),
        "norm_ffn_g": 1.0 + nrm(ks[2], (DEPTH, D_MODEL), 0.02),
        "gla_w_in": nrm(ks[3], (N_GLA, D_MODEL, GLA_IN_DIM), D_MODEL ** -0.5),
        "gla_w_gate_up": nrm(ks[4], (N_GLA, GLA_GATE_RANK, GLA_KEY_DIM), GLA_GATE_RANK ** -0.5),
        "gla_b_gate": nrm(ks[5], (N_GLA, GLA_KEY_DIM), 0.1),
        "gla_head_norm_g": 1.0 + nrm(ks[6], (N_GLA, GLA_HEADS, GLA_HEAD_V), 0.02),
        "gla_w_out": nrm(ks[7], (N_GLA, GLA_VAL_DIM, D_MODEL), GLA_VAL_DIM ** -0.5 * out_scale),
        "sc_w_in": nrm(ks[8], (N_SC, D_MODEL, 3 * SC_WIDTH), D_MODEL ** -0.5),
        "sc_conv_w": nrm(ks[9], (N_SC, SC_WIDTH, CONV_WIDTH), CONV_WIDTH ** -0.5),
        "sc_w_out": nrm(ks[10], (N_SC, SC_WIDTH, D_MODEL), SC_WIDTH ** -0.5 * out_scale),
        "ffn_w_up": nrm(ks[11], (DEPTH, D_MODEL, 2 * D_FF_2), D_MODEL ** -0.5),
        "ffn_conv_w": nrm(ks[12], (DEPTH, 2 * D_FF_2, CONV_WIDTH), CONV_WIDTH ** -0.5),
        "ffn_w_down": nrm(ks[13], (DEPTH, D_FF_2, D_MODEL), D_FF_2 ** -0.5 * out_scale),
        "final_norm_g": 1.0 + nrm(ks[14], (D_MODEL,), 0.02),
    }

def second_block(x, norm_mix_g, norm_ffn_g, gla_w_in, gla_w_gate_up, gla_b_gate, gla_head_norm_g, gla_w_out,
              sc_w_in, sc_conv_w, sc_w_out, ffn_w_up, ffn_conv_w, ffn_w_down, final_norm_g):
    for i in range(DEPTH):
        h = rmsnorm(x, norm_mix_g[i])
        j = i // N_MIXERS
        if i % N_MIXERS == 0:
            x = x + gla_mixer(h, gla_w_in[j], gla_w_gate_up[j], gla_b_gate[j], gla_head_norm_g[j], gla_w_out[j])
        else:
            x = x + short_conv_mixer(h, sc_w_in[j], sc_conv_w[j], sc_w_out[j])
        h = rmsnorm(x, norm_ffn_g[i])
        x = x + conv_ffn(h, ffn_w_up[i], ffn_conv_w[i], ffn_w_down[i])
    return rmsnorm(x, final_norm_g)


def setup_inputs(seed=0):
    out = dict(first_inputs(seed))
    for name, value in second_inputs(seed + 1).items():
        if name != "x":
            out[name + "_2"] = value
    return out


def reference(
    x, norm_mix_g, norm_ffn_g, fox_w_in, fox_b_f, fox_w_out, kv_norm_g, mla_w_kv_a,
    mla_kv_a_norm_g, mla_w_kv_b, mla_w_q_a, mla_q_a_norm_g, mla_w_q_b, mla_w_out, ffn_w_up,
    ffn_w_down, final_norm_g, norm_mix_g_2, norm_ffn_g_2, gla_w_in_2, gla_w_gate_up_2,
    gla_b_gate_2, gla_head_norm_g_2, gla_w_out_2, sc_w_in_2, sc_conv_w_2, sc_w_out_2,
    ffn_w_up_2, ffn_conv_w_2, ffn_w_down_2, final_norm_g_2,
):
    x = first_block(
        x, norm_mix_g, norm_ffn_g, fox_w_in, fox_b_f, fox_w_out, kv_norm_g, mla_w_kv_a,
        mla_kv_a_norm_g, mla_w_kv_b, mla_w_q_a, mla_q_a_norm_g, mla_w_q_b, mla_w_out, ffn_w_up,
        ffn_w_down, final_norm_g,
    )
    return second_block(
        x, norm_mix_g_2, norm_ffn_g_2, gla_w_in_2, gla_w_gate_up_2, gla_b_gate_2,
        gla_head_norm_g_2, gla_w_out_2, sc_w_in_2, sc_conv_w_2, sc_w_out_2, ffn_w_up_2,
        ffn_conv_w_2, ffn_w_down_2, final_norm_g_2,
    )


_drawn_inputs = setup_inputs


def setup_inputs(seed=0):
    import zlib

    import numpy as np

    out = dict(_drawn_inputs(seed))
    spreads = {}
    factors = {'kv_norm_g': 7.687,
     'mla_kv_a_norm_g': 7.947,
     'mla_q_a_norm_g': 8.0,
     'norm_ffn_g_2': 4.701,
     'gla_head_norm_g_2': 8.0,
     'final_norm_g_2': 2.861}
    for name, (base, spread) in spreads.items():
        noise = np.random.default_rng([zlib.crc32(name.encode()), seed]).standard_normal(out[name].shape)
        drawn = base * np.exp(spread * noise) if base else spread * noise
        out[name] = __import__('jax').numpy.asarray(drawn.astype(out[name].dtype))
    for name, factor in factors.items():
        out[name] = (out[name] * factor).astype(out[name].dtype)
    return out
```

```python
from contextlib import ExitStack

import numpy as np

import concourse.bass as bass
from concourse import mybir

F32 = mybir.dt.float32
F32R = mybir.dt.float32r
U32 = mybir.dt.uint32
ALU = mybir.AluOpType
ACT = mybir.ActivationFunctionType
ds = bass.ds

P = 128
T = 256
TT = T // P
D = 1024
KD = D // P
EPS = 1e-6
FOX_H, FOX_DH = 16, 64
MLA_H, NOPE, ROPE, VDIM = 8, 128, 64, 128
QLORA, KVLORA = 384, 256
DFF = 4 * D
DFF2 = 2816
NT2 = DFF2 // P
GLA_H, GLA_DK, GLA_DV, GLA_C = 4, 128, 256, 64
GATE_RANK, GATE_TAU = 16, 16.0
FOX_SCALE = FOX_DH ** -0.5
MLA_SCALE = (NOPE + ROPE) ** -0.5
GLA_SCALE = GLA_DK ** -0.5
MASKED = -1.0e30

CW = 256
CHUNK = KD * CW
RAW_SLOTS = 4
W_SLOTS = 2
AHEAD = 3
CD_K = (6, 6, 5, 5)

STAGES = [("FV", 4), ("FG", 1), ("FQK", 8), ("FO", 4), ("U0", 16), ("D0", 16), ("KVQ", 3), ("KB", 1), ("VB", 1),
          ("QB", 3), ("MO", 4), ("U1", 16), ("D1", 16), ("GA", 1), ("GQK", 4), ("GV", 4), ("GG", 4), ("GO", 4),
          ("CU0", 22), ("CD0", 16), ("SI", 12), ("SO", 4), ("CU1", 22), ("CD1", 16)]
C0 = {}
N_CHUNKS = 0
for _name, _n in STAGES:
    C0[_name] = N_CHUNKS
    N_CHUNKS += _n

VEC = {}
N_VEC = 0
for _name, _n in [("mix0", 8), ("ffn0", 8), ("kv", 8), ("mix1", 8), ("ffn1", 8), ("final1", 8), ("mix2", 8),
                  ("ffn2", 8), ("mix3", 8), ("ffn3", 8), ("final2", 8), ("kv_a", 2), ("q_a", 3), ("head", 8),
                  ("sc_conv", 24), ("conv0", 132), ("conv1", 132)]:
    VEC[_name] = N_VEC
    N_VEC += _n

CON = {}
N_CON = 0
for _name, _n in [("ones", 128), ("ident", 128), ("mask", 256), ("tri", 512), ("tri_chunk", 128), ("cos", 256),
                  ("sin", 256), ("rot", 128), ("chunk_mask", 128)]:
    CON[_name] = N_CON
    N_CON += _n


def shape_constants():
    con = np.zeros((P, N_CON), np.float32)
    at = lambda name, n: con[:, CON[name]:CON[name] + n]
    i = np.arange(P)
    at("ones", 128)[:] = 1.0
    at("ident", 128)[:] = np.eye(P)
    at("mask", 256)[:, 128:] = np.where(i[None, :] <= i[:, None], 0.0, MASKED)
    tri = np.where(np.arange(T)[:, None] <= np.arange(T)[None, :], -1.0 / FOX_SCALE, 0.0)
    at("tri", 512)[:] = tri.reshape(TT, P, T).transpose(1, 0, 2).reshape(P, 512)
    same = (i[:, None] // GLA_C) == (i[None, :] // GLA_C)
    upto = same & (i[:, None] <= i[None, :])
    at("tri_chunk", 128)[:] = np.where(upto, 1.0 / GATE_TAU, 0.0)
    at("chunk_mask", 128)[:] = np.where(upto, 1.0, 0.0)
    inv = (1.0 / (np.float32(10000.0) ** (np.arange(0, ROPE, 2, dtype=np.float32) / np.float32(ROPE)))).astype(np.float32)
    ang = np.arange(T, dtype=np.float32)[:, None] * inv[None, :]
    at("cos", 256)[:] = np.tile(np.cos(ang).T, (4, 1))
    at("sin", 256)[:] = np.tile(np.sin(ang).T, (4, 1))
    half = ROPE // 2
    for m in range(P):
        if m % ROPE < half:
            at("rot", 128)[m + half, m] = -1.0
        else:
            at("rot", 128)[m - half, m] = 1.0
    sel = np.zeros((P, FOX_H, P), np.float32)
    for h in range(FOX_H):
        sel[64 * (h % 2) + h, h] = 1.0
        sel[64 * (h % 2) + 32 + h, h] = 1.0
    return con, sel.reshape(P, FOX_H * P)


def build(nc, io):
    ctx = ExitStack()
    with ctx:
        used = [16512]

        def sb(name, shape, dt=F32, at=None):
            n = int(np.prod(shape[1:])) * 4
            if at is None:
                at = used[0]
                used[0] += (n + 31) // 32 * 32
            return nc.alloc_sbuf_tensor_at(name, shape, dt, offset=at)

        def bank(name):
            return ctx.enter_context(nc.psum_tensor(name, [P, 512], F32))

        def sem(name):
            return ctx.enter_context(nc.semaphore(name))

        w_raw = sb("w_raw", [P, RAW_SLOTS, CHUNK])
        w_hi = sb("w_hi", [P, W_SLOTS, CHUNK], F32R)
        w_lo = sb("w_lo", [P, W_SLOTS, CHUNK], F32R)
        x = sb("x", [P, KD, T])
        act_a = sb("act_a", [P, KD, 2, T], F32R)
        act_b = sb("act_b", [P, KD, 2, T], F32R)
        vec = sb("vec", [P, N_VEC])
        con = sb("con", [P, N_CON])
        ssq = sb("ssq", [P, T])
        sqt = sb("sqt", [P, T])
        var = sb("var", [P, T + TT])
        std = sb("std", [P, T + TT])
        rstd = sb("rstd", [P, 3, T + TT])
        tmp = sb("tmp", [P, 4, T])
        tmp2 = sb("tmp2", [P, 4, T])
        rstd_sq = sb("rstd_sq", [P, T])
        g_last = sb("g_last", [P, GLA_H * (T // GLA_C)])
        arena = used[0]

        def overlay():
            used[0] = arena

        overlay()
        hid = sb("hid", [P, DFF // P, 2, T], F32R)
        end_hid = used[0]
        overlay()
        f_q = sb("f_q", [P, KD, T])
        f_k = sb("f_k", [P, KD, T])
        f_v = sb("f_v", [P, TT, D])
        f_logit = sb("f_logit", [P, 2, 384])
        f_prob = sb("f_prob", [P, 2, 384])
        f_probT = sb("f_probT", [P, 2, 384])
        f_sel = sb("f_sel", [P, FOX_H, P], F32R)
        f_sel_raw = sb("f_sel_raw", [P, FOX_H * P])
        f_cum = sb("f_cum", [P, T], F32R)
        f_bias = sb("f_bias", [P, FOX_H])
        f_z = sb("f_z", [P, TT, FOX_H])
        f_neg_abs = sb("f_neg_abs", [P, TT, FOX_H])
        f_exp = sb("f_exp", [P, TT, FOX_H])
        f_ln = sb("f_ln", [P, TT, FOX_H])
        f_ls = sb("f_ls", [P, TT, FOX_H])
        row_max = sb("row_max", [P, 2, 2])
        neg_max = sb("neg_max", [P, 2, 2])
        row_sum = sb("row_sum", [P, 2, 2])
        inv_sum = sb("inv_sum", [P, 2, 2])
        assert used[0] <= end_hid
        overlay()
        m_q = sb("m_q", [P, MLA_H, T])
        m_k = sb("m_k", [P, MLA_H, T])
        m_v = sb("m_v", [P, TT, D])
        m_qr_raw = sb("m_qr_raw", [P, 4, T])
        m_qr = sb("m_qr", [P, 4, T])
        m_kr_raw = sb("m_kr_raw", [P, T])
        m_kr = sb("m_kr", [P, T])
        m_lat = sb("m_lat", [P, 5, T])
        m_act = sb("m_act", [P, 5, 2, T], F32R)
        m_logit = sb("m_logit", [P, 2, 384])
        m_prob = sb("m_prob", [P, 2, 384])
        m_probT = sb("m_probT", [P, 2, 384])
        m_cos = sb("m_cos", [P, T])
        m_max = sb("m_max", [P, 2, 2])
        m_nmax = sb("m_nmax", [P, 2, 2])
        m_sum = sb("m_sum", [P, 2, 2])
        m_inv = sb("m_inv", [P, 2, 2])
        assert used[0] <= end_hid
        overlay()
        g_q = sb("g_q", [P, GLA_H, T])
        g_k = sb("g_k", [P, GLA_H, T])
        g_v = sb("g_v", [P, TT, D])
        g_z = sb("g_z", [P, TT, 512])
        g_e = sb("g_e", [P, TT, 512])
        g_s = sb("g_s", [P, 3, GLA_H, GLA_DV])
        g_eb = sb("g_eb", [P, GLA_H, T])
        g_ki = sb("g_ki", [P, GLA_H, T])
        g_kd = sb("g_kd", [P, GLA_H, T])
        g_qi = sb("g_qi", [P, GLA_H, T])
        g_kdT = sb("g_kdT", [P, TT, 512])
        g_sT = sb("g_sT", [P, TT, 512])
        g_aT = sb("g_aT", [GATE_RANK, T])
        end_gla = used[0]
        g_o = nc.alloc_sbuf_tensor_at("g_o", [P, KD, T], F32, offset=arena)
        g_g = nc.alloc_sbuf_tensor_at("g_g", [P, KD, T], F32, offset=arena + 16384)
        overlay()
        used[0] = max(end_hid, end_gla)
        g_up = sb("g_up", [GATE_RANK, 512])
        g_bias = sb("g_bias", [P, 512])
        s_c = sb("s_c", [P, 2, T])
        assert used[0] <= nc.sbuf_usable_end, used[0]

        gemm = [bank(f"gemm{i}") for i in range(4)]
        score = [bank("score0"), bank("score1")]
        trans = bank("trans")
        misc = bank("misc")

        ones = con[:, CON["ones"]:CON["ones"] + 128]
        ident = con[:, CON["ident"]:CON["ident"] + 128]
        mask = con[:, CON["mask"]:CON["mask"] + 256]
        tri = con[:, CON["tri"]:CON["tri"] + 512].rearrange("p (t n) -> p t n", t=TT)
        tri_chunk = con[:, CON["tri_chunk"]:CON["tri_chunk"] + 128]
        cos_t = con[:, CON["cos"]:CON["cos"] + 256]
        sin_t = con[:, CON["sin"]:CON["sin"] + 256]
        rot = con[:, CON["rot"]:CON["rot"] + 128]
        chunk_mask = con[:, CON["chunk_mask"]:CON["chunk_mask"] + 128].bitcast(U32)

        def gain(name, k):
            return vec[:, VEC[name] + k:VEC[name] + k + 1]

        x_landed = sem("x_landed")
        vec_landed = sem("vec_landed")
        con_landed = sem("con_landed")
        fox_small_landed = sem("fox_small_landed")
        gla_small_landed = sem("gla_small_landed")
        raw_landed = [sem(f"raw_landed{s}") for s in range(RAW_SLOTS)]
        w_hi_ready = sem("w_hi_ready")
        w_lo_ready = sem("w_lo_ready")
        half_done = sem("half_done")
        act_evac = sem("act_evac")
        dve_evac = sem("dve_evac")
        resid_ready = sem("resid_ready")
        act_hi_ready = sem("act_hi_ready")
        act_ready = sem("act_ready")
        pool_sq = sem("pool_sq")
        pool_sum = sem("pool_sum")
        stat_done = sem("stat_done")
        var_ready = sem("var_ready")
        std_ready = sem("std_ready")
        rstd_ready = sem("rstd_ready")
        sq_ready = sem("sq_ready")
        tap_ready = sem("tap_ready")
        tap_mid = sem("tap_mid")
        silu_ready = sem("silu_ready")
        gated_ready = sem("gated_ready")
        scores_done = sem("scores_done")
        logits_ready = sem("logits_ready")
        negmax_ready = sem("negmax_ready")
        probs_ready = sem("probs_ready")
        invsum_ready = sem("invsum_ready")
        probs_normed = sem("probs_normed")
        transposed = sem("transposed")
        probsT_ready = sem("probsT_ready")
        pv_done = sem("pv_done")
        gate_step = sem("gate_step")
        cum_done = sem("cum_done")
        cum_ready = sem("cum_ready")
        rot_done = sem("rot_done")
        rope_step = sem("rope_step")
        sel_ready = sem("sel_ready")
        gla_pe = sem("gla_pe")
        gla_act = sem("gla_act")
        gla_dve = sem("gla_dve")
        sc_ready = sem("sc_ready")
        dve_own = sem("dve_own")
        out_landed = sem("out_landed")

        STRAIGHT = (0, 0, 0)

        def halves_before(c, j, it=STRAIGHT):
            return 2 * c + j + 2 * it[1] * it[0]

        DE, AE = {}, {}
        n_d = n_a = 0
        for name, d, a in [("FV", 0, 8), ("FG", 2, 0), ("FQK", 16, 0), ("FO", 8, 0), ("U0", 0, 32), ("D0", 8, 0),
                           ("KVQ", 6, 0), ("KB", 8, 0), ("VB", 0, 4), ("QB", 12, 0), ("MO", 8, 0), ("U1", 0, 32),
                           ("D1", 8, 0), ("GA", 1, 0), ("GQK", 8, 0), ("GV", 0, 8), ("GG", 8, 0), ("GO", 8, 0),
                           ("CU0", 44, 0), ("CD0", 8, 0), ("SI", 16, 8), ("SO", 8, 0), ("CU1", 44, 0), ("CD1", 8, 0)]:
            DE[name], AE[name] = n_d, n_a
            n_d, n_a = n_d + d, n_a + a
        AT = {}
        n_t = 0
        for name, n in [("x", 8), ("fctx", 8), ("FO", 8), ("U0", 32), ("D0", 16), ("lat", 5), ("mctx", 8), ("MO", 8),
                        ("U1", 32), ("x1", 8), ("gla", 8), ("GO", 8), ("CU0", 22), ("CD0", 8), ("sc", 8), ("SO", 8),
                        ("CU1", 22)]:
            AT[name] = n_t
            n_t += n
        GT = {}
        n_t = 0
        for name, n in [("gla", 8), ("GO", 8), ("CU0", 22), ("SO", 8), ("CU1", 22)]:
            GT[name] = n_t
            n_t += n
        RT = {"D0": 0, "D1": 8, "x1": 16}
        SQ = {"U0": 0, "U1": 32}
        TURN = {}
        n_t = 0
        for name, n in [("FV", 8), ("FG", 2), ("FQK", 16), ("FO", 8), ("U0", 32), ("D0", 2), ("KVQ", 6), ("KB", 8),
                        ("VB", 4), ("QB", 12), ("MO", 8), ("U1", 32), ("D1", 2), ("GA", 1), ("GQK", 8), ("GV", 8),
                        ("GG", 8), ("GO", 8), ("CU0", 44), ("CD0", 2), ("SI", 24), ("SO", 8), ("CU1", 44), ("CD1", 2)]:
            TURN[name] = n_t
            n_t += n

        def bank_of(stage, n):
            return gemm[(TURN[stage] + n) % 4]

        def tmp_of(k):
            return (tmp, tmp2)[k // 4][:, k % 4, :]

        CV = {"CU0": 0, "SI": 44, "CU1": 52}
        SL = {"GG": 0, "CU0": 8, "CU1": 30}
        NORMS = {}
        n_t = 0
        for n, (name, tiles, tok, feats) in enumerate(
                [("mix0", 8, True, D), ("ffn0", 8, False, D), ("mix1", 8, False, D), ("kv_a", 2, True, KVLORA),
                 ("q_a", 3, False, QLORA), ("ffn1", 8, False, D), ("final1", 8, False, D), ("mix2", 8, True, D),
                 ("ffn2", 8, False, D), ("mix3", 8, False, D), ("ffn3", 8, False, D), ("final2", 8, False, D)]):
            NORMS[name] = (n, tiles, n_t, tok, feats)
            n_t += tiles
        ROOTS = [n for n in NORMS if n not in ("ffn0", "ffn1")]

        def rstd_of(name):
            return rstd[:, NORMS[name][0] % 3, :]

        def chunk_view(t, slot, kind):
            k = {"full": 8, "lat": 3, "kvb": 2}[kind]
            n = {"full": 256, "lat": 512, "kvb": 1024}[kind]
            return t[:, slot, 0:k * n].rearrange("p (k n) -> p k n", k=k)

        def kind_of(c):
            if C0["QB"] <= c < C0["MO"]:
                return "lat", 3
            if C0["KB"] <= c < C0["QB"]:
                return "kvb", 2
            for s in ("CD0", "CD1"):
                if C0[s] <= c < C0[s] + 16:
                    return "full", CD_K[(c - C0[s]) % 4]
            return "full", 8

        def half_view(t, slot, c, j):
            kind, nk = kind_of(c)
            v = chunk_view(t, slot, kind)
            w = {"full": 128, "lat": 256, "kvb": 512}[kind]
            return v[:, 0:nk, j * w:(j + 1) * w]

        def ahead(c, j):
            h = 2 * c + j + AHEAD
            return (h // 2, h % 2) if h < 2 * N_CHUNKS else None

        block = ctx.enter_context(nc.Block())

        @block.sync
        def _(sp):
            def load(c, parts, it=STRAIGHT):
                if c >= RAW_SLOTS:
                    sp.wait_ge(w_lo_ready, halves_before(c - RAW_SLOTS + 1, 0, it))
                assert len(parts) == 1
                for dst, src in parts:
                    sp.dma_start(dst, src).then_inc(raw_landed[c % RAW_SLOTS], 16)

            def ktiles(w):
                return w.rearrange("(k p) n -> p k n", p=P)

            def full(c):
                return chunk_view(w_raw, c % RAW_SLOTS, "full")

            def plain(stage, w, cols):
                for j, col in enumerate(cols):
                    c = C0[stage] + j
                    load(c, [(full(c), ktiles(w)[:, :, col:col + CW])])

            def up(stage, w):
                with sp.Fori(0, 4) as i:
                    for cc in range(4):
                        c = C0[stage] + cc
                        load(c, [(full(c), ktiles(w)[:, :, ds(i * (4 * CW) + cc * CW, CW)])], (i, 4, 8))

            def down(stage, w):
                with sp.Fori(0, 4) as i:
                    for cc in range(4):
                        c = C0[stage] + cc
                        load(c, [(full(c), ktiles(w)[:, 8 * cc:8 * cc + 8, ds(i * CW, CW)])], (i, 4, 2))

            def conv_up(stage, w):
                def body(i, cc, it):
                    c = C0[stage] + cc
                    col = (cc // 2) * CW + (cc % 2) * DFF2 + i * (2 * CW)
                    src = ktiles(w)[:, :, ds(col, CW)] if it[1] else ktiles(w)[:, :, col:col + CW]
                    load(c, [(full(c), src)], it)

                with sp.Fori(0, 5) as i:
                    for cc in range(4):
                        body(i, cc, (i, 4, 8))
                for cc in range(20, 22):
                    body(0, cc, STRAIGHT)

            def conv_down(stage, w):
                def body(i, cc, it):
                    c = C0[stage] + cc
                    k0, nk = sum(CD_K[:cc % 4]), CD_K[cc % 4]
                    cols = ds(i * CW, CW) if it[1] else slice((cc // 4) * CW, (cc // 4 + 1) * CW)
                    load(c, [(full(c)[:, 0:nk, :], ktiles(w)[:, k0:k0 + nk, cols])], it)

                with sp.Fori(0, 3) as i:
                    for cc in range(4):
                        body(i, cc, (i, 4, 2))
                for cc in range(12, 16):
                    body(0, cc, STRAIGHT)

            w = io["fox_w_in"][0]
            plain("FV", w, [2 * D + CW * j for j in range(4)])
            c = C0["FG"]
            load(c, [(full(c)[:, :, 0:FOX_H], ktiles(w)[:, :, 3 * D:3 * D + FOX_H])])
            plain("FQK", w, [CW * (j // 2) + D * (j % 2) for j in range(8)])
            plain("FO", io["fox_w_out"][0], [CW * j for j in range(4)])
            up("U0", io["ffn_w_up"][0])
            down("D0", io["ffn_w_down"][0])
            c = C0["KVQ"]
            wkv, wq = ktiles(io["mla_w_kv_a"]), ktiles(io["mla_w_q_a"][0])
            load(c, [(full(c), wkv[:, :, 0:KVLORA])])
            load(c + 1, [(full(c + 1), wq[:, :, 0:256])])
            sp.wait_ge(w_lo_ready, halves_before(c + 2 - RAW_SLOTS + 1, 0))
            for dst, src in [(full(c + 2)[:, :, 0:64], wkv[:, :, KVLORA:KVLORA + ROPE]),
                             (full(c + 2)[:, :, 64:128], wkv[:, :, KVLORA:KVLORA + ROPE]),
                             (full(c + 2)[:, :, 128:256], wq[:, :, 256:384])]:
                sp.dma_start(dst, src).then_inc(raw_landed[(c + 2) % RAW_SLOTS], 16)
            wb = io["mla_w_kv_b"].rearrange("(k p) (h n) -> p k h n", p=P, h=MLA_H)
            for part, c in ((0, C0["KB"]), (1, C0["VB"])):
                sp.wait_ge(w_lo_ready, halves_before(c - RAW_SLOTS + 1, 0))
                for k in range(2):
                    dst = chunk_view(w_raw, c % RAW_SLOTS, "kvb")[:, k, :].rearrange("p (h n) -> p h n", h=MLA_H)
                    sp.dma_start(dst, wb[:, k, :, NOPE * part:NOPE * (part + 1)]).then_inc(raw_landed[c % RAW_SLOTS], 16)
            wb = io["mla_w_q_b"][0].rearrange("(k p) (h n) -> p k h n", p=P, h=MLA_H)
            for n in range(3):
                c = C0["QB"] + n
                sp.wait_ge(w_lo_ready, halves_before(c - RAW_SLOTS + 1, 0))
                for k in range(3):
                    dst = chunk_view(w_raw, c % RAW_SLOTS, "lat")[:, k, :]
                    if n == 0:
                        src = wb[:, k, :, NOPE:NOPE + ROPE]
                        dst = dst.rearrange("p (h n) -> p h n", h=MLA_H)
                    else:
                        src = wb[:, k, 4 * (n - 1):4 * n, 0:NOPE]
                        dst = dst.rearrange("p (h n) -> p h n", h=4)
                    sp.dma_start(dst, src).then_inc(raw_landed[c % RAW_SLOTS], 16)
            plain("MO", io["mla_w_out"][0], [CW * j for j in range(4)])
            up("U1", io["ffn_w_up"][1])
            down("D1", io["ffn_w_down"][1])
            w = io["gla_w_in_2"][0]
            c = C0["GA"]
            load(c, [(full(c)[:, :, 0:GATE_RANK], ktiles(w)[:, :, 3 * D:3 * D + GATE_RANK])])
            plain("GQK", w, [CW * j for j in range(4)])
            plain("GV", w, [D + CW * j for j in range(4)])
            plain("GG", w, [2 * D + CW * j for j in range(4)])
            plain("GO", io["gla_w_out_2"][0], [CW * j for j in range(4)])
            conv_up("CU0", io["ffn_w_up_2"][0])
            conv_down("CD0", io["ffn_w_down_2"][0])
            plain("SI", io["sc_w_in_2"][0], [CW * (j // 3) + D * ((j % 3 + 1) % 3) for j in range(12)])
            plain("SO", io["sc_w_out_2"][0], [CW * j for j in range(4)])
            conv_up("CU1", io["ffn_w_up_2"][1])
            conv_down("CD1", io["ffn_w_down_2"][1])
            sp.wait_ge(resid_ready, RT["x1"] + 16)
            sp.dma_start(io["out"].rearrange("(k p) t -> p k t", p=P), x[:]).then_inc(out_landed, 16)
            sp.wait_ge(out_landed, 16)

        @block.gpsimd
        def _(pool):
            zeroed = [0]

            def zero(name):
                n, tiles, before, _, _ = NORMS[name]
                if n:
                    pool.wait_ge(stat_done, n)
                nc.gpsimd.memset(ssq[:], 0.0).then_inc(pool_sum, 1)

            def add(name, m, tile, i=0, step=0):
                n, tiles, before, _, _ = NORMS[name]
                t = before + m + step * i
                pool.wait_ge(pool_sum, t + n + 1)
                nc.gpsimd.tensor_tensor(sqt[:], tile, tile, ALU.mult).then_inc(pool_sq, 1)
                pool.wait_ge(pool_sq, t + 1)
                nc.gpsimd.tensor_tensor(ssq[:], ssq[:], sqt[:], ALU.add).then_inc(pool_sum, 1)

            def straight(name, sig, base):
                zero(name)
                for m in range(KD):
                    pool.wait_ge(sig, base + m + 1)
                    add(name, m, x[:, m, :])

            def looped(name, sig, base):
                zero(name)
                with pool.Fori(0, 4) as i:
                    for j in range(2):
                        pool.wait_ge(sig, base + j + 1 + 2 * i)
                        add(name, j, x[:, ds(2 * i + j, 1), :], i, 2)

            zero("mix0")
            pool.wait_ge(x_landed, 16)
            for m in range(KD):
                add("mix0", m, x[:, m, :])
            straight("ffn0", dve_evac, DE["FO"])
            looped("mix1", resid_ready, RT["D0"])
            zero("kv_a")
            for m in range(2):
                pool.wait_ge(dve_evac, DE["KVQ"] + m + 1)
                add("kv_a", m, m_lat[:, m, :])
            zero("q_a")
            for m in range(3):
                pool.wait_ge(dve_evac, DE["KVQ"] + (3, 4, 6)[m])
                add("q_a", m, m_lat[:, 2 + m, :])
            straight("ffn1", dve_evac, DE["MO"])
            looped("final1", resid_ready, RT["D1"])
            straight("mix2", resid_ready, RT["x1"])
            straight("ffn2", dve_evac, DE["GO"])
            straight("mix3", dve_evac, DE["CD0"])
            straight("ffn3", dve_evac, DE["SO"])
            straight("final2", dve_evac, DE["CD1"])

        @block.tensor
        def _(pe):
            freed = [None] * 4

            def take_bank(stage, n, done):
                b = (TURN[stage] + n) % 4
                if freed[b] is not None:
                    pe.wait_ge(*freed[b])
                freed[b] = done
                return gemm[b]

            def w_at(c, kind="full"):
                return chunk_view(w_hi, c % W_SLOTS, kind), chunk_view(w_lo, c % W_SLOTS, kind)

            def split_ready(c, j, it=STRAIGHT):
                pe.wait_ge(w_lo_ready, halves_before(c, j, it) + 1)

            def feature_block(ps, c, cols, act, nk=8, k0=0, kind="full", start=True, stop=True, tiles=None):
                wh, wl = w_at(c, kind)
                last = None
                for k in range(nk):
                    if tiles is not None:
                        pe.wait_ge(act_ready, tiles + k + 1)
                    nc.tensor.matmul(ps, wh[:, k, cols], act[:, k0 + k, 0, :], start=start and k == 0, stop=False)
                    nc.tensor.matmul(ps, wh[:, k, cols], act[:, k0 + k, 1, :], start=False, stop=False)
                    last = nc.tensor.matmul(ps, wl[:, k, cols], act[:, k0 + k, 0, :], start=False,
                                            stop=stop and k == nk - 1)
                return last

            def token_block(ps, c, t, cols, act, nk=8, kind="full", tiles=None):
                wh, wl = w_at(c, kind)
                tok = slice(t * P, (t + 1) * P)
                for k in range(nk):
                    if tiles is not None:
                        pe.wait_ge(act_ready, tiles + k + 1)
                    nc.tensor.matmul(ps, act[:, k, 0, tok], wh[:, k, cols], start=k == 0, stop=False)
                    nc.tensor.matmul(ps, act[:, k, 1, tok], wh[:, k, cols], start=False, stop=False)
                    last = nc.tensor.matmul(ps, act[:, k, 0, tok], wl[:, k, cols], start=False, stop=k == nk - 1)
                return last

            def stat(name):
                n, tiles, before, tok, _ = NORMS[name]
                pe.wait_ge(pool_sum, before + n + 1 + tiles)
                if n:
                    pe.wait_ge(var_ready, n)
                last = nc.tensor.matmul(misc[:, 0:T], ones, ssq[:], start=True, stop=True)
                if tok:
                    for t in range(TT):
                        last = nc.tensor.matmul(misc[:, T + t:T + t + 1], ssq[:, t * P:(t + 1) * P], ones[:, 0:1],
                                                start=True, stop=True)
                last.then_inc(stat_done, 1)

            def plain(stage, act, tiles, evac, base, after_first=None, nch=4):
                for n in range(2 * nch):
                    c, j = C0[stage] + n // 2, n % 2
                    split_ready(c, j)
                    ps = take_bank(stage, n, (evac, base + n + 1))
                    feature_block(ps[:, 0:T], c, slice(j * P, (j + 1) * P), act,
                                  tiles=tiles if n == 0 else None).then_inc(half_done, 1)
                    if n == 0 and after_first:
                        stat(after_first)

            def token_chunk(stage, n, act, evac, base, cols=slice(0, CW), tiles=None):
                c = C0[stage] + n
                split_ready(c, 1)
                for t in range(TT):
                    ps = take_bank(stage, 2 * n + t, (evac, base + 2 * n + t + 1))
                    last = token_block(ps[:, 0:cols.stop - cols.start], c, t, cols, act, tiles=tiles if t == 0 else None)
                last.then_inc(half_done, 2)

            def up(stage, tiles, norm):
                b0 = TURN[stage]
                before = list(freed)
                with pe.Fori(0, 4) as i:
                    it = (i, 4, 8)
                    for n in range(8):
                        c, j = C0[stage] + n // 2, n % 2
                        split_ready(c, j, it)
                        b = (b0 + n) % 4
                        if n < 4:
                            pe.wait_ge(*before[b])
                        pe.wait_ge(act_evac, AE[stage] + n - 3 + 8 * i)
                        feature_block(gemm[b][:, 0:T], c, slice(j * P, (j + 1) * P), act_a,
                                      tiles=tiles if n == 0 else None).then_inc(half_done, 1)
                for b in range(4):
                    freed[(b0 + b) % 4] = (act_evac, AE[stage] + 28 + b + 1)
                stat(norm)

            def down(stage, tiles):
                b0 = TURN[stage]
                before = list(freed)
                with pe.Fori(0, 4) as i:
                    it = (i, 4, 2)
                    for cc in range(4):
                        c = C0[stage] + cc
                        for j in range(2):
                            b = (b0 + j) % 4
                            split_ready(c, j, it)
                            if cc == 0:
                                pe.wait_ge(*before[b])
                                pe.wait_ge(dve_evac, DE[stage] + j - 1 + 2 * i)
                            feature_block(gemm[b][:, 0:T], c, slice(j * P, (j + 1) * P), hid, k0=8 * cc,
                                          start=cc == 0, stop=cc == 3,
                                          tiles=tiles + 8 * cc if j == 0 else None).then_inc(half_done, 1)
                for j in range(2):
                    freed[(b0 + j) % 4] = (dve_evac, DE[stage] + 6 + j + 1)

            def conv_up(stage, tiles):
                b0 = TURN[stage]
                before = list(freed)

                def body(n, it, i):
                    c, j = C0[stage] + n // 2, n % 2
                    b = (b0 + n) % 4
                    split_ready(c, j, it)
                    if n < 4:
                        pe.wait_ge(*before[b])
                    pe.wait_ge(dve_evac, DE[stage] + n - 3 + 8 * i)
                    feature_block(gemm[b][:, 0:T], c, slice(j * P, (j + 1) * P), act_a,
                                  tiles=tiles if n == 0 else None).then_inc(half_done, 1)

                with pe.Fori(0, 5) as i:
                    for n in range(8):
                        body(n, (i, 4, 8), i)
                for n in range(40, 44):
                    body(n, STRAIGHT, 0)
                    freed[(b0 + n) % 4] = (dve_evac, DE[stage] + n + 1)

            def conv_down(stage, tiles):
                b0 = TURN[stage]
                before = list(freed)

                def body(cc, it, i):
                    c = C0[stage] + cc
                    k0, nk = sum(CD_K[:cc % 4]), CD_K[cc % 4]
                    for j in range(2):
                        b = (b0 + j) % 4
                        split_ready(c, j, it)
                        if cc % 4 == 0:
                            pe.wait_ge(*before[b])
                            pe.wait_ge(dve_evac, DE[stage] + j - 1 + 2 * i)
                        feature_block(gemm[b][:, 0:T], c, slice(j * P, (j + 1) * P), hid, nk=nk, k0=k0,
                                      start=cc % 4 == 0, stop=cc % 4 == 3,
                                      tiles=tiles + k0 if j == 0 else None).then_inc(half_done, 1)

                with pe.Fori(0, 3) as i:
                    for cc in range(4):
                        body(cc, (i, 4, 2), i)
                for cc in range(12, 16):
                    body(cc, STRAIGHT, 3)
                for j in range(2):
                    freed[(b0 + j) % 4] = (dve_evac, DE[stage] + 6 + j + 1)

            def transposes(n, prob, base):
                g = base + n
                pe.wait_ge(probs_normed, 2 * g + 2)
                if g:
                    pe.wait_ge(probsT_ready, g)
                nc.tensor.transpose(trans[:, 0:128], prob[:, n % 2, 0:128], ident)
                nc.tensor.transpose(trans[:, 128:256], prob[:, n % 2, 128:256], ident)
                nc.tensor.transpose(trans[:, 256:384], prob[:, n % 2, 256:384], ident).then_inc(transposed, 1)

            pe.wait_ge(con_landed, 16)
            for n in range(4):
                token_chunk("FV", n, act_a, act_evac, AE["FV"], tiles=AT["x"] if n == 0 else None)
                if n == 0:
                    stat("mix0")
            token_chunk("FG", 0, act_a, dve_evac, DE["FG"], cols=slice(0, FOX_H))

            def fox_cum():
                pe.wait_ge(gate_step, 4)
                for t in range(TT):
                    last = nc.tensor.matmul(trans[0:FOX_H, 0:T], f_ls[:, t, :], tri[:, t, :], start=t == 0, stop=t == TT - 1)
                last.then_inc(cum_done, 1)

            def fox_scores(h):
                tile, r = h // 2, slice(64 * (h % 2), 64 * (h % 2) + 64)
                pe.wait_ge(dve_evac, DE["FQK"] + 4 * (tile // 2) + 3 + tile % 2)
                if h == 0:
                    pe.wait_ge(cum_ready, 4)
                    pe.wait_ge(sel_ready, 1)
                if h >= 2:
                    pe.wait_ge(logits_ready, 2 * (h - 2) + 2)
                s = score[h % 2]
                for q, out, keys in ((0, s[:, 0:128], 128), (1, s[:, 128:384], 256)):
                    nc.tensor.matmul(out, f_q[r, tile, q * P:(q + 1) * P], f_k[r, tile, 0:keys], start=True, stop=False)
                    last = nc.tensor.matmul(out, f_sel[r, h, :], f_cum[r, 0:keys], start=False, stop=True)
                last.then_inc(scores_done, 1)

            def fox_pv(h):
                r = slice(64 * (h % 2), 64 * (h % 2) + 64)
                cols = slice(64 * h, 64 * h + 64)
                pe.wait_ge(probsT_ready, h + 1)
                if h == 0:
                    pe.wait_ge(act_evac, AE["FV"] + 8)
                    pe.wait_ge(var_ready, 1)
                if h % 2 == 0 and h:
                    pe.wait_ge(act_ready, AT["fctx"] + h // 2)
                nc.tensor.matmul(misc[r, 0:T], f_v[:, 0, cols], f_probT[:, h % 2, 0:256], start=True, stop=False)
                nc.tensor.matmul(misc[r, P:T], f_v[:, 1, cols], f_probT[:, h % 2, 256:384], start=False,
                                 stop=True).then_inc(pv_done, 1)

            for s in range(FOX_H + 6):
                if s < 16:
                    c, j = C0["FQK"] + s // 2, s % 2
                    split_ready(c, j)
                    ps = take_bank("FQK", s, (dve_evac, DE["FQK"] + s + 1))
                    feature_block(ps[:, 0:T], c, slice(j * P, (j + 1) * P), act_a).then_inc(half_done, 1)
                if s == 1:
                    fox_cum()
                if 4 <= s < 20:
                    fox_scores(s - 4)
                if 5 <= s < 21:
                    transposes(s - 5, f_prob, 0)
                if 6 <= s:
                    fox_pv(s - 6)
            plain("FO", act_b, AT["fctx"], dve_evac, DE["FO"])

            up("U0", AT["FO"], "ffn0")
            down("D0", AT["U0"])

            c = C0["KVQ"]
            for n, (cc, j, act) in enumerate([(0, 0, act_b), (0, 1, act_b), (1, 0, act_a), (1, 1, act_a),
                                              (2, 0, act_b), (2, 1, act_a)]):
                split_ready(c + cc, j)
                ps = take_bank("KVQ", n, (dve_evac, DE["KVQ"] + n + 1))
                if n == 0:
                    pe.wait_ge(act_ready, AT["D0"] + 16)
                feature_block(ps[:, 0:T], c + cc, slice(j * P, (j + 1) * P), act).then_inc(half_done, 1)
                if n == 0:
                    stat("mix1")
            stat("kv_a")
            pe.wait_ge(act_ready, AT["lat"] + 2)
            for j in range(2):
                split_ready(C0["KB"], j)
                for n in range(4 * j, 4 * j + 4):
                    ps = take_bank("KB", n, (dve_evac, DE["KB"] + n + 1))
                    last = feature_block(ps[:, 0:T], C0["KB"], slice(n * P, (n + 1) * P), m_act, nk=2, kind="kvb")
                last.then_inc(half_done, 1)
            stat("q_a")
            split_ready(C0["VB"], 1)
            for n in range(4):
                ps = take_bank("VB", n, (act_evac, AE["VB"] + n + 1))
                last = token_block(ps[:, 0:512], C0["VB"], n % 2, slice(512 * (n // 2), 512 * (n // 2) + 512), m_act,
                                   nk=2, kind="kvb")
            last.then_inc(half_done, 2)
            pe.wait_ge(act_ready, AT["lat"] + 5)

            def q_half(s):
                c, j = C0["QB"] + s // 2, s % 2
                split_ready(c, j)
                wh, wl = w_at(c, "lat")
                for n in range(2):
                    ps = take_bank("QB", 2 * s + n, (dve_evac, DE["QB"] + 2 * s + n + 1))[:, 0:T]
                    cols = slice((2 * j + n) * P, (2 * j + n + 1) * P)
                    for k in range(3):
                        nc.tensor.matmul(ps, wh[:, k, cols], m_act[:, 2 + k, 0, :], start=k == 0, stop=False)
                        nc.tensor.matmul(ps, wh[:, k, cols], m_act[:, 2 + k, 1, :], start=False, stop=False)
                        last = nc.tensor.matmul(ps, wl[:, k, cols], m_act[:, 2 + k, 0, :], start=False, stop=k == 2)
                last.then_inc(half_done, 1)

            def rotate(n):
                src = m_kr_raw[:] if n == 0 else m_qr_raw[:, n - 1, :]
                pe.wait_ge(dve_evac, DE["KVQ"] + 5 if n == 0 else DE["QB"] + n)
                if n >= 1:
                    pe.wait_ge(rope_step, 3 * (n - 1) + 2)
                else:
                    pe.wait_ge(probsT_ready, FOX_H)
                nc.tensor.matmul(trans[:, 0:T], rot, src, start=True, stop=True).then_inc(rot_done, 1)

            def mla_scores(h):
                r = slice(64 * (h % 2), 64 * (h % 2) + 64)
                g = FOX_H + h
                pe.wait_ge(dve_evac, DE["QB"] + 4 + h + 1)
                pe.wait_ge(rope_step, 15)
                pe.wait_ge(logits_ready, 2 * (g - 2) + 2)
                s = score[h % 2]
                for q, out, keys in ((0, s[:, 0:128], 128), (1, s[:, 128:384], 256)):
                    qs = slice(q * P, (q + 1) * P)
                    nc.tensor.matmul(out, m_q[:, h, qs], m_k[:, h, 0:keys], start=True, stop=False)
                    last = nc.tensor.matmul(out, m_qr[r, h // 2, qs], m_kr[r, 0:keys], start=False, stop=True)
                last.then_inc(scores_done, 1)

            def mla_pv(h):
                cols = slice(VDIM * h, VDIM * h + VDIM)
                pe.wait_ge(probsT_ready, FOX_H + h + 1)
                if h == 0:
                    pe.wait_ge(act_evac, AE["VB"] + 4)
                    pe.wait_ge(var_ready, NORMS["q_a"][0] + 1)
                else:
                    pe.wait_ge(act_ready, AT["mctx"] + h)
                nc.tensor.matmul(misc[:, 0:T], m_v[:, 0, cols], m_probT[:, h % 2, 0:256], start=True, stop=False)
                nc.tensor.matmul(misc[:, P:T], m_v[:, 1, cols], m_probT[:, h % 2, 256:384], start=False,
                                 stop=True).then_inc(pv_done, 1)

            for s in range(6):
                q_half(s)
                if s == 1:
                    rotate(0)
                if 2 <= s < 6:
                    rotate(s - 1)
            for s in range(MLA_H + 2):
                if s < MLA_H:
                    mla_scores(s)
                if 1 <= s <= MLA_H:
                    transposes(s - 1, m_prob, FOX_H)
                if s >= 2:
                    mla_pv(s - 2)
            plain("MO", act_b, AT["mctx"], dve_evac, DE["MO"])
            up("U1", AT["MO"], "ffn1")
            down("D1", AT["U1"])
            stat("final1")

            split_ready(C0["GA"], 1)
            ps = take_bank("GA", 0, (dve_evac, DE["GA"] + 1))
            feature_block(ps[:, 0:T], C0["GA"], slice(0, P), act_a, tiles=AT["x1"]).then_inc(half_done, 2)
            stat("mix2")
            pe_step = [0]

            def step(last):
                pe_step[0] += 1
                last.then_inc(gla_pe, 1)

            def gla_gates():
                pe.wait_ge(dve_evac, DE["GA"] + 1)
                pe.wait_ge(gla_small_landed, 32)
                for t in range(TT):
                    step(nc.tensor.matmul(score[t][:, 0:512], g_aT[:, t * P:(t + 1) * P], g_up[:], start=True, stop=True))

            def gla_cum():
                pe.wait_ge(gla_dve, 4)
                for g in range(2):
                    for h in range(2 * g, 2 * g + 2):
                        for t in range(TT):
                            last = nc.tensor.matmul(score[g][:, (h % 2) * T + t * P:(h % 2) * T + (t + 1) * P],
                                                    g_z[:, t, h * P:(h + 1) * P], tri_chunk, start=True, stop=True)
                    step(last)

            for n in range(8):
                c, j = C0["GQK"] + n // 2, n % 2
                split_ready(c, j)
                ps = take_bank("GQK", n, (dve_evac, DE["GQK"] + n + 1))
                feature_block(ps[:, 0:T], c, slice(j * P, (j + 1) * P), act_a).then_inc(half_done, 1)
                if n == 0:
                    gla_gates()
                if n == 5:
                    gla_cum()
            for n in range(4):
                token_chunk("GV", n, act_a, act_evac, AE["GV"])

            def gla_scores(t):
                pe.wait_ge(gla_dve, 10)
                for h in range(GLA_H):
                    tok = slice(t * P, (t + 1) * P)
                    last = nc.tensor.matmul(score[t][:, h * P:(h + 1) * P], g_ki[:, h, tok], g_qi[:, h, tok], start=True,
                                            stop=True)
                step(last)

            def gla_transpose(t):
                pe.wait_ge(gla_dve, 10)
                if t:
                    pe.wait_ge(gla_act, 8)
                else:
                    pe.wait_ge(probsT_ready, FOX_H + MLA_H)
                for h in range(GLA_H):
                    last = nc.tensor.transpose(trans[:, h * P:(h + 1) * P], g_kd[:, h, t * P:(t + 1) * P], ident)
                step(last)

            def gla_state(n):
                t, r = n // 2, slice(GLA_C * (n % 2), GLA_C * (n % 2) + GLA_C)
                pe.wait_ge(gla_act, 8 + t)
                pe.wait_ge(act_evac, AE["GV"] + 8)
                if n:
                    pe.wait_ge(gla_dve, 12 + 4 * n)
                else:
                    pe.wait_ge(gla_dve, 12)
                for h in range(GLA_H):
                    last = nc.tensor.matmul(score[h // 2][:, (h % 2) * T:(h % 2) * T + T], g_kdT[r, t, h * P:(h + 1) * P],
                                            g_v[r, t, h * GLA_DV:(h + 1) * GLA_DV], start=True, stop=True)
                step(last)

            def gla_out(n):
                h = n // 2
                e = slice(n * P, (n + 1) * P)
                s = slice((n % 2) * P, (n % 2) * P + P)
                bank_ = (trans, score[0])[n % 2]
                if n == 0:
                    pe.wait_ge(gla_act, 9)
                    pe.wait_ge(gla_dve, 24)
                if n >= 2:
                    pe.wait_ge(gla_act, 9 + n - 1)
                for t in range(TT):
                    nc.tensor.matmul(bank_[:, t * P:(t + 1) * P], g_v[:, t, e], g_sT[:, t, h * P:(h + 1) * P],
                                     start=t == 0, stop=False)
                for m in range(1, T // GLA_C):
                    tok = slice(m * GLA_C, (m + 1) * GLA_C)
                    last = nc.tensor.matmul(bank_[:, tok], g_s[:, m - 1, h, s], g_qi[:, h, tok], start=False,
                                            stop=m == T // GLA_C - 1)
                step(last)

            def gla_stat(h):
                if h == 0:
                    pe.wait_ge(gla_act, 17)
                pe.wait_ge(gla_dve, 24 + 2 * h + 2)
                for e in range(2):
                    last = nc.tensor.matmul(score[h // 2][:, (h % 2) * T:(h % 2) * T + T], ones, tmp[:, 2 * (h % 2) + e, :],
                                            start=e == 0, stop=e == 1)
                step(last)

            for n in range(8):
                c, j = C0["GG"] + n // 2, n % 2
                split_ready(c, j)
                ps = take_bank("GG", n, (dve_evac, DE["GG"] + n + 1))
                feature_block(ps[:, 0:T], c, slice(j * P, (j + 1) * P), act_a).then_inc(half_done, 1)
                if n == 0:
                    gla_scores(0)
                    gla_scores(1)
                    gla_transpose(0)
                if n == 1:
                    gla_transpose(1)
                if n in (2, 3, 4):
                    gla_state(n - 2)
                if n >= 6:
                    for m in range(4):
                        gla_out(4 * (n - 6) + m)
            for h in range(GLA_H):
                gla_stat(h)
            plain("GO", act_b, AT["gla"], dve_evac, DE["GO"])
            stat("ffn2")

            conv_up("CU0", AT["GO"])
            conv_down("CD0", AT["CU0"])
            for n in range(24):
                c, j = C0["SI"] + n // 2, n % 2
                split_ready(c, j)
                g, part = n // 6, (n % 6) // 2
                done = (act_evac, AE["SI"] + 2 * g + j + 1) if part == 0 else (dve_evac, DE["SI"] + 4 * g + 2 * (part - 1) + j + 1)
                ps = take_bank("SI", n, done)
                feature_block(ps[:, 0:T], c, slice(j * P, (j + 1) * P), act_a,
                              tiles=AT["CD0"] if n == 0 else None).then_inc(half_done, 1)
                if n == 0:
                    stat("mix3")
            plain("SO", act_b, AT["sc"], dve_evac, DE["SO"])
            stat("ffn3")
            conv_up("CU1", AT["SO"])
            conv_down("CD1", AT["CU1"])
            stat("final2")

        @block.scalar
        def _(act):
            act.dma_start(vec[:], io["vec"]).then_inc(vec_landed, 16)
            act.dma_start(x[:], io["xT"].rearrange("(k p) t -> p k t", p=P)).then_inc(x_landed, 16)
            act.dma_start(con[:], io["con"]).then_inc(con_landed, 16)
            act.dma_start(f_sel_raw[:], io["sel"]).then_inc(fox_small_landed, 16)
            act.dma_start(f_bias[:], io["fox_b_f"][0:1, :].partition_broadcast(P)).then_inc(fox_small_landed, 16)
            act.dma_start(g_bias[:], io["gla_b_gate_2"][0:1, :].partition_broadcast(P)).then_inc(gla_small_landed, 16)
            act.dma_start(g_up[:], io["gla_w_gate_up_2"][0]).then_inc(gla_small_landed, 16)

            def prep(c, j, it=STRAIGHT, first=False):
                nxt = (c, j) if first else ahead(c, j)
                if nxt is None:
                    return
                nc_, nj = nxt
                h = halves_before(nc_, nj, it)
                if nj == 0:
                    act.wait_ge(raw_landed[nc_ % RAW_SLOTS], raw_count(nc_, it))
                if 2 * nc_ + nj >= 2 * W_SLOTS:
                    both = kind_of(nc_)[0] != kind_of(nc_ - W_SLOTS)[0] and nj == 0
                    act.wait_ge(half_done, h - 2 * W_SLOTS + (2 if both else 1))
                nc.scalar.copy(half_view(w_hi, nc_ % W_SLOTS, nc_, nj),
                               half_view(w_raw, nc_ % RAW_SLOTS, nc_, nj)).then_inc(w_hi_ready, 1)

            def dmas(c):
                if c == C0["KVQ"] + 2 or C0["QB"] <= c < C0["MO"]:
                    return 3
                return 2 if C0["KB"] <= c < C0["QB"] else 1

            def raw_count(c, it):
                return 16 * sum(dmas(k) for k in range(c % RAW_SLOTS, c + 1, RAW_SLOTS)) + 16 * (it[1] // RAW_SLOTS) * it[0]

            def round_tile(dst, src, scale=None):
                if scale is None:
                    nc.scalar.copy(dst, src).then_inc(act_hi_ready, 1)
                else:
                    nc.scalar.activation(dst, src, ACT.Copy, scale=scale).then_inc(act_hi_ready, 1)

            def root(name):
                n = ROOTS.index(name)
                act.wait_ge(var_ready, NORMS[name][0] + 1)
                cols = T + TT if NORMS[name][3] else T
                nc.scalar.activation(std[:, 0:cols], var[:, 0:cols], ACT.Sqrt).then_inc(std_ready, 1)

            def plain_preps(stage, nch=4):
                for n in range(2 * nch):
                    prep(C0[stage] + n // 2, n % 2)
                    yield n

            def residual(stage, name, sig=None):
                for n in plain_preps(stage):
                    if name is not None:
                        act.wait_ge(dve_evac, DE[stage] + n + 1)
                        round_tile(act_a[:, n, 0, :], x[:, n, :], gain(name, n))

            def up(stage):
                nc.scalar.preload_act_table(ACT.Sqrt)
                with act.Fori(0, 4) as i:
                    def rounded(n):
                        act.wait_ge(sq_ready, SQ[stage] + n + 1 + 8 * i)
                        round_tile(hid[:, ds(8 * i + n, 1), 0, :], tmp2[:, n % 4, :])

                    for n in range(8):
                        c, j = C0[stage] + n // 2, n % 2
                        prep(c, j, (i, 4, 8))
                        if n:
                            rounded(n - 1)
                        act.wait_ge(half_done, halves_before(c, j, (i, 4, 8)) + 1)
                        nc.scalar.activation(tmp[:, n % 4, :], bank_of(stage, n)[:, 0:T], ACT.Relu).then_inc(act_evac, 1)
                    rounded(7)

            def down(stage, names):
                nc.scalar.preload_act_table(ACT.Sqrt)
                with act.Fori(0, 4) as i:
                    for cc in range(4):
                        for j in range(2):
                            prep(C0[stage] + cc, j, (i, 4, 2))
                    for j in range(2):
                        for name, dst in names:
                            act.wait_ge(resid_ready, RT[stage] + j + 1 + 2 * i)
                            g = vec[:, ds(2 * i + VEC[name] + j, 1)]
                            round_tile(dst[:, ds(2 * i + j, 1), 0, :], x[:, ds(2 * i + j, 1), :], g)

            def conv_up(stage, conv):
                nc.scalar.preload_act_table(ACT.Silu)

                def step(n, it, i, unroll):
                    c, j = C0[stage] + n // 2, n % 2
                    prep(c, j, it)
                    if n % unroll:
                        finish(n - 1, i)
                    act.wait_ge(half_done, halves_before(c, j, it) + 1)
                    tile = 2 * (n // 4) + n % 2 + (NT2 if n % 4 >= 2 else 0)
                    col = VEC[conv] + 3 * tile + 2
                    w = vec[:, ds(col + 12 * i, 1)] if it[1] else vec[:, col:col + 1]
                    if n % 4 >= 2:
                        act.wait_ge(act_ready, AT[stage] + 2 * (n // 4) + n % 2 - 1 + 4 * i)
                    nc.scalar.activation(tmp[:, n % 4, :], bank_of(stage, n)[:, 0:T], ACT.Copy,
                                         scale=w).then_inc(tap_ready, 1)

                def finish(n, i):
                    if n % 4 < 2:
                        act.wait_ge(dve_evac, DE[stage] + n + 1 + 8 * i)
                        nc.scalar.activation(tmp2[:, n % 2, :], tmp[:, n % 4, :], ACT.Silu).then_inc(silu_ready, 1)
                    else:
                        t = 2 * (n // 4) + n % 2
                        act.wait_ge(gated_ready, GT[stage] + t + 1 + 4 * i)
                        dst = hid[:, t, 0, :] if isinstance(i, int) else hid[:, ds(4 * i + t, 1), 0, :]
                        round_tile(dst, tmp[:, n % 4, :])

                with act.Fori(0, 5) as i:
                    for n in range(8):
                        step(n, (i, 4, 8), i, 8)
                    finish(7, i)
                for n in range(40, 44):
                    step(n, STRAIGHT, 0, 4)
                finish(43, 0)

            def conv_down(stage, name):
                nc.scalar.preload_act_table(ACT.Sqrt)

                def body(cc, it, i):
                    for j in range(2):
                        prep(C0[stage] + cc, j, it)
                    if cc % 4 == 3 and name is not None:
                        for j in range(2):
                            act.wait_ge(dve_evac, DE[stage] + j + 1 + 2 * i)
                            if it[1]:
                                round_tile(act_a[:, ds(2 * i + j, 1), 0, :], x[:, ds(2 * i + j, 1), :],
                                           vec[:, ds(2 * i + VEC[name] + j, 1)])
                            else:
                                round_tile(act_a[:, 6 + j, 0, :], x[:, 6 + j, :], gain(name, 6 + j))

                with act.Fori(0, 3) as i:
                    for cc in range(4):
                        body(cc, (i, 4, 2), i)
                for cc in range(12, 16):
                    body(cc, STRAIGHT, 3)

            def normed(stage):
                for k in range(KD):
                    act.wait_ge(gated_ready, GT[stage] + k + 1)
                    round_tile(act_a[:, k, 0, :], tmp_of(k))

            def exps(n, base, logit, prob, nmax, total, scale):
                g = base + n
                act.wait_ge(negmax_ready, g + 1)
                if g >= 2:
                    act.wait_ge(transposed, g - 1)
                for q, cols in ((0, slice(0, 128)), (1, slice(128, 384))):
                    nc.scalar.activation(prob[:, n % 2, cols], logit[:, n % 2, cols], ACT.Exp, bias=nmax[:, n % 2, q:q + 1],
                                         scale=scale, accum_out=total[:, n % 2, q:q + 1]).then_inc(probs_ready, 1)

            def copy_transposed(n, base, probT):
                g = base + n
                act.wait_ge(transposed, g + 1)
                if g >= 2:
                    act.wait_ge(pv_done, g - 1)
                nc.scalar.copy(probT[:, n % 2, :], trans[:, 0:384]).then_inc(probsT_ready, 1)

            for h in range(AHEAD):
                prep(h // 2, h % 2, first=True)
                if h == 0:
                    act.wait_ge(vec_landed, 16)
                    act.wait_ge(x_landed, 16)
                    for k in range(KD):
                        round_tile(act_a[:, k, 0, :], x[:, k, :], gain("mix0", k))

            for n in range(4):
                c = C0["FV"] + n
                for j in range(2):
                    prep(c, j)
                if n == 0:
                    root("mix0")
                    act.wait_ge(rstd_ready, 1)
                act.wait_ge(half_done, 2 * c + 2)
                for t in range(TT):
                    nc.scalar.activation(f_v[:, t, n * CW:(n + 1) * CW], bank_of("FV", 2 * n + t)[:, 0:CW], ACT.Copy,
                                         scale=rstd_of("mix0")[:, T + t:T + t + 1]).then_inc(act_evac, 1)
            for j in range(2):
                prep(C0["FG"], j)
            act.wait_ge(gate_step, 1)
            nc.scalar.activation(f_exp[:], f_neg_abs[:], ACT.Exp).then_inc(gate_step, 1)
            act.wait_ge(gate_step, 2)
            nc.scalar.activation(f_ln[:], f_exp[:], ACT.Ln, bias=1.0).then_inc(gate_step, 1)
            for s in range(FOX_H + 6):
                if s < 16:
                    prep(C0["FQK"] + s // 2, s % 2)
                if 4 <= s < 20:
                    exps(s - 4, 0, f_logit, f_prob, neg_max, row_sum, FOX_SCALE)
                if 5 <= s < 21:
                    copy_transposed(s - 5, 0, f_probT)
                if 6 <= s and s % 2:
                    act.wait_ge(pv_done, s - 6 + 1)
                    round_tile(act_b[:, (s - 6) // 2, 0, :], misc[:, 0:T])
            residual("FO", "ffn0")
            up("U0")
            down("D0", [("kv", act_b), ("mix1", act_a)])

            for n in range(6):
                prep(C0["KVQ"] + n // 2, n % 2)
                if n == 0:
                    root("mix1")
                if n != 4:
                    m = n if n < 4 else n - 1
                    act.wait_ge(dve_evac, DE["KVQ"] + n + 1)
                    g = gain("kv_a", m) if m < 2 else gain("q_a", m - 2)
                    round_tile(m_act[:, m, 0, :], m_lat[:, m, :], g)
            root("kv_a")
            for j in range(2):
                prep(C0["KB"], j)
            root("q_a")
            for j in range(2):
                prep(C0["VB"], j)
            act.wait_ge(half_done, 2 * C0["VB"] + 2)
            act.wait_ge(rstd_ready, ROOTS.index("kv_a") + 1)
            for n in range(4):
                t = n % 2
                nc.scalar.activation(m_v[:, t, 512 * (n // 2):512 * (n // 2) + 512], bank_of("VB", n)[:], ACT.Copy,
                                     scale=rstd_of("kv_a")[:, T + t:T + t + 1]).then_inc(act_evac, 1)
            for s in range(6):
                prep(C0["QB"] + s // 2, s % 2)
            for s in range(MLA_H + 2):
                if s < MLA_H:
                    exps(s, FOX_H, m_logit, m_prob, m_nmax, m_sum, MLA_SCALE)
                if 1 <= s <= MLA_H:
                    copy_transposed(s - 1, FOX_H, m_probT)
                if s >= 2:
                    act.wait_ge(pv_done, FOX_H + s - 1)
                    round_tile(act_b[:, s - 2, 0, :], misc[:, 0:T])
            residual("MO", "ffn1")
            up("U1")
            down("D1", [])
            root("final1")

            for k in range(KD):
                act.wait_ge(resid_ready, RT["x1"] + k + 1)
                round_tile(act_a[:, k, 0, :], x[:, k, :], gain("mix2", k))
            for j in range(2):
                prep(C0["GA"], j)
            root("mix2")
            act_step = [0]

            def step(last):
                act_step[0] += 1
                last.then_inc(gla_act, 1)

            for n in range(8):
                prep(C0["GQK"] + n // 2, n % 2)
                if n == 1:
                    act.wait_ge(gla_dve, 2)
                    step(nc.scalar.activation(g_e[:], g_e[:], ACT.Exp))
                    act.wait_ge(gla_act, 1)
                    step(nc.scalar.activation(g_e[:], g_e[:], ACT.Ln, bias=1.0))
                if n == 7:
                    for g in range(2):
                        act.wait_ge(gla_pe, 3 + g)
                        hs = slice(2 * g, 2 * g + 2)
                        v = score[g][:].rearrange("p (h t) -> p h t", h=2)
                        step(nc.scalar.activation(g_eb[:, hs, :], v, ACT.Exp))
                        step(nc.scalar.activation(g_ki[:, hs, :], v, ACT.Exp, scale=-1.0))
            act.wait_ge(gla_dve, 6)
            step(nc.scalar.activation(g_kd[:], g_kd[:], ACT.Exp))
            act.wait_ge(rstd_ready, ROOTS.index("mix2") + 1)
            for n in range(4):
                c = C0["GV"] + n
                for j in range(2):
                    prep(c, j)
                act.wait_ge(half_done, 2 * c + 2)
                for t in range(TT):
                    nc.scalar.activation(g_v[:, t, n * CW:(n + 1) * CW], bank_of("GV", 2 * n + t)[:, 0:CW], ACT.Copy,
                                         scale=rstd_of("mix2")[:, T + t:T + t + 1]).then_inc(act_evac, 1)
            for n in range(8):
                prep(C0["GG"] + n // 2, n % 2)
                if n in (0, 1):
                    act.wait_ge(gla_pe, 7 + n)
                    step(nc.scalar.copy(g_kdT[:, n, :], trans[:]))
                if n >= 6:
                    for m in range(4 * (n - 6), 4 * (n - 6) + 4):
                        act.wait_ge(gla_pe, 12 + m)
                        if m == 0:
                            act.wait_ge(gla_dve, 10)
                        step(nc.scalar.copy(g_o[:, m, :], (trans, score[0])[m % 2][:, 0:T]))
            for g in range(2):
                act.wait_ge(gla_dve, 33 + g)
                step(nc.scalar.activation(tmp2[:, 2 * g:2 * g + 2, :], tmp2[:, 2 * g:2 * g + 2, :], ACT.Sqrt))
            for m in range(KD):
                act.wait_ge(dve_evac, DE["GG"] + m + 1)
                nc.scalar.activation(g_g[:, m, :], g_g[:, m, :], ACT.Silu).then_inc(silu_ready, 1)
            for m in range(KD):
                act.wait_ge(gated_ready, GT["gla"] + m + 1)
                round_tile(act_b[:, m, 0, :], g_o[:, m, :])
            residual("GO", None)
            root("ffn2")
            normed("GO")

            conv_up("CU0", "conv0")
            conv_down("CD0", "mix3")
            for n in range(24):
                c, j = C0["SI"] + n // 2, n % 2
                prep(c, j)
                if n == 0:
                    root("mix3")
                g, part = n // 6, (n % 6) // 2
                m = 2 * g + j
                if part == 0:
                    act.wait_ge(half_done, 2 * c + j + 1)
                    if g:
                        act.wait_ge(dve_evac, DE["SI"] + 4 * (g - 1) + j + 1)
                    nc.scalar.copy(s_c[:, j, :], bank_of("SI", n)[:, 0:T]).then_inc(act_evac, 1)
                if part == 1:
                    act.wait_ge(sc_ready, m + 1)
                    nc.scalar.activation(tmp[:, j, :], tmp2[:, j, :], ACT.Copy,
                                         scale=gain("sc_conv", 3 * m + 2)).then_inc(tap_ready, 1)
                if part == 2:
                    act.wait_ge(dve_evac, DE["SI"] + 4 * g + 2 + j + 1)
                    round_tile(act_b[:, m, 0, :], tmp[:, 2 + j, :])
            residual("SO", None)
            root("ffn3")
            normed("SO")
            conv_up("CU1", "conv1")
            conv_down("CD1", None)
            root("final2")

        @block.vector
        def _(dve):
            def prep(c, j, it=STRAIGHT, first=False):
                nxt = (c, j) if first else ahead(c, j)
                if nxt is None:
                    return
                nc_, nj = nxt
                dve.wait_ge(w_hi_ready, halves_before(nc_, nj, it) + 1)
                nc.vector.tensor_tensor(half_view(w_lo, nc_ % W_SLOTS, nc_, nj),
                                        half_view(w_raw, nc_ % RAW_SLOTS, nc_, nj),
                                        half_view(w_hi, nc_ % W_SLOTS, nc_, nj).bitcast(F32),
                                        ALU.subtract).then_inc(w_lo_ready, 1)

            def low_tile(n, dst, src, hi, scale=None, extra=None):
                dve.wait_ge(act_hi_ready, n + 1)
                if scale is None:
                    nc.vector.tensor_tensor(dst, src, hi.bitcast(F32), ALU.subtract).then_inc(act_ready, 1)
                else:
                    nc.vector.scalar_tensor_tensor(out=dst, in0=src, scalar=scale, in1=hi.bitcast(F32), op0=ALU.mult,
                                                   op1=ALU.subtract).then_inc(act_ready, 1)

            def variance(name):
                n, _, _, tok, feats = NORMS[name]
                cols = T + TT if tok else T
                dve.wait_ge(stat_done, n + 1)
                if n and name in ROOTS and ROOTS.index(name):
                    dve.wait_ge(std_ready, ROOTS.index(name))
                nc.vector.tensor_scalar(var[:, 0:cols], misc[:, 0:cols], 1.0 / feats, EPS, ALU.mult,
                                        ALU.add).then_inc(var_ready, 1)

            def inverse_rms(name):
                n = ROOTS.index(name)
                cols = T + TT if NORMS[name][3] else T
                dve.wait_ge(std_ready, n + 1)
                nc.vector.reciprocal(rstd_of(name)[:, 0:cols], std[:, 0:cols]).then_inc(rstd_ready, 1)
                dve.wait_ge(rstd_ready, n + 1)

            def norm(name):
                variance(name)
                inverse_rms(name)

            def inverse_square(name):
                variance(name)
                dve.wait_ge(var_ready, NORMS[name][0] + 1)
                link(nc.vector.reciprocal(rstd_of(name)[:, 0:T], var[:, 0:T]))

            own_n = [0]

            def link(last):
                own_n[0] += 1
                last.then_inc(dve_own, 1)
                dve.wait_ge(dve_own, own_n[0])

            def residual(stage, name, at):
                for n in range(8):
                    c, j = C0[stage] + n // 2, n % 2
                    prep(c, j)
                    dve.wait_ge(half_done, 2 * c + j + 1)
                    nc.vector.tensor_tensor(x[:, n, :], bank_of(stage, n)[:, 0:T], x[:, n, :], ALU.add).then_inc(dve_evac, 1)
                    if name is not None:
                        low_tile(AT[at] + n, act_a[:, n, 1, :], x[:, n, :], act_a[:, n, 0, :], gain(name, n))

            def up(stage):
                with dve.Fori(0, 4) as i:
                    def low(n):
                        t = ds(8 * i + n, 1)
                        low_tile(AT[stage] + n + 8 * i, hid[:, t, 1, :], tmp2[:, n % 4, :], hid[:, t, 0, :])

                    for n in range(8):
                        prep(C0[stage] + n // 2, n % 2, (i, 4, 8))
                        if n:
                            low(n - 1)
                        dve.wait_ge(act_evac, AE[stage] + n + 1 + 8 * i)
                        nc.vector.tensor_tensor(tmp2[:, n % 4, :], tmp[:, n % 4, :], tmp[:, n % 4, :],
                                                ALU.mult).then_inc(sq_ready, 1)
                    low(7)

            def down(stage, norm_name, names, at):
                inverse_square(norm_name)
                with dve.Fori(0, 4) as i:
                    it = (i, 4, 2)
                    for cc in range(4):
                        for j in range(2):
                            c = C0[stage] + cc
                            prep(c, j, it)
                            if cc == 3:
                                dve.wait_ge(half_done, halves_before(c, j, it) + 1)
                                nc.vector.tensor_tensor(tmp[:, j, :], bank_of(stage, j)[:, 0:T], rstd_of(norm_name)[:, 0:T],
                                                        ALU.mult).then_inc(dve_evac, 1)
                                dve.wait_ge(dve_evac, DE[stage] + j + 1 + 2 * i)
                                t = ds(2 * i + j, 1)
                                nc.vector.tensor_tensor(x[:, t, :], x[:, t, :], tmp[:, j, :], ALU.add).then_inc(resid_ready, 1)
                    for j in range(2):
                        t = ds(2 * i + j, 1)
                        for m, (name, dst) in enumerate(names):
                            low_tile(AT[at] + len(names) * j + m + 2 * len(names) * i, dst[:, t, 1, :], x[:, t, :],
                                     dst[:, t, 0, :], vec[:, ds(2 * i + VEC[name] + j, 1)])

            def conv_up(stage, conv):
                def low(n, i):
                    t = 2 * (n // 4) + n % 2
                    if isinstance(i, int):
                        hi, lo = hid[:, t, 0, :], hid[:, t, 1, :]
                    else:
                        hi, lo = hid[:, ds(4 * i + t, 1), 0, :], hid[:, ds(4 * i + t, 1), 1, :]
                    low_tile(AT[stage] + t + 4 * i, lo, tmp[:, n % 4, :], hi)

                def step(n, it, i, unroll):
                    c, j = C0[stage] + n // 2, n % 2
                    prep(c, j, it)
                    if n % unroll and (n - 1) % 4 >= 2:
                        low(n - 1, i)
                    tile = 2 * (n // 4) + n % 2 + (NT2 if n % 4 >= 2 else 0)
                    col = VEC[conv] + 3 * tile
                    w0, w1 = (vec[:, ds(col + k + 12 * i, 1)] if it[1] else vec[:, col + k:col + k + 1] for k in range(2))
                    y, ps = tmp[:, n % 4, :], bank_of(stage, n)
                    dve.wait_ge(tap_ready, CV[stage] + n + 1 + 8 * i)
                    nc.vector.scalar_tensor_tensor(out=y[:, 1:T], in0=ps[:, 0:T - 1], scalar=w1, in1=y[:, 1:T],
                                                   op0=ALU.mult, op1=ALU.add).then_inc(tap_mid, 1)
                    dve.wait_ge(tap_mid, CV[stage] + n + 1 + 8 * i)
                    nc.vector.scalar_tensor_tensor(out=y[:, 2:T], in0=ps[:, 0:T - 2], scalar=w0, in1=y[:, 2:T],
                                                   op0=ALU.mult, op1=ALU.add).then_inc(dve_evac, 1)
                    if n % 4 >= 2:
                        t = 2 * (n // 4) + n % 2
                        dve.wait_ge(dve_evac, DE[stage] + n + 1 + 8 * i)
                        dve.wait_ge(silu_ready, SL[stage] + t + 1 + 4 * i)
                        nc.vector.tensor_tensor(y, y, tmp2[:, n % 2, :], ALU.mult).then_inc(gated_ready, 1)

                with dve.Fori(0, 5) as i:
                    for n in range(8):
                        step(n, (i, 4, 8), i, 8)
                    low(7, i)
                for n in range(40, 44):
                    step(n, STRAIGHT, 0, 4)
                low(43, 0)

            def conv_down(stage, name, at):
                def body(cc, it, i):
                    c = C0[stage] + cc
                    for j in range(2):
                        prep(c, j, it)
                        if cc % 4 == 3:
                            dve.wait_ge(half_done, halves_before(c, j, it) + 1)
                            xt = x[:, ds(2 * i + j, 1), :] if it[1] else x[:, 6 + j, :]
                            ps = bank_of(stage, j)[:, 0:T]
                            nc.vector.tensor_tensor(xt, ps, xt, ALU.add).then_inc(dve_evac, 1)
                    if cc % 4 == 3 and name is not None:
                        for j in range(2):
                            if it[1]:
                                t = ds(2 * i + j, 1)
                                low_tile(AT[at] + j + 2 * i, act_a[:, t, 1, :], x[:, t, :], act_a[:, t, 0, :],
                                         vec[:, ds(2 * i + VEC[name] + j, 1)])
                            else:
                                low_tile(AT[at] + 6 + j, act_a[:, 6 + j, 1, :], x[:, 6 + j, :], act_a[:, 6 + j, 0, :],
                                         gain(name, 6 + j))

                with dve.Fori(0, 3) as i:
                    for cc in range(4):
                        body(cc, (i, 4, 2), i)
                for cc in range(12, 16):
                    body(cc, STRAIGHT, 3)

            def normed(stage, name):
                for k in range(KD):
                    nc.vector.scalar_tensor_tensor(out=tmp_of(k), in0=x[:, k, :], scalar=gain(name, k),
                                                   in1=rstd_of(name)[:, 0:T], op0=ALU.mult, op1=ALU.mult).then_inc(gated_ready, 1)
                    if k >= 1:
                        low_tile(AT[stage] + k - 1, act_a[:, k - 1, 1, :], tmp_of(k - 1), act_a[:, k - 1, 0, :])
                low_tile(AT[stage] + KD - 1, act_a[:, KD - 1, 1, :], tmp_of(KD - 1), act_a[:, KD - 1, 0, :])

            def scaled(stage, n, half, dst, norm_name, rows=P):
                dve.wait_ge(half_done, half)
                nc.vector.tensor_tensor(dst, bank_of(stage, n)[0:rows, 0:T], rstd_of(norm_name)[0:rows, 0:T],
                                        ALU.mult).then_inc(dve_evac, 1)

            def maxima(n, base, logit, rmax, nmax, scale):
                g = base + n
                dve.wait_ge(scores_done, g + 1)
                s = score[n % 2]
                nc.vector.tensor_tensor_reduce(logit[:, n % 2, 0:128], s[:, 0:128], mask[:, 128:256], 1.0, -3.0e38, ALU.add,
                                               ALU.max, rmax[:, n % 2, 0:1]).then_inc(logits_ready, 1)
                nc.vector.tensor_tensor_reduce(logit[:, n % 2, 128:384], s[:, 128:384], mask, 1.0, -3.0e38, ALU.add,
                                               ALU.max, rmax[:, n % 2, 1:2]).then_inc(logits_ready, 1)
                dve.wait_ge(logits_ready, 2 * g + 2)
                nc.vector.tensor_scalar(nmax[:, n % 2, :], rmax[:, n % 2, :], -scale, None, ALU.mult).then_inc(negmax_ready, 1)

            def norm_probs(n, base, prob, total, inv):
                g = base + n
                dve.wait_ge(probs_ready, 2 * g + 2)
                nc.vector.reciprocal(inv[:, n % 2, :], total[:, n % 2, :]).then_inc(invsum_ready, 1)
                dve.wait_ge(invsum_ready, g + 1)
                for q, cols in ((0, slice(0, 128)), (1, slice(128, 384))):
                    nc.vector.tensor_scalar(prob[:, n % 2, cols], prob[:, n % 2, cols], inv[:, n % 2, q:q + 1], None,
                                            ALU.mult).then_inc(probs_normed, 1)

            for h in range(AHEAD):
                prep(h // 2, h % 2, first=True)
                if h == 0:
                    dve.wait_ge(x_landed, 16)
                    dve.wait_ge(vec_landed, 16)
                    for k in range(KD):
                        low_tile(AT["x"] + k, act_a[:, k, 1, :], x[:, k, :], act_a[:, k, 0, :], gain("mix0", k))
            dve.wait_ge(con_landed, 16)
            dve.wait_ge(fox_small_landed, 32)
            nc.vector.tensor_copy(f_sel[:].rearrange("p h n -> p (h n)"), f_sel_raw[:]).then_inc(sel_ready, 1)
            link(nc.vector.memset(f_cum[:].bitcast(F32), 0.0))

            for n in range(4):
                for j in range(2):
                    prep(C0["FV"] + n, j)
                if n == 0:
                    norm("mix0")
            c = C0["FG"]
            for j in range(2):
                prep(c, j)
            dve.wait_ge(half_done, 2 * c + 2)
            for t in range(TT):
                nc.vector.scalar_tensor_tensor(out=f_z[:, t, :], in0=bank_of("FG", t)[:, 0:FOX_H],
                                               scalar=rstd_of("mix0")[:, T + t:T + t + 1], in1=f_bias[:], op0=ALU.mult,
                                               op1=ALU.add).then_inc(dve_evac, 1)
            dve.wait_ge(dve_evac, DE["FG"] + 2)
            nc.vector.scalar_tensor_tensor(out=f_neg_abs[:], in0=f_z[:], scalar=-1.0, in1=f_z[:], op0=ALU.mult,
                                           op1=ALU.min).then_inc(gate_step, 1)
            dve.wait_ge(gate_step, 3)
            nc.vector.scalar_tensor_tensor(out=f_ls[:], in0=f_z[:], scalar=0.0, in1=f_ln[:], op0=ALU.min,
                                           op1=ALU.subtract).then_inc(gate_step, 1)
            for s in range(FOX_H + 6):
                if s < 16:
                    c, j = C0["FQK"] + s // 2, s % 2
                    prep(c, j)
                    dst = (f_q, f_k)[s // 2 % 2][:, 2 * (s // 4) + j, :]
                    scaled("FQK", s, 2 * c + j + 1, dst, "mix0")
                if s == 1:
                    dve.wait_ge(cum_done, 1)
                    for row in (0, 64):
                        nc.vector.tensor_copy(f_cum[row:row + 16, :], trans[0:16, 0:T]).then_inc(cum_ready, 1)
                    dve.wait_ge(cum_ready, 1)
                    for row in (32, 96):
                        nc.vector.tensor_tensor(f_cum[row:row + 16, :], trans[0:16, 0:T], f_cum[0:16, :].bitcast(F32),
                                                ALU.subtract).then_inc(cum_ready, 1)
                if 5 <= s < 21:
                    norm_probs(s - 5, 0, f_prob, row_sum, inv_sum)
                if 4 <= s < 20:
                    maxima(s - 4, 0, f_logit, row_max, neg_max, FOX_SCALE)
                if 6 <= s and s % 2:
                    k = (s - 6) // 2
                    low_tile(AT["fctx"] + k, act_b[:, k, 1, :], misc[:, 0:T], act_b[:, k, 0, :])
            residual("FO", "ffn0", "FO")
            up("U0")
            down("D0", "ffn0", [("kv", act_b), ("mix1", act_a)], "D0")

            for n in range(6):
                c, j = C0["KVQ"] + n // 2, n % 2
                prep(c, j)
                if n == 0:
                    norm("mix1")
                m = n if n < 4 else n - 1
                scaled("KVQ", n, 2 * c + j + 1, m_kr_raw[:] if n == 4 else m_lat[:, m, :], "mix1")
                if n != 4:
                    g = gain("kv_a", m) if m < 2 else gain("q_a", m - 2)
                    low_tile(AT["lat"] + m, m_act[:, m, 1, :], m_lat[:, m, :], m_act[:, m, 0, :], g)
            norm("kv_a")
            for j in range(2):
                prep(C0["KB"], j)
                for n in range(4 * j, 4 * j + 4):
                    scaled("KB", n, 2 * C0["KB"] + j + 1, m_k[:, n, :], "kv_a")
            norm("q_a")
            for j in range(2):
                prep(C0["VB"], j)

            def rope(n):
                src = m_kr_raw[:] if n == 0 else m_qr_raw[:, n - 1, :]
                dst = m_kr[:] if n == 0 else m_qr[:, n - 1, :]
                if n:
                    dve.wait_ge(rope_step, 3 * n)
                nc.vector.tensor_tensor(m_cos[:], src, cos_t, ALU.mult).then_inc(rope_step, 1)
                dve.wait_ge(rot_done, n + 1)
                nc.vector.tensor_tensor(dst, trans[:, 0:T], sin_t, ALU.mult).then_inc(rope_step, 1)
                dve.wait_ge(rope_step, 3 * n + 2)
                nc.vector.tensor_tensor(dst, dst, m_cos[:], ALU.add).then_inc(rope_step, 1)

            for s in range(6):
                c, j = C0["QB"] + s // 2, s % 2
                prep(c, j)
                for n in range(2):
                    b = 2 * s + n
                    scaled("QB", b, 2 * c + j + 1, m_qr_raw[:, b, :] if b < 4 else m_q[:, b - 4, :], "q_a")
                if s == 1:
                    dve.wait_ge(dve_evac, DE["QB"] + 4)
                    rope(0)
                if s >= 2:
                    rope(s - 1)
            for s in range(MLA_H + 2):
                if 1 <= s <= MLA_H:
                    norm_probs(s - 1, FOX_H, m_prob, m_sum, m_inv)
                if s < MLA_H:
                    maxima(s, FOX_H, m_logit, m_max, m_nmax, MLA_SCALE)
                if s >= 2:
                    low_tile(AT["mctx"] + s - 2, act_b[:, s - 2, 1, :], misc[:, 0:T], act_b[:, s - 2, 0, :])
            residual("MO", "ffn1", "MO")
            up("U1")
            down("D1", "ffn1", [], None)
            norm("final1")

            for k in range(KD):
                nc.vector.scalar_tensor_tensor(out=x[:, k, :], in0=x[:, k, :], scalar=gain("final1", k),
                                               in1=rstd_of("final1")[:, 0:T], op0=ALU.mult, op1=ALU.mult).then_inc(resid_ready, 1)
                if k:
                    low_tile(AT["x1"] + k - 1, act_a[:, k - 1, 1, :], x[:, k - 1, :], act_a[:, k - 1, 0, :], gain("mix2", k - 1))
            low_tile(AT["x1"] + 7, act_a[:, 7, 1, :], x[:, 7, :], act_a[:, 7, 0, :], gain("mix2", 7))
            for j in range(2):
                prep(C0["GA"], j)
            norm("mix2")
            scaled("GA", 0, 2 * C0["GA"] + 2, g_aT[:], "mix2", rows=GATE_RANK)
            dve_step = [0]

            def step(last, wait=False):
                dve_step[0] += 1
                last.then_inc(gla_dve, 1)
                if wait:
                    dve.wait_ge(gla_dve, dve_step[0])

            def bcum(g):
                return score[g][:].rearrange("p (c s) -> p c s", s=GLA_C)

            for n in range(8):
                c, j = C0["GQK"] + n // 2, n % 2
                prep(c, j)
                scaled("GQK", n, 2 * c + j + 1, (g_q, g_k)[n // 4][:, n % 4, :], "mix2")
                if n == 0:
                    for t in range(TT):
                        dve.wait_ge(gla_pe, 1 + t)
                        dve.wait_ge(gla_small_landed, 32)
                        link(nc.vector.tensor_tensor(g_z[:, t, :], score[t][:], g_bias[:], ALU.add))
                        step(nc.vector.scalar_tensor_tensor(out=g_e[:, t, :], in0=g_z[:, t, :], scalar=-1.0, in1=g_z[:, t, :],
                                                            op0=ALU.mult, op1=ALU.min))
                if n == 4:
                    dve.wait_ge(gla_act, 2)
                    for t in range(TT):
                        step(nc.vector.scalar_tensor_tensor(out=g_z[:, t, :], in0=g_z[:, t, :], scalar=0.0, in1=g_e[:, t, :],
                                                            op0=ALU.min, op1=ALU.subtract))
            for g in range(2):
                dve.wait_ge(gla_act, 4 + 2 * g)
                hs = slice(2 * g, 2 * g + 2)
                cum = bcum(g)
                last_of = score[g][:].rearrange("p (c s) -> p c s", s=GLA_C)[:, :, GLA_C - 1:GLA_C]
                link(nc.vector.tensor_copy(g_last[:, 8 * g:8 * g + 8], last_of.squeeze(2)))
                step(nc.vector.tensor_tensor(
                    g_kd[:, hs, :].rearrange("p h (c s) -> p (h c) s", s=GLA_C),
                    g_last[:, 8 * g:8 * g + 8].unsqueeze(2).broadcast_to([P, 8, GLA_C]), cum, ALU.subtract))
            dve.wait_ge(dve_evac, DE["GQK"] + 8)
            step(nc.vector.tensor_tensor(g_ki[:], g_ki[:], g_k[:], ALU.mult))
            step(nc.vector.scalar_tensor_tensor(out=g_qi[:], in0=g_q[:], scalar=GLA_SCALE, in1=g_eb[:], op0=ALU.mult,
                                                op1=ALU.mult))
            step(nc.vector.memset(g_sT[:], 0.0))
            dve.wait_ge(gla_act, 7)
            step(nc.vector.tensor_tensor(g_kd[:], g_kd[:], g_k[:], ALU.mult))
            for n in range(4):
                for j in range(2):
                    prep(C0["GV"] + n, j)
            for n in range(8):
                c, j = C0["GG"] + n // 2, n % 2
                prep(c, j)
                if n == 1:
                    for t in range(TT):
                        dve.wait_ge(gla_pe, 5 + t)
                        dve.wait_ge(gla_dve, 9)
                        step(nc.vector.copy_predicated(
                            g_sT[:, t, :].rearrange("p (h s) -> p h s", h=GLA_H),
                            chunk_mask.unsqueeze(1).broadcast_to([P, GLA_H, P]),
                            score[t][:].rearrange("p (h s) -> p h s", h=GLA_H)))
                if n in (3, 4, 5):
                    m = n - 3
                    dve.wait_ge(gla_pe, 9 + m)
                    if m:
                        dve.wait_ge(gla_dve, 12 + 4 * m)
                    for h in range(GLA_H):
                        kv = score[h // 2][:, (h % 2) * T:(h % 2) * T + T]
                        if m == 0:
                            step(nc.vector.tensor_copy(g_s[:, 0, h, :], kv))
                        else:
                            decay = g_eb[:, h, m * GLA_C + GLA_C - 1:m * GLA_C + GLA_C]
                            step(nc.vector.scalar_tensor_tensor(out=g_s[:, m, h, :], in0=g_s[:, m - 1, h, :], scalar=decay,
                                                                in1=kv, op0=ALU.mult, op1=ALU.add))
                scaled("GG", n, 2 * c + j + 1, g_g[:, n, :], "mix2")
            for h in range(GLA_H):
                for e in range(2):
                    dve.wait_ge(gla_act, 9 + 2 * h + e + 1)
                    if h >= 2:
                        dve.wait_ge(gla_pe, 19 + h - 1)
                    step(nc.vector.tensor_tensor(tmp[:, 2 * (h % 2) + e, :], g_o[:, 2 * h + e, :], g_o[:, 2 * h + e, :],
                                                 ALU.mult))
            for g in range(2):
                dve.wait_ge(gla_pe, 21 + 2 * g)
                step(nc.vector.tensor_scalar(tmp2[:, 2 * g:2 * g + 2, :], score[g][:].rearrange("p (h t) -> p h t", h=2),
                                             1.0 / GLA_DV, EPS, ALU.mult, ALU.add))
            for g in range(2):
                dve.wait_ge(gla_act, 18 + g)
                step(nc.vector.reciprocal(tmp2[:, 2 * g:2 * g + 2, :], tmp2[:, 2 * g:2 * g + 2, :]), wait=True)
            for m in range(KD):
                link(nc.vector.scalar_tensor_tensor(out=g_o[:, m, :], in0=g_o[:, m, :], scalar=gain("head", m),
                                                    in1=tmp2[:, m // 2, :], op0=ALU.mult, op1=ALU.mult))
                dve.wait_ge(silu_ready, SL["GG"] + m + 1)
                nc.vector.tensor_tensor(g_o[:, m, :], g_o[:, m, :], g_g[:, m, :], ALU.mult).then_inc(gated_ready, 1)
                if m:
                    low_tile(AT["gla"] + m - 1, act_b[:, m - 1, 1, :], g_o[:, m - 1, :], act_b[:, m - 1, 0, :])
            low_tile(AT["gla"] + 7, act_b[:, 7, 1, :], g_o[:, 7, :], act_b[:, 7, 0, :])
            residual("GO", None, None)
            norm("ffn2")
            normed("GO", "ffn2")

            conv_up("CU0", "conv0")
            conv_down("CD0", "mix3", "CD0")
            for n in range(24):
                c, j = C0["SI"] + n // 2, n % 2
                prep(c, j)
                if n == 0:
                    norm("mix3")
                    link(nc.vector.tensor_tensor(rstd_sq[:], rstd_of("mix3")[:, 0:T], rstd_of("mix3")[:, 0:T], ALU.mult))
                g, part = n // 6, (n % 6) // 2
                m = 2 * g + j
                ps = bank_of("SI", n)[:, 0:T]
                if part == 1:
                    dve.wait_ge(act_evac, AE["SI"] + m + 1)
                    dve.wait_ge(half_done, 2 * c + j + 1)
                    nc.vector.tensor_tensor(tmp2[:, 2 + j, :], ps, s_c[:, j, :], ALU.mult).then_inc(dve_evac, 1)
                    dve.wait_ge(dve_evac, DE["SI"] + 4 * g + j + 1)
                    nc.vector.tensor_tensor(tmp2[:, j, :], tmp2[:, 2 + j, :], rstd_sq[:], ALU.mult).then_inc(sc_ready, 1)
                    y, v = tmp[:, j, :], tmp2[:, j, :]
                    dve.wait_ge(tap_ready, CV["SI"] + m + 1)
                    nc.vector.scalar_tensor_tensor(out=y[:, 1:T], in0=v[:, 0:T - 1], scalar=gain("sc_conv", 3 * m + 1),
                                                   in1=y[:, 1:T], op0=ALU.mult, op1=ALU.add).then_inc(tap_mid, 1)
                    dve.wait_ge(tap_mid, CV["SI"] + m + 1)
                    link(nc.vector.scalar_tensor_tensor(out=y[:, 2:T], in0=v[:, 0:T - 2], scalar=gain("sc_conv", 3 * m),
                                                        in1=y[:, 2:T], op0=ALU.mult, op1=ALU.add))
                    link(nc.vector.tensor_tensor(y, y, rstd_of("mix3")[:, 0:T], ALU.mult))
                if part == 2:
                    dve.wait_ge(half_done, 2 * c + j + 1)
                    if g:
                        dve.wait_ge(act_ready, AT["sc"] + m - 2 + 1)
                    nc.vector.tensor_tensor(tmp[:, 2 + j, :], ps, tmp[:, j, :], ALU.mult).then_inc(dve_evac, 1)
                    low_tile(AT["sc"] + m, act_b[:, m, 1, :], tmp[:, 2 + j, :], act_b[:, m, 0, :])
            residual("SO", None, None)
            norm("ffn3")
            normed("SO", "ffn3")
            conv_up("CU1", "conv1")
            conv_down("CD1", None, None)
            norm("final2")
            for k in range(KD):
                nc.vector.scalar_tensor_tensor(out=x[:, k, :], in0=x[:, k, :], scalar=gain("final2", k),
                                               in1=rstd_of("final2")[:, 0:T], op0=ALU.mult, op1=ALU.mult).then_inc(resid_ready, 1)


_WEIGHTS = ["fox_w_in", "fox_b_f", "fox_w_out", "mla_w_kv_a", "mla_w_kv_b", "mla_w_q_a", "mla_w_q_b", "mla_w_out",
            "ffn_w_up", "ffn_w_down", "gla_w_in_2", "gla_w_gate_up_2", "gla_b_gate_2", "gla_w_out_2", "sc_w_in_2",
            "sc_w_out_2", "ffn_w_up_2", "ffn_w_down_2"]


def kernel(**inputs):
    import concourse.bacc as bacc
    from concourse.bass_utils import run_bass_kernel_spmd

    a = {name: np.ascontiguousarray(v) for name, v in inputs.items()}
    tiles = lambda v: v.reshape(-1, P).T
    taps = lambda v: v.reshape(-1, P, 3).transpose(1, 0, 2).reshape(P, -1)
    vec = np.concatenate(
        [tiles(v) for v in (a["norm_mix_g"][0], a["norm_ffn_g"][0], a["kv_norm_g"], a["norm_mix_g"][1], a["norm_ffn_g"][1],
                            a["final_norm_g"], a["norm_mix_g_2"][0], a["norm_ffn_g_2"][0], a["norm_mix_g_2"][1],
                            a["norm_ffn_g_2"][1], a["final_norm_g_2"], a["mla_kv_a_norm_g"], a["mla_q_a_norm_g"][0],
                            a["gla_head_norm_g_2"][0])]
        + [taps(a["sc_conv_w_2"][0]), taps(a["ffn_conv_w_2"][0]), taps(a["ffn_conv_w_2"][1])], axis=1)
    con, sel = shape_constants()
    arrays = {name: a[name] for name in _WEIGHTS}
    arrays.update(xT=np.ascontiguousarray(a["x"][0].T), vec=np.ascontiguousarray(vec), con=con, sel=sel)
    nc = bacc.Bacc("TRN2", target_bir_lowering=False, num_devices=1)
    io = {name: nc.dram_tensor(f"in_{name}", v.shape, mybir.dt.from_np(v.dtype), kind="ExternalInput").ap()
          for name, v in arrays.items()}
    io["out"] = nc.dram_tensor("outT", (D, T), F32, kind="ExternalOutput").ap()
    build(nc, io)
    r = run_bass_kernel_spmd(nc, [{f"in_{name}": v for name, v in arrays.items()}], core_ids=[0])
    return np.ascontiguousarray(r.results[0]["outT"].T).reshape(1, T, D)
```

```python
from contextlib import ExitStack

import numpy as np

import concourse.bass as bass
from concourse import mybir

F32 = mybir.dt.float32
F32R = mybir.dt.float32r
U32 = mybir.dt.uint32
ALU = mybir.AluOpType
ACT = mybir.ActivationFunctionType
ds = bass.ds

P = 128
T = 256
TT = T // P
D = 1024
KD = D // P
EPS = 1e-6
FOX_H, FOX_DH = 16, 64
MLA_H, NOPE, ROPE, VDIM = 8, 128, 64, 128
QLORA, KVLORA = 384, 256
DFF = 4 * D
DFF2 = 2816
NT2 = DFF2 // P
GLA_H, GLA_DK, GLA_DV, GLA_C = 4, 128, 256, 64
GATE_RANK, GATE_TAU = 16, 16.0
FOX_SCALE = FOX_DH ** -0.5
MLA_SCALE = (NOPE + ROPE) ** -0.5
GLA_SCALE = GLA_DK ** -0.5
MASKED = -1.0e30

CW = 256
CHUNK = KD * CW
RAW_SLOTS = 4
W_SLOTS = 2
AHEAD = 3
FOX_T = 14
CD_K = (6, 6, 5, 5)

STAGES = [("FG", 1), ("FQK", 8), ("FV", 4), ("FO", 4), ("U0", 16), ("D0", 16), ("KVQ", 3), ("KB", 1), ("QR", 1),
          ("QA", 1), ("VB", 1), ("QN", 1), ("MO", 4), ("U1", 16), ("D1", 16), ("GA", 1), ("GQK", 4), ("GV", 4), ("GG", 4), ("GO", 4),
          ("CU0", 22), ("CD0", 16), ("SI", 12), ("SO", 4), ("CU1", 22), ("CD1", 16)]
C0 = {}
N_CHUNKS = 0
for _name, _n in STAGES:
    C0[_name] = N_CHUNKS
    N_CHUNKS += _n

VEC = {}
N_VEC = 0
for _name, _n in [("mix0", 8), ("ffn0", 8), ("kv", 8), ("mix1", 8), ("ffn1", 8), ("final1", 8), ("mix2", 8),
                  ("ffn2", 8), ("mix3", 8), ("ffn3", 8), ("final2", 8), ("kv_a", 2), ("q_a", 3), ("head", 8),
                  ("sc_conv", 24), ("conv0", 132), ("conv1", 132)]:
    VEC[_name] = N_VEC
    N_VEC += _n

VEC["x1"] = N_VEC
VEC["final1_sq"] = N_VEC + KD

CON = {}
N_CON = 0
for _name, _n in [("ones", 128), ("ident", 128), ("mask", 256), ("tri", 512), ("tri_chunk", 128), ("cos", 256),
                  ("sin", 256), ("rot", 128), ("chunk_mask", 128), ("pick", FOX_H)]:
    CON[_name] = N_CON
    N_CON += _n


def shape_constants():
    con = np.zeros((P, N_CON), np.float32)
    at = lambda name, n: con[:, CON[name]:CON[name] + n]
    i = np.arange(P)
    at("ones", 128)[:] = 1.0
    at("ident", 128)[:] = np.eye(P)
    at("mask", 256)[:, 128:] = np.where(i[None, :] <= i[:, None], 0.0, MASKED)
    tri = np.where(np.arange(T)[:, None] <= np.arange(T)[None, :], -1.0 / FOX_SCALE, 0.0)
    at("tri", 512)[:] = tri.reshape(TT, P, T).transpose(1, 0, 2).reshape(P, 512)
    same = (i[:, None] // GLA_C) == (i[None, :] // GLA_C)
    upto = same & (i[:, None] <= i[None, :])
    at("tri_chunk", 128)[:] = np.where(upto, 1.0 / GATE_TAU, 0.0)
    at("chunk_mask", 128)[:] = np.where(upto, 1.0, 0.0)
    inv = (1.0 / (np.float32(10000.0) ** (np.arange(0, ROPE, 2, dtype=np.float32) / np.float32(ROPE)))).astype(np.float32)
    ang = np.arange(T, dtype=np.float32)[:, None] * inv[None, :]
    at("cos", 256)[:] = np.tile(np.cos(ang).T, (4, 1))
    at("sin", 256)[:] = np.tile(np.sin(ang).T, (4, 1))
    half = ROPE // 2
    for m in range(P):
        if m % ROPE < half:
            at("rot", 128)[m + half, m] = -1.0
        else:
            at("rot", 128)[m - half, m] = 1.0
    for h in range(FOX_H):
        at("pick", FOX_H)[[64 * (h % 2) + h, 64 * (h % 2) + 32 + h], h] = 1.0
    return con


def build(nc, io):
    ctx = ExitStack()
    with ctx:
        used = [16512]

        def sb(name, shape, dt=F32, at=None):
            n = int(np.prod(shape[1:])) * 4
            if at is None:
                at = used[0]
                used[0] += (n + 31) // 32 * 32
            return nc.alloc_sbuf_tensor_at(name, shape, dt, offset=at)

        def bank(name):
            return ctx.enter_context(nc.psum_tensor(name, [P, 512], F32))

        def sem(name):
            return ctx.enter_context(nc.semaphore(name))

        w_raw = sb("w_raw", [P, RAW_SLOTS, CHUNK])
        w_hi = sb("w_hi", [P, W_SLOTS, CHUNK], F32R)
        w_lo = sb("w_lo", [P, W_SLOTS, CHUNK], F32R)
        x = sb("x", [P, KD, T])
        act_a = sb("act_a", [P, KD, 2, T], F32R)
        act_b = sb("act_b", [P, KD, 2, T], F32R)
        vec = sb("vec", [P, N_VEC + 2 * KD])
        con = sb("con", [P, N_CON])
        ssq = sb("ssq", [P, T])
        sqt = sb("sqt", [P, T])
        ssq_x1 = sb("ssq_x1", [P, T])
        sqt_x1 = sb("sqt_x1", [P, T])
        var = sb("var", [P, T + TT])
        var_x1 = sb("var_x1", [P, T + TT])
        std = sb("std", [P, T + TT])
        rstd = sb("rstd", [P, 3, T + TT])
        tmp = sb("tmp", [P, 4, T])
        tmp2 = sb("tmp2", [P, 4, T])
        rstd_sq = sb("rstd_sq", [P, T])
        g_last = sb("g_last", [P, GLA_H * (T // GLA_C)])
        arena = used[0]

        def overlay():
            used[0] = arena

        overlay()
        hid = sb("hid", [P, DFF // P, 2, T], F32R)
        end_hid = used[0]
        overlay()
        f_q = sb("f_q", [P, KD, T])
        f_k = sb("f_k", [P, KD, T])
        f_v = sb("f_v", [P, TT, D])
        f_logit = sb("f_logit", [P, 2, 384])
        f_prob = sb("f_prob", [P, 3, 384])
        f_probT = sb("f_probT", [P, FOX_T, 384])
        f_sel = sb("f_sel", [P, FOX_H, P], F32R)
        f_cum = sb("f_cum", [P, T], F32R)
        f_bias = sb("f_bias", [P, FOX_H])
        f_z = sb("f_z", [P, TT, FOX_H])
        f_neg_abs = sb("f_neg_abs", [P, TT, FOX_H])
        f_exp = sb("f_exp", [P, TT, FOX_H])
        f_ln = sb("f_ln", [P, TT, FOX_H])
        f_ls = sb("f_ls", [P, TT, FOX_H])
        row_max = sb("row_max", [P, 2, 2])
        neg_max = sb("neg_max", [P, 2, 2])
        row_sum = sb("row_sum", [P, 3, 2])
        inv_sum = sb("inv_sum", [P, 3, 2])
        assert used[0] <= end_hid
        overlay()
        m_q = sb("m_q", [P, MLA_H, T])
        m_k = sb("m_k", [P, MLA_H, T])
        m_v = sb("m_v", [P, TT, D])
        m_qr_raw = sb("m_qr_raw", [P, 4, T])
        m_qr = sb("m_qr", [P, 4, T])
        m_kr_raw = sb("m_kr_raw", [P, T])
        m_kr = sb("m_kr", [P, T])
        m_lat = sb("m_lat", [P, 5, T])
        m_act = sb("m_act", [P, 5, 2, T], F32R)
        m_logit = sb("m_logit", [P, 2, 384])
        m_prob = sb("m_prob", [P, 3, 384])
        m_probT = sb("m_probT", [P, 2, 384])
        m_max = sb("m_max", [P, 2, 2])
        m_nmax = sb("m_nmax", [P, 2, 2])
        m_sum = sb("m_sum", [P, 3, 2])
        m_inv = sb("m_inv", [P, 3, 2])
        assert used[0] <= end_hid
        overlay()
        g_q = sb("g_q", [P, GLA_H, T])
        g_k = sb("g_k", [P, GLA_H, T])
        g_v = sb("g_v", [P, TT, D])
        g_z = sb("g_z", [P, TT, 512])
        g_e = sb("g_e", [P, TT, 512])
        g_s = sb("g_s", [P, 3, GLA_H, GLA_DV])
        g_eb = sb("g_eb", [P, GLA_H, T])
        g_ki = sb("g_ki", [P, GLA_H, T])
        g_kd = sb("g_kd", [P, GLA_H, T])
        g_qi = sb("g_qi", [P, GLA_H, T])
        g_kdT = sb("g_kdT", [P, TT, 512])
        g_sT = sb("g_sT", [P, TT, 512])
        g_aT = sb("g_aT", [GATE_RANK, T])
        g_var = sb("g_var", [P, GLA_H * TT])
        g_std = sb("g_std", [P, GLA_H * TT])
        g_rec = sb("g_rec", [P, GLA_H * TT])
        end_gla = used[0]
        g_o = nc.alloc_sbuf_tensor_at("g_o", [P, KD, T], F32, offset=arena)
        g_g = nc.alloc_sbuf_tensor_at("g_g", [P, KD, T], F32, offset=arena + 16384)
        overlay()
        used[0] = max(end_hid, end_gla)
        g_up = sb("g_up", [GATE_RANK, 512])
        g_bias = sb("g_bias", [P, 512])
        s_c = sb("s_c", [P, 2, T])
        assert used[0] <= nc.sbuf_usable_end, used[0]

        gemm = [bank(f"gemm{i}") for i in range(4)]
        score = [bank("score0"), bank("score1")]
        trans = bank("trans")
        misc = bank("misc")

        gla_bank = [trans, score[0], score[1], misc]
        rot_place = [b[:, 0:T] for b in (trans, score[0], score[1], trans, score[0])]

        ones = con[:, CON["ones"]:CON["ones"] + 128]
        ident = con[:, CON["ident"]:CON["ident"] + 128]
        mask = con[:, CON["mask"]:CON["mask"] + 256]
        tri = con[:, CON["tri"]:CON["tri"] + 512].rearrange("p (t n) -> p t n", t=TT)
        tri_chunk = con[:, CON["tri_chunk"]:CON["tri_chunk"] + 128]
        cos_t = con[:, CON["cos"]:CON["cos"] + 256]
        sin_t = con[:, CON["sin"]:CON["sin"] + 256]
        pick = con[:, CON["pick"]:CON["pick"] + FOX_H]
        rot = con[:, CON["rot"]:CON["rot"] + 128]
        chunk_mask = con[:, CON["chunk_mask"]:CON["chunk_mask"] + 128].bitcast(U32)

        def gain(name, k):
            return vec[:, VEC[name] + k:VEC[name] + k + 1]

        x_landed = [sem("x_landed0"), sem("x_landed1")]
        vec_landed = sem("vec_landed")
        con_landed = sem("con_landed")
        fox_small_landed = sem("fox_small_landed")
        gla_small_landed = sem("gla_small_landed")
        raw_landed = [sem(f"raw_landed{s}") for s in range(RAW_SLOTS)]
        w_hi_ready = sem("w_hi_ready")
        w_lo_ready = sem("w_lo_ready")
        half_done = sem("half_done")
        act_evac = sem("act_evac")
        dve_evac = sem("dve_evac")
        resid_ready = sem("resid_ready")
        act_hi_ready = sem("act_hi_ready")
        act_ready = sem("act_ready")
        pool_sq = sem("pool_sq")
        gains_ready = sem("gains_ready")
        x1_scaled = sem("x1_scaled")
        x1_sum = sem("x1_sum")
        gla_zeroed = sem("gla_zeroed")
        pool_sum = sem("pool_sum")
        stat_done = sem("stat_done")
        var_ready = sem("var_ready")
        std_ready = sem("std_ready")
        rstd_ready = sem("rstd_ready")
        sq_ready = sem("sq_ready")
        tap_ready = sem("tap_ready")
        tap_mid = sem("tap_mid")
        conv_done = sem("conv_done")
        silu_ready = sem("silu_ready")
        gated_ready = sem("gated_ready")
        scores_done = sem("scores_done")
        logits_ready = sem("logits_ready")
        negmax_ready = sem("negmax_ready")
        probs_ready = sem("probs_ready")
        invsum_ready = sem("invsum_ready")
        probs_normed = sem("probs_normed")
        transposed = sem("transposed")
        probsT_ready = sem("probsT_ready")
        pv_done = sem("pv_done")
        gate_step = sem("gate_step")
        cum_done = sem("cum_done")
        cum_ready = sem("cum_ready")
        rot_done = sem("rot_done")
        rope_step = sem("rope_step")
        rope_cos = sem("rope_cos")
        sel_ready = sem("sel_ready")
        gla_pe = sem("gla_pe")
        gla_act = sem("gla_act")
        gla_dve = sem("gla_dve")
        head_normed = sem("head_normed")
        sc_ready = sem("sc_ready")
        dve_own = sem("dve_own")
        out_landed = sem("out_landed")

        STRAIGHT = (0, 0, 0)

        def halves_before(c, j, it=STRAIGHT):
            return 2 * c + j + 2 * it[1] * it[0]

        DE, AE = {}, {}
        n_d = n_a = 0
        for name, d, a in [("FG", 2, 0), ("FQK", 16, 0), ("FV", 0, 8), ("FO", 8, 0), ("U0", 0, 32), ("D0", 8, 0),
                           ("KVQ", 6, 0), ("KB", 8, 0), ("QR", 4, 0), ("QA", 4, 0), ("VB", 0, 4), ("QN", 4, 0), ("MO", 8, 0), ("U1", 0, 32),
                           ("D1", 8, 0), ("GA", 1, 0), ("GQK", 8, 0), ("GV", 0, 8), ("GG", 8, 0), ("GO", 8, 0),
                           ("CU0", 44, 0), ("CD0", 8, 0), ("SI", 16, 8), ("SO", 8, 0), ("CU1", 44, 0), ("CD1", 8, 0)]:
            DE[name], AE[name] = n_d, n_a
            n_d, n_a = n_d + d, n_a + a
        AT = {}
        n_t = 0
        for name, n in [("x", 8), ("fctx", 8), ("FO", 8), ("U0", 32), ("D0", 16), ("lat", 5), ("mctx", 8), ("MO", 8),
                        ("U1", 32), ("x1", 8), ("gla", 8), ("GO", 8), ("CU0", 22), ("CD0", 8), ("sc", 8), ("SO", 8),
                        ("CU1", 22)]:
            AT[name] = n_t
            n_t += n
        GT = {}
        n_t = 0
        for name, n in [("gla", 8), ("CU0", 22), ("CU1", 22)]:
            GT[name] = n_t
            n_t += n
        RT = {"D0": 0, "D1": 8, "x1": 16}
        SQ = {"U0": 0, "U1": 32}
        TURN = {}
        n_t = 0
        for name, n in [("FG", 2), ("FQK", 16), ("FV", 8), ("FO", 8), ("U0", 32), ("D0", 2), ("KVQ", 6), ("KB", 8),
                        ("QR", 4), ("QA", 4), ("VB", 4), ("QN", 4), ("MO", 8), ("U1", 32), ("D1", 2), ("GA", 1), ("GQK", 8), ("GV", 8),
                        ("GG", 8), ("GO", 8), ("CU0", 44), ("CD0", 2), ("SI", 24), ("SO", 8), ("CU1", 44), ("CD1", 2)]:
            TURN[name] = n_t
            n_t += n

        def bank_of(stage, n):
            return gemm[(TURN[stage] + n) % 4]

        def tmp_of(k):
            return (tmp, tmp2)[k // 4][:, k % 4, :]

        CV = {"CU0": 0, "SI": 44, "CU1": 52}
        CONV = {"CU0": 0, "CU1": 44}
        SL = {"GG": 0, "CU0": 8, "CU1": 30}
        NORMS = {}
        n_t = 0
        for n, (name, tiles, tok, feats) in enumerate(
                [("mix0", 8, True, D), ("ffn0", 8, False, D), ("mix1", 8, False, D), ("kv_a", 2, True, KVLORA),
                 ("q_a", 3, False, QLORA), ("ffn1", 8, False, D), ("final1", 8, True, D), ("mix2", 0, True, D),
                 ("ffn2", 8, False, D), ("mix3", 8, False, D), ("ffn3", 8, False, D), ("final2", 8, False, D)]):
            NORMS[name] = (n, tiles, n_t, tok, feats)
            n_t += tiles
        ROOTS = ["mix0", "mix1", "kv_a", "q_a", "mix2", "final1", "ffn2", "mix3", "ffn3", "final2"]

        def sums_before(name):
            n, _, tiles_before, _, _ = NORMS[name]
            return tiles_before + n - (n > NORMS["mix2"][0])

        def rstd_of(name):
            return rstd[:, NORMS[name][0] % 3, :]

        def chunk_view(t, slot, kind):
            k = {"full": 8, "narrow": 8, "lat": 3, "kvb": 2}[kind]
            n = {"full": 256, "narrow": 128, "lat": 512, "kvb": 1024}[kind]
            return t[:, slot, 0:k * n].rearrange("p (k n) -> p k n", k=k)

        def kind_of(c):
            if c == C0["FG"]:
                return "narrow", 8
            if c in (C0["QR"], C0["QA"], C0["QN"]):
                return "lat", 3
            if c in (C0["KB"], C0["VB"]):
                return "kvb", 2
            for s in ("CD0", "CD1"):
                if C0[s] <= c < C0[s] + 16:
                    return "full", CD_K[(c - C0[s]) % 4]
            return "full", 8

        HALF = {"full": 128, "narrow": 64, "lat": 256, "kvb": 512}

        def raw_half(c, j):
            kind, nk = kind_of(c)
            w = HALF[kind]
            return chunk_view(w_raw, c % RAW_SLOTS, kind)[:, 0:nk, j * w:(j + 1) * w]

        def split_half(t, c, j):
            kind, nk = kind_of(c)
            w = HALF[kind]
            at = j * (CHUNK // 2)
            return t[:, c % W_SLOTS, at:at + nk * w].rearrange("p (k n) -> p k n", k=nk)

        def ahead(c, j):
            h = 2 * c + j + AHEAD
            return (h // 2, h % 2) if h < 2 * N_CHUNKS else None

        block = ctx.enter_context(nc.Block())

        @block.sync
        def _(sp):
            def load(c, parts, it=STRAIGHT):
                if c >= RAW_SLOTS:
                    sp.wait_ge(w_lo_ready, halves_before(c - RAW_SLOTS + 1, 0, it))
                assert len(parts) == 1
                for dst, src in parts:
                    sp.dma_start(dst, src).then_inc(raw_landed[c % RAW_SLOTS], 16)

            def ktiles(w):
                return w.rearrange("(k p) n -> p k n", p=P)

            def full(c):
                return chunk_view(w_raw, c % RAW_SLOTS, "full")

            def plain(stage, w, cols):
                for j, col in enumerate(cols):
                    c = C0[stage] + j
                    load(c, [(full(c), ktiles(w)[:, :, col:col + CW])])

            def up(stage, w):
                with sp.Fori(0, 4) as i:
                    for cc in range(4):
                        c = C0[stage] + cc
                        load(c, [(full(c), ktiles(w)[:, :, ds(i * (4 * CW) + cc * CW, CW)])], (i, 4, 8))

            def down(stage, w):
                with sp.Fori(0, 4) as i:
                    for cc in range(4):
                        c = C0[stage] + cc
                        load(c, [(full(c), ktiles(w)[:, 8 * cc:8 * cc + 8, ds(i * CW, CW)])], (i, 4, 2))

            def conv_up(stage, w):
                def body(i, cc, it):
                    c = C0[stage] + cc
                    col = (cc // 2) * CW + (cc % 2) * DFF2 + i * (2 * CW)
                    src = ktiles(w)[:, :, ds(col, CW)] if it[1] else ktiles(w)[:, :, col:col + CW]
                    load(c, [(full(c), src)], it)

                for cc in range(2):
                    body(0, cc, STRAIGHT)
                with sp.Fori(0, 5) as i:
                    for cc in range(2, 6):
                        body(i, cc, (i, 4, 8))

            def conv_down(stage, w):
                def body(i, cc, it):
                    c = C0[stage] + cc
                    k0, nk = sum(CD_K[:cc % 4]), CD_K[cc % 4]
                    cols = ds(i * CW, CW) if it[1] else slice((cc // 4) * CW, (cc // 4 + 1) * CW)
                    load(c, [(full(c)[:, 0:nk, :], ktiles(w)[:, k0:k0 + nk, cols])], it)

                with sp.Fori(0, 3) as i:
                    for cc in range(4):
                        body(i, cc, (i, 4, 2))
                for cc in range(12, 16):
                    body(0, cc, STRAIGHT)

            w = io["fox_w_in"][0]
            load(C0["FG"], [(chunk_view(w_raw, 0, "narrow"), ktiles(w)[:, :, 3 * D + FOX_H - P:3 * D + FOX_H])])
            for k in range(0, KD, 4):
                sp.dma_start(x[:, k:k + 4, :], ktiles(io["xT"])[:, k:k + 4, :]).then_inc(x_landed[k // 4], 16)
            plain("FQK", w, [CW * (j // 2) + D * (j % 2) for j in range(8)])
            plain("FV", w, [2 * D + CW * j for j in range(4)])
            plain("FO", io["fox_w_out"][0], [CW * j for j in range(4)])
            up("U0", io["ffn_w_up"][0])
            down("D0", io["ffn_w_down"][0])
            c = C0["KVQ"]
            wkv, wq = ktiles(io["mla_w_kv_a"]), ktiles(io["mla_w_q_a"][0])
            load(c, [(full(c), wkv[:, :, 0:KVLORA])])
            load(c + 1, [(full(c + 1), wq[:, :, 0:256])])
            sp.wait_ge(w_lo_ready, halves_before(c + 2 - RAW_SLOTS + 1, 0))
            for dst, src in [(full(c + 2)[:, :, 0:64], wkv[:, :, KVLORA:KVLORA + ROPE]),
                             (full(c + 2)[:, :, 64:128], wkv[:, :, KVLORA:KVLORA + ROPE]),
                             (full(c + 2)[:, :, 128:256], wq[:, :, 256:384])]:
                sp.dma_start(dst, src).then_inc(raw_landed[(c + 2) % RAW_SLOTS], 16)
            wkvb = io["mla_w_kv_b"].rearrange("(k p) (h n) -> p k h n", p=P, h=MLA_H)
            wqb = io["mla_w_q_b"][0].rearrange("(k p) (h n) -> p k h n", p=P, h=MLA_H)
            for stage, w, heads, cols in (("KB", wkvb, slice(0, 8), slice(0, NOPE)), ("QR", wqb, slice(0, 8), slice(NOPE, NOPE + ROPE)),
                                          ("QA", wqb, slice(0, 4), slice(0, NOPE)), ("VB", wkvb, slice(0, 8), slice(NOPE, NOPE + VDIM)),
                                          ("QN", wqb, slice(4, 8), slice(0, NOPE))):
                c = C0[stage]
                kind, nk = kind_of(c)
                sp.wait_ge(w_lo_ready, halves_before(c - RAW_SLOTS + 1, 0))
                for k in range(nk):
                    dst = chunk_view(w_raw, c % RAW_SLOTS, kind)[:, k, :].rearrange("p (h n) -> p h n", h=heads.stop - heads.start)
                    sp.dma_start(dst, w[:, k, heads, cols]).then_inc(raw_landed[c % RAW_SLOTS], 16)
            plain("MO", io["mla_w_out"][0], [CW * j for j in range(4)])
            up("U1", io["ffn_w_up"][1])
            down("D1", io["ffn_w_down"][1])
            w = io["gla_w_in_2"][0]
            c = C0["GA"]
            load(c, [(full(c)[:, :, 0:GATE_RANK], ktiles(w)[:, :, 3 * D:3 * D + GATE_RANK])])
            plain("GQK", w, [CW * j for j in range(4)])
            plain("GV", w, [D + CW * j for j in range(4)])
            plain("GG", w, [2 * D + CW * j for j in range(4)])
            plain("GO", io["gla_w_out_2"][0], [CW * j for j in range(4)])
            conv_up("CU0", io["ffn_w_up_2"][0])
            conv_down("CD0", io["ffn_w_down_2"][0])
            plain("SI", io["sc_w_in_2"][0], [CW * (j // 3) + D * ((j % 3 + 1) % 3) for j in range(12)])
            plain("SO", io["sc_w_out_2"][0], [CW * j for j in range(4)])
            conv_up("CU1", io["ffn_w_up_2"][1])
            conv_down("CD1", io["ffn_w_down_2"][1])
            sp.wait_ge(resid_ready, RT["x1"] + 16)
            sp.dma_start(io["out"].rearrange("(k p) t -> p k t", p=P), x[:]).then_inc(out_landed, 16)
            sp.wait_ge(out_landed, 16)

        @block.gpsimd
        def _(pool):
            zeroed = [0]

            def zero(name):
                n, tiles, before, _, _ = NORMS[name]
                if n:
                    pool.wait_ge(stat_done, n)
                nc.gpsimd.memset(ssq[:], 0.0).then_inc(pool_sum, 1)

            def add(name, m, tile, i=0, step=0):
                n, tiles, before, _, _ = NORMS[name]
                t = before + m + step * i
                pool.wait_ge(pool_sum, sums_before(name) + 1 + m + step * i)
                nc.gpsimd.tensor_tensor(sqt[:], tile, tile, ALU.mult).then_inc(pool_sq, 1)
                pool.wait_ge(pool_sq, t + 1)
                nc.gpsimd.tensor_tensor(ssq[:], ssq[:], sqt[:], ALU.add).then_inc(pool_sum, 1)

            def straight(name, sig, base):
                zero(name)
                for m in range(KD):
                    pool.wait_ge(sig, base + m + 1)
                    add(name, m, x[:, m, :])

            def looped(name, sig, base):
                zero(name)
                with pool.Fori(0, 4) as i:
                    for j in range(2):
                        pool.wait_ge(sig, base + j + 1 + 2 * i)
                        add(name, j, x[:, ds(2 * i + j, 1), :], i, 2)

            def gate(stage):
                def tile(t, i):
                    n = 4 * (t // 2) + 2 + t % 2
                    y = tmp[:, n % 4, :]
                    hi, lo = (hid[:, t, k, :] if isinstance(i, int) else hid[:, ds(4 * i + t, 1), k, :] for k in range(2))
                    pool.wait_ge(conv_done, CONV[stage] + n + 1 + 8 * i)
                    pool.wait_ge(silu_ready, SL[stage] + t + 1 + 4 * i)
                    nc.gpsimd.tensor_tensor(y, y, tmp2[:, n % 2, :], ALU.mult).then_inc(gated_ready, 1)
                    pool.wait_ge(act_hi_ready, AT[stage] + t + 1 + 4 * i)
                    nc.gpsimd.tensor_tensor(lo, y, hi.bitcast(F32), ALU.subtract).then_inc(act_ready, 1)

                for t in range(2):
                    tile(t, 0)
                with pool.Fori(0, 5) as i:
                    for t in range(2, 6):
                        tile(t, i)

            zero("mix0")
            for m in range(KD):
                pool.wait_ge(x_landed[m // 4], 16)
                add("mix0", m, x[:, m, :])
            straight("ffn0", dve_evac, DE["FO"])
            looped("mix1", resid_ready, RT["D0"])
            zero("kv_a")
            for m in range(2):
                pool.wait_ge(dve_evac, DE["KVQ"] + m + 1)
                add("kv_a", m, m_lat[:, m, :])
            zero("q_a")
            for m in range(3):
                pool.wait_ge(dve_evac, DE["KVQ"] + (3, 4, 6)[m])
                add("q_a", m, m_lat[:, 2 + m, :])
            for n in range(5):
                pool.wait_ge(dve_evac, DE["KVQ"] + 5 if n == 0 else DE["QR"] + n)
                if n == 0:
                    pool.wait_ge(act_ready, AT["lat"] + 5)
                nc.gpsimd.tensor_tensor(m_lat[:, n, :], m_kr_raw[:] if n == 0 else m_qr_raw[:, n - 1, :], cos_t,
                                        ALU.mult).then_inc(rope_cos, 1)
            straight("ffn1", dve_evac, DE["MO"])
            zero("final1")
            nc.gpsimd.memset(ssq_x1[:], 0.0).then_inc(x1_sum, 1)
            pool.wait_ge(gains_ready, 2)
            before, sums = NORMS["final1"][2], sums_before("final1")
            with pool.Fori(0, 4) as i:
                for j in range(2):
                    pool.wait_ge(resid_ready, RT["D1"] + j + 1 + 2 * i)
                    t = ds(2 * i + j, 1)
                    pool.wait_ge(pool_sum, sums + 1 + j + 2 * i)
                    nc.gpsimd.tensor_tensor(sqt[:], x[:, t, :], x[:, t, :], ALU.mult).then_inc(pool_sq, 1)
                    pool.wait_ge(pool_sq, before + j + 1 + 2 * i)
                    pool.wait_ge(x1_sum, 1 + j + 2 * i)
                    gain_sq = vec[:, ds(2 * i + VEC["final1_sq"] + j, 1)]
                    nc.gpsimd.tensor_tensor(sqt_x1[:], sqt[:], gain_sq.broadcast_to([P, T]), ALU.mult).then_inc(x1_scaled, 1)
                    pool.wait_ge(x1_scaled, 1 + j + 2 * i)
                    nc.gpsimd.tensor_tensor(ssq_x1[:], ssq_x1[:], sqt_x1[:], ALU.add).then_inc(x1_sum, 1)
                    nc.gpsimd.tensor_tensor(ssq[:], ssq[:], sqt[:], ALU.add).then_inc(pool_sum, 1)
            pool.wait_ge(dve_evac, DE["GQK"] + 1)
            nc.gpsimd.memset(g_sT[:], 0.0).then_inc(gla_zeroed, 1)
            straight("ffn2", dve_evac, DE["GO"])
            gate("CU0")
            straight("mix3", dve_evac, DE["CD0"])
            straight("ffn3", dve_evac, DE["SO"])
            gate("CU1")
            straight("final2", dve_evac, DE["CD1"])

        @block.tensor
        def _(pe):
            freed = [None] * 4

            def take_bank(stage, n, done):
                b = (TURN[stage] + n) % 4
                if freed[b] is not None:
                    pe.wait_ge(*freed[b])
                freed[b] = done
                return gemm[b]

            def split_ready(c, j, it=STRAIGHT):
                pe.wait_ge(w_lo_ready, halves_before(c, j, it) + 1)

            def feature_block(ps, c, j, act, k0=0, col=0, start=True, stop=True, tiles=None):
                wh, wl = split_half(w_hi, c, j), split_half(w_lo, c, j)
                nk, cols = kind_of(c)[1], slice(col, col + P)
                last = None
                for k in range(nk):
                    if tiles is not None:
                        pe.wait_ge(act_ready, tiles[k] if isinstance(tiles, list) else tiles + k + 1)
                    nc.tensor.matmul(ps, wh[:, k, cols], act[:, k0 + k, 0, :], start=start and k == 0, stop=False)
                    nc.tensor.matmul(ps, wh[:, k, cols], act[:, k0 + k, 1, :], start=False, stop=False)
                    last = nc.tensor.matmul(ps, wl[:, k, cols], act[:, k0 + k, 0, :], start=False,
                                            stop=stop and k == nk - 1)
                return last

            def token_block(ps, wh, wl, t, act):
                tok = slice(t * P, (t + 1) * P)
                nk = act.shape[1]
                for k in range(nk):
                    nc.tensor.matmul(ps, act[:, k, 0, tok], wh(k), start=k == 0, stop=False)
                    nc.tensor.matmul(ps, act[:, k, 1, tok], wh(k), start=False, stop=False)
                    last = nc.tensor.matmul(ps, act[:, k, 0, tok], wl(k), start=False, stop=k == nk - 1)
                return last

            def stat(name):
                n, tiles, _, tok, _ = NORMS[name]
                if name == "mix2":
                    pe.wait_ge(x1_sum, 1 + KD)
                    pe.wait_ge(probsT_ready, FOX_H + MLA_H)
                    to, sums = trans, ssq_x1
                else:
                    pe.wait_ge(pool_sum, sums_before(name) + 1 + tiles)
                    if n:
                        pe.wait_ge(var_ready, n)
                    to, sums = misc, ssq
                last = nc.tensor.matmul(to[:, 0:T], ones, sums[:], start=True, stop=True)
                if tok:
                    for t in range(TT):
                        last = nc.tensor.matmul(to[:, T + t:T + t + 1], sums[:, t * P:(t + 1) * P], ones[:, 0:1],
                                                start=True, stop=True)
                last.then_inc(stat_done, 1)

            def plain(stage, act, tiles, evac, base, after_first=None, nch=4):
                for n in range(2 * nch):
                    c, j = C0[stage] + n // 2, n % 2
                    split_ready(c, j)
                    ps = take_bank(stage, n, (evac, base + n + 1))
                    feature_block(ps[:, 0:T], c, j, act, tiles=tiles if n == 0 else None).then_inc(half_done, 1)
                    if n == 0 and after_first:
                        stat(after_first)

            def token_half(stage, n, act, evac, base):
                c, t = C0[stage] + n // 2, n % 2
                split_ready(c, 1)

                def both_halves(w):
                    v = w[:, c % W_SLOTS, :].rearrange("p (j k n) -> p j k n", j=2, k=KD)
                    return lambda k: v[:, :, k, :]

                ps = take_bank(stage, n, (evac, base + n + 1))[:, 0:CW].rearrange("p (j n) -> p j n", j=2)
                last = token_block(ps, both_halves(w_hi), both_halves(w_lo), t, act)
                if t == 1:
                    last.then_inc(half_done, 2)

            def up(stage, tiles, norm):
                b0 = TURN[stage]
                before = list(freed)
                with pe.Fori(0, 4) as i:
                    it = (i, 4, 8)
                    for n in range(8):
                        c, j = C0[stage] + n // 2, n % 2
                        split_ready(c, j, it)
                        b = (b0 + n) % 4
                        if n < 4:
                            pe.wait_ge(*before[b])
                        pe.wait_ge(act_evac, AE[stage] + n - 3 + 8 * i)
                        feature_block(gemm[b][:, 0:T], c, j, act_a, tiles=tiles if n == 0 else None).then_inc(half_done, 1)
                for b in range(4):
                    freed[(b0 + b) % 4] = (act_evac, AE[stage] + 28 + b + 1)
                stat(norm)

            def down(stage, tiles):
                b0 = TURN[stage]
                before = list(freed)
                with pe.Fori(0, 4) as i:
                    it = (i, 4, 2)
                    for cc in range(4):
                        c = C0[stage] + cc
                        for j in range(2):
                            b = (b0 + j) % 4
                            split_ready(c, j, it)
                            if cc == 0:
                                pe.wait_ge(*before[b])
                                pe.wait_ge(dve_evac, DE[stage] + j - 1 + 2 * i)
                            feature_block(gemm[b][:, 0:T], c, j, hid, k0=8 * cc,
                                          start=cc == 0, stop=cc == 3,
                                          tiles=tiles + 8 * cc if j == 0 else None).then_inc(half_done, 1)
                for j in range(2):
                    freed[(b0 + j) % 4] = (dve_evac, DE[stage] + 6 + j + 1)

            def conv_up(stage, tiles, norm):
                b0 = TURN[stage]
                before = list(freed)

                def body(n, it, i):
                    c, j = C0[stage] + n // 2, n % 2
                    b = (b0 + n) % 4
                    split_ready(c, j, it)
                    if n < 4:
                        pe.wait_ge(*before[b])
                    else:
                        pe.wait_ge(dve_evac, DE[stage] + n - 3 + 8 * i)
                    feature_block(gemm[b][:, 0:T], c, j, act_a, tiles=tiles if n == 0 else None).then_inc(half_done, 1)

                for n in range(4):
                    body(n, STRAIGHT, 0)
                    if n == 0:
                        stat(norm)
                with pe.Fori(0, 5) as i:
                    for n in range(4, 12):
                        body(n, (i, 4, 8), i)
                for n in range(40, 44):
                    freed[(b0 + n) % 4] = (dve_evac, DE[stage] + n + 1)

            def conv_down(stage, tiles):
                b0 = TURN[stage]
                before = list(freed)

                def body(cc, it, i):
                    c = C0[stage] + cc
                    k0 = sum(CD_K[:cc % 4])
                    for j in range(2):
                        b = (b0 + j) % 4
                        split_ready(c, j, it)
                        if cc % 4 == 0:
                            pe.wait_ge(*before[b])
                            pe.wait_ge(dve_evac, DE[stage] + j - 1 + 2 * i)
                        feature_block(gemm[b][:, 0:T], c, j, hid, k0=k0,
                                      start=cc % 4 == 0, stop=cc % 4 == 3,
                                      tiles=tiles + k0 if j == 0 else None).then_inc(half_done, 1)

                with pe.Fori(0, 3) as i:
                    for cc in range(4):
                        body(cc, (i, 4, 2), i)
                for cc in range(12, 16):
                    body(cc, STRAIGHT, 3)
                for j in range(2):
                    freed[(b0 + j) % 4] = (dve_evac, DE[stage] + 6 + j + 1)

            def transposes(n, prob, base, slots):
                g = base + n
                pe.wait_ge(probs_normed, 2 * g + 2)
                if g:
                    pe.wait_ge(probsT_ready, g)
                nc.tensor.transpose(trans[:, 0:128], prob[:, n % slots, 0:128], ident)
                nc.tensor.transpose(trans[:, 128:256], prob[:, n % slots, 128:256], ident)
                nc.tensor.transpose(trans[:, 256:384], prob[:, n % slots, 256:384], ident).then_inc(transposed, 1)

            pe.wait_ge(con_landed, 16)
            c = C0["FG"]
            split_ready(c, 1)
            wh, wl = split_half(w_hi, c, 1), split_half(w_lo, c, 1)
            gates = slice(64 - FOX_H, 64)
            pe.wait_ge(act_ready, AT["x"] + KD)
            for t in range(TT):
                ps = take_bank("FG", t, (dve_evac, DE["FG"] + t + 1))
                last = token_block(ps[:, 0:FOX_H], lambda k: wh[:, k, gates], lambda k: wl[:, k, gates], t, act_a)
            last.then_inc(half_done, 2)

            def fox_cum():
                pe.wait_ge(gate_step, 4)
                for t in range(TT):
                    last = nc.tensor.matmul(trans[0:FOX_H, 0:T], f_ls[:, t, :], tri[:, t, :], start=t == 0, stop=t == TT - 1)
                last.then_inc(cum_done, 1)

            def fox_scores(h):
                tile, r = h // 2, slice(64 * (h % 2), 64 * (h % 2) + 64)
                pe.wait_ge(dve_evac, DE["FQK"] + 4 * (tile // 2) + 3 + tile % 2)
                if h == 0:
                    pe.wait_ge(cum_ready, 4)
                    pe.wait_ge(sel_ready, 1)
                if h >= 2:
                    pe.wait_ge(logits_ready, 2 * (h - 2) + 2)
                s = score[h % 2]
                for q, out, keys in ((0, s[:, 0:128], 128), (1, s[:, 128:384], 256)):
                    nc.tensor.matmul(out, f_q[r, tile, q * P:(q + 1) * P], f_k[r, tile, 0:keys], start=True, stop=False)
                    last = nc.tensor.matmul(out, f_sel[r, h, :], f_cum[r, 0:keys], start=False, stop=True)
                last.then_inc(scores_done, 1)

            def fox_pv(h):
                r = slice(64 * (h % 2), 64 * (h % 2) + 64)
                cols = slice(64 * h, 64 * h + 64)
                pe.wait_ge(probsT_ready, h + 1)
                if h % 4 == 0:
                    pe.wait_ge(act_evac, AE["FV"] + 2 * (h // 4) + 2)
                if h % 2 == 0 and h:
                    pe.wait_ge(act_ready, AT["fctx"] + h // 2)
                nc.tensor.matmul(misc[r, 0:T], f_v[:, 0, cols], f_probT[:, h % FOX_T, 0:256], start=True, stop=False)
                nc.tensor.matmul(misc[r, P:T], f_v[:, 1, cols], f_probT[:, h % FOX_T, 256:384], start=False,
                                 stop=True).then_inc(pv_done, 1)

            for s in range(26):
                if s < 16:
                    c, j = C0["FQK"] + s // 2, s % 2
                    split_ready(c, j)
                    ps = take_bank("FQK", s, (dve_evac, DE["FQK"] + s + 1))
                    feature_block(ps[:, 0:T], c, j, act_a).then_inc(half_done, 1)
                elif s < 24:
                    token_half("FV", s - 16, act_a, act_evac, AE["FV"])
                if s == 0:
                    stat("mix0")
                if s == 2:
                    fox_cum()
                if 4 <= s < 20:
                    fox_scores(s - 4)
                if 6 <= s < 22:
                    transposes(s - 6, f_prob, 0, 3)
                if s >= 18:
                    fox_pv(2 * (s - 18))
                    fox_pv(2 * (s - 18) + 1)
            plain("FO", act_b, AT["fctx"], dve_evac, DE["FO"])

            up("U0", AT["FO"], "ffn0")
            down("D0", AT["U0"])

            c = C0["KVQ"]
            for n, act in enumerate([act_b, act_b, act_a, act_a, act_b, act_a]):
                split_ready(c + n // 2, n % 2)
                ps = take_bank("KVQ", n, (dve_evac, DE["KVQ"] + n + 1))
                tiles = [AT["D0"] + 4 * (k // 2) + k % 2 + 1 + n for k in range(KD)] if n in (0, 2) else None
                feature_block(ps[:, 0:T], c + n // 2, n % 2, act, tiles=tiles).then_inc(half_done, 1)
                if n == 0:
                    stat("mix1")
                if n == 4:
                    stat("kv_a")
            pe.wait_ge(act_ready, AT["lat"] + 2)
            for j in range(2):
                split_ready(C0["KB"], j)
                for n in range(4 * j, 4 * j + 4):
                    ps = take_bank("KB", n, (dve_evac, DE["KB"] + n + 1))
                    last = feature_block(ps[:, 0:T], C0["KB"], j, m_act, col=(n % 4) * P)
                last.then_inc(half_done, 1)
            pe.wait_ge(act_ready, AT["lat"] + 5)

            def q_half(stage, j):
                c = C0[stage]
                split_ready(c, j)
                for n in range(2):
                    ps = take_bank(stage, 2 * j + n, (dve_evac, DE[stage] + 2 * j + n + 1))[:, 0:T]
                    last = feature_block(ps, c, j, m_act, k0=2, col=n * P)
                last.then_inc(half_done, 1)

            def v_half(j):
                split_ready(C0["VB"], j)
                wh, wl = split_half(w_hi, C0["VB"], j), split_half(w_lo, C0["VB"], j)
                for t in range(TT):
                    ps = take_bank("VB", 2 * j + t, (act_evac, AE["VB"] + 2 * j + t + 1))
                    last = token_block(ps[:], lambda k: wh[:, k, :], lambda k: wl[:, k, :], t, m_act[:, 0:2])
                last.then_inc(half_done, 1)

            def rotate(n):
                src = m_kr_raw[:] if n == 0 else m_qr_raw[:, n - 1, :]
                pe.wait_ge(dve_evac, DE["KVQ"] + 5 if n == 0 else DE["QR"] + n)
                if n == 0:
                    pe.wait_ge(probsT_ready, FOX_H)
                    pe.wait_ge(logits_ready, 2 * FOX_H)
                if n >= 3:
                    pe.wait_ge(rope_step, 2 * (n - 3) + 1)
                nc.tensor.matmul(rot_place[n], rot, src, start=True, stop=True).then_inc(rot_done, 1)

            def mla_scores(h):
                r = slice(64 * (h % 2), 64 * (h % 2) + 64)
                g = FOX_H + h
                pe.wait_ge(dve_evac, DE["QA"] + h + 1 if h < 4 else DE["QN"] + h - 4 + 1)
                pe.wait_ge(rope_step, 10)
                pe.wait_ge(logits_ready, 2 * (g - 2) + 2)
                s = score[h % 2]
                for q, out, keys in ((0, s[:, 0:128], 128), (1, s[:, 128:384], 256)):
                    qs = slice(q * P, (q + 1) * P)
                    nc.tensor.matmul(out, m_q[:, h, qs], m_k[:, h, 0:keys], start=True, stop=False)
                    last = nc.tensor.matmul(out, m_qr[r, h // 2, qs], m_kr[r, 0:keys], start=False, stop=True)
                last.then_inc(scores_done, 1)

            def mla_pv(h):
                cols = slice(VDIM * h, VDIM * h + VDIM)
                pe.wait_ge(probsT_ready, FOX_H + h + 1)
                if h == 0:
                    pe.wait_ge(act_evac, AE["VB"] + 4)
                    pe.wait_ge(var_ready, NORMS["q_a"][0] + 1)
                else:
                    pe.wait_ge(act_ready, AT["mctx"] + h)
                nc.tensor.matmul(misc[:, 0:T], m_v[:, 0, cols], m_probT[:, h % 2, 0:256], start=True, stop=False)
                nc.tensor.matmul(misc[:, P:T], m_v[:, 1, cols], m_probT[:, h % 2, 256:384], start=False,
                                 stop=True).then_inc(pv_done, 1)

            stat("q_a")
            q_half("QR", 0)
            rotate(0)
            q_half("QR", 1)
            rotate(1)
            rotate(2)
            for s in range(MLA_H + 4):
                if s < 6:
                    (q_half, q_half, v_half, v_half, q_half, q_half)[s](
                        *(("QA", 0), ("QA", 1), (0,), (1,), ("QN", 0), ("QN", 1))[s])
                if s == 0:
                    rotate(3)
                    rotate(4)
                if 1 <= s <= MLA_H:
                    mla_scores(s - 1)
                if 3 <= s < MLA_H + 3:
                    transposes(s - 3, m_prob, FOX_H, 3)
                if s >= 4:
                    mla_pv(s - 4)
            plain("MO", act_b, AT["mctx"], dve_evac, DE["MO"])
            up("U1", AT["MO"], "ffn1")
            down("D1", AT["U1"])

            split_ready(C0["GA"], 1)
            ps = take_bank("GA", 0, (dve_evac, DE["GA"] + 1))
            feature_block(ps[:, 0:T], C0["GA"], 0, act_a, tiles=AT["x1"]).then_inc(half_done, 2)
            pe_step = [0]

            def step(last):
                pe_step[0] += 1
                last.then_inc(gla_pe, 1)

            def gla_gates():
                pe.wait_ge(dve_evac, DE["GA"] + 1)
                pe.wait_ge(gla_small_landed, 32)
                for t in range(TT):
                    step(nc.tensor.matmul(score[t][:, 0:512], g_aT[:, t * P:(t + 1) * P], g_up[:], start=True, stop=True))

            def gla_cum():
                pe.wait_ge(gla_dve, 4)
                for g in range(2):
                    for h in range(2 * g, 2 * g + 2):
                        for t in range(TT):
                            last = nc.tensor.matmul(score[g][:, (h % 2) * T + t * P:(h % 2) * T + (t + 1) * P],
                                                    g_z[:, t, h * P:(h + 1) * P], tri_chunk, start=True, stop=True)
                    step(last)

            for n in range(8):
                c, j = C0["GQK"] + n // 2, n % 2
                split_ready(c, j)
                ps = take_bank("GQK", n, (dve_evac, DE["GQK"] + n + 1))
                feature_block(ps[:, 0:T], c, j, act_a).then_inc(half_done, 1)
                if n == 0:
                    stat("final1")
                    stat("mix2")
                if n == 2:
                    gla_gates()
                if n == 6:
                    gla_cum()

            def gla_scores(t):
                pe.wait_ge(gla_dve, 8)
                for h in range(GLA_H):
                    tok = slice(t * P, (t + 1) * P)
                    last = nc.tensor.matmul(score[t][:, h * P:(h + 1) * P], g_ki[:, h, tok], g_qi[:, h, tok], start=True,
                                            stop=True)
                step(last)

            def gla_transpose(t):
                pe.wait_ge(gla_dve, 9)
                if t:
                    pe.wait_ge(gla_act, 8)
                for h in range(GLA_H):
                    last = nc.tensor.transpose(trans[:, h * P:(h + 1) * P], g_kd[:, h, t * P:(t + 1) * P], ident)
                step(last)

            def gla_state(n):
                t, r = n // 2, slice(GLA_C * (n % 2), GLA_C * (n % 2) + GLA_C)
                pe.wait_ge(gla_act, 8 + t)
                pe.wait_ge(act_evac, AE["GV"] + 8)
                pe.wait_ge(gla_dve, 11 + 4 * n)
                for h in range(GLA_H):
                    last = nc.tensor.matmul(score[h // 2][:, (h % 2) * T:(h % 2) * T + T], g_kdT[r, t, h * P:(h + 1) * P],
                                            g_v[r, t, h * GLA_DV:(h + 1) * GLA_DV], start=True, stop=True)
                step(last)

            def gla_out(n):
                h = n // 2
                e = slice(n * P, (n + 1) * P)
                s = slice((n % 2) * P, (n % 2) * P + P)
                bank_ = gla_bank[n % 4]
                if n == 0:
                    pe.wait_ge(gla_act, 9)
                    pe.wait_ge(gla_dve, 23)
                if n >= 4:
                    pe.wait_ge(gla_act, 9 + 2 * (n - 4) + 2)
                for t in range(TT):
                    nc.tensor.matmul(bank_[:, t * P:(t + 1) * P], g_v[:, t, e], g_sT[:, t, h * P:(h + 1) * P],
                                     start=t == 0, stop=False)
                for m in range(1, T // GLA_C):
                    tok = slice(m * GLA_C, (m + 1) * GLA_C)
                    last = nc.tensor.matmul(bank_[:, tok], g_s[:, m - 1, h, s], g_qi[:, h, tok], start=False,
                                            stop=m == T // GLA_C - 1)
                step(last)

            def gla_stat():
                pe.wait_ge(gla_act, 25)
                for h in range(GLA_H):
                    for t in range(TT):
                        for e in range(2):
                            last = nc.tensor.matmul(misc[:, 2 * h + t:2 * h + t + 1], tmp_of(2 * h + e)[:, t * P:(t + 1) * P],
                                                    ones[:, 0:1], start=e == 0, stop=e == 1)
                step(last)

            def gla_spread(g):
                pe.wait_ge(gla_dve, 25)
                for h in range(2 * g, 2 * g + 2):
                    for t in range(TT):
                        c = 2 * h + t
                        at = (h % 2) * T + t * P
                        last = nc.tensor.matmul(score[g][:, at:at + P], g_rec[:, c:c + 1].broadcast_to([P, P]), ident,
                                                start=True, stop=True)
                step(last)

            for n in range(8):
                token_half("GV", n, act_a, act_evac, AE["GV"])
                if n == 5:
                    gla_scores(0)
                    gla_scores(1)
                    gla_transpose(0)
            gla_transpose(1)
            for n in range(8):
                c, j = C0["GG"] + n // 2, n % 2
                split_ready(c, j)
                ps = take_bank("GG", n, (dve_evac, DE["GG"] + n + 1))
                feature_block(ps[:, 0:T], c, j, act_a).then_inc(half_done, 1)
                if n < 3:
                    gla_state(n)
                if n in (3, 4):
                    for m in range(4):
                        gla_out(4 * (n - 3) + m)
                if n == 5:
                    gla_stat()
                if n == 6:
                    gla_spread(0)
                    gla_spread(1)
            plain("GO", act_b, AT["gla"], dve_evac, DE["GO"])

            conv_up("CU0", AT["GO"], "ffn2")
            conv_down("CD0", AT["CU0"])
            for n in range(24):
                c, j = C0["SI"] + n // 2, n % 2
                split_ready(c, j)
                g, part = n // 6, (n % 6) // 2
                done = (act_evac, AE["SI"] + 2 * g + j + 1) if part == 0 else (dve_evac, DE["SI"] + 4 * g + 2 * (part - 1) + j + 1)
                ps = take_bank("SI", n, done)
                feature_block(ps[:, 0:T], c, j, act_a, tiles=AT["CD0"] if n == 0 else None).then_inc(half_done, 1)
                if n == 0:
                    stat("mix3")
            plain("SO", act_b, AT["sc"], dve_evac, DE["SO"])
            conv_up("CU1", AT["SO"], "ffn3")
            conv_down("CD1", AT["CU1"])
            stat("final2")

        @block.scalar
        def _(act):
            act.dma_start(vec[:, 0:N_VEC], io["vec"]).then_inc(vec_landed, 16)
            act.dma_start(con[:], io["con"]).then_inc(con_landed, 16)
            act.dma_start(f_bias[:], io["fox_b_f"][0:1, :].partition_broadcast(P)).then_inc(fox_small_landed, 16)
            act.dma_start(g_bias[:], io["gla_b_gate_2"][0:1, :].partition_broadcast(P)).then_inc(gla_small_landed, 16)
            act.dma_start(g_up[:], io["gla_w_gate_up_2"][0]).then_inc(gla_small_landed, 16)

            def prep(c, j, it=STRAIGHT, first=False):
                nxt = (c, j) if first else ahead(c, j)
                if nxt is None:
                    return
                nc_, nj = nxt
                h = halves_before(nc_, nj, it)
                if nj == 0:
                    act.wait_ge(raw_landed[nc_ % RAW_SLOTS], raw_count(nc_, it))
                if 2 * nc_ + nj >= 2 * W_SLOTS:
                    act.wait_ge(half_done, h - 2 * W_SLOTS + 1)
                nc.scalar.copy(split_half(w_hi, nc_, nj), raw_half(nc_, nj)).then_inc(w_hi_ready, 1)

            def dmas(c):
                if c == C0["KVQ"] + 2:
                    return 3
                return kind_of(c)[1] if kind_of(c)[0] in ("lat", "kvb") else 1

            def raw_count(c, it):
                return 16 * sum(dmas(k) for k in range(c % RAW_SLOTS, c + 1, RAW_SLOTS)) + 16 * (it[1] // RAW_SLOTS) * it[0]

            def round_tile(dst, src, scale=None):
                if scale is None:
                    nc.scalar.copy(dst, src).then_inc(act_hi_ready, 1)
                else:
                    nc.scalar.activation(dst, src, ACT.Copy, scale=scale).then_inc(act_hi_ready, 1)

            def root(name):
                act.wait_ge(var_ready, NORMS[name][0] + 1)
                cols = T + TT if NORMS[name][3] else T
                nc.scalar.activation(std[:, 0:cols], (var_x1 if name == "mix2" else var)[:, 0:cols], ACT.Sqrt).then_inc(std_ready, 1)

            def plain_preps(stage, nch=4):
                for n in range(2 * nch):
                    prep(C0[stage] + n // 2, n % 2)
                    yield n

            def residual(stage, name, sig=None):
                for n in plain_preps(stage):
                    if name is not None:
                        act.wait_ge(dve_evac, DE[stage] + n + 1)
                        round_tile(act_a[:, n, 0, :], x[:, n, :], gain(name, n))

            def up(stage):
                nc.scalar.preload_act_table(ACT.Sqrt)
                with act.Fori(0, 4) as i:
                    def rounded(n):
                        act.wait_ge(sq_ready, SQ[stage] + n + 1 + 8 * i)
                        round_tile(hid[:, ds(8 * i + n, 1), 0, :], tmp2[:, n % 4, :])

                    for n in range(8):
                        c, j = C0[stage] + n // 2, n % 2
                        prep(c, j, (i, 4, 8))
                        if n:
                            rounded(n - 1)
                        act.wait_ge(half_done, halves_before(c, j, (i, 4, 8)) + 1)
                        nc.scalar.activation(tmp[:, n % 4, :], bank_of(stage, n)[:, 0:T], ACT.Relu).then_inc(act_evac, 1)
                    rounded(7)

            def down(stage, names):
                nc.scalar.preload_act_table(ACT.Sqrt)
                with act.Fori(0, 4) as i:
                    for cc in range(4):
                        for j in range(2):
                            prep(C0[stage] + cc, j, (i, 4, 2))
                    for name, dst in names:
                        for j in range(2):
                            act.wait_ge(resid_ready, RT[stage] + j + 1 + 2 * i)
                            g = vec[:, ds(2 * i + VEC[name] + j, 1)]
                            round_tile(dst[:, ds(2 * i + j, 1), 0, :], x[:, ds(2 * i + j, 1), :], g)

            def conv_up(stage, conv, norm):
                def step(n, it, i):
                    c, j = C0[stage] + n // 2, n % 2
                    prep(c, j, it)
                    if n == 0:
                        root(norm)
                        nc.scalar.preload_act_table(ACT.Silu)
                    if n >= 3:
                        rounded(n - 3, i)
                    if n >= 2:
                        silu(n - 2, i)
                    tile = 2 * (n // 4) + n % 2 + (NT2 if n % 4 >= 2 else 0)
                    col = VEC[conv] + 3 * tile + 2
                    w = vec[:, ds(col + 12 * i, 1)] if it[1] else vec[:, col:col + 1]
                    act.wait_ge(dve_evac, DE[stage] + n + 1 + 8 * i)
                    if n % 4 >= 2 and n >= 4:
                        act.wait_ge(act_ready, AT[stage] + 2 * (n // 4) + n % 2 - 1 + 4 * i)
                    nc.scalar.activation(tmp[:, n % 4, :], tmp2[:, 2 + n % 2, :], ACT.Copy, scale=w).then_inc(tap_ready, 1)

                def silu(n, i):
                    if n % 4 < 2:
                        act.wait_ge(conv_done, CONV[stage] + n + 1 + 8 * i)
                        nc.scalar.activation(tmp2[:, n % 2, :], tmp[:, n % 4, :], ACT.Silu).then_inc(silu_ready, 1)

                def rounded(n, i):
                    if n % 4 >= 2:
                        t = 2 * (n // 4) + n % 2
                        act.wait_ge(gated_ready, GT[stage] + t + 1 + 4 * i)
                        dst = hid[:, t, 0, :] if isinstance(i, int) else hid[:, ds(4 * i + t, 1), 0, :]
                        round_tile(dst, tmp[:, n % 4, :])

                for n in range(4):
                    step(n, STRAIGHT, 0)
                with act.Fori(0, 5) as i:
                    for n in range(4, 12):
                        step(n, (i, 4, 8), i)
                rounded(42, 0)
                rounded(43, 0)

            def conv_down(stage, name):
                nc.scalar.preload_act_table(ACT.Sqrt)

                def body(cc, it, i):
                    for j in range(2):
                        prep(C0[stage] + cc, j, it)
                    if cc % 4 == 3 and name is not None:
                        for j in range(2):
                            act.wait_ge(dve_evac, DE[stage] + j + 1 + 2 * i)
                            if it[1]:
                                round_tile(act_a[:, ds(2 * i + j, 1), 0, :], x[:, ds(2 * i + j, 1), :],
                                           vec[:, ds(2 * i + VEC[name] + j, 1)])
                            else:
                                round_tile(act_a[:, 6 + j, 0, :], x[:, 6 + j, :], gain(name, 6 + j))

                with act.Fori(0, 3) as i:
                    for cc in range(4):
                        body(cc, (i, 4, 2), i)
                for cc in range(12, 16):
                    body(cc, STRAIGHT, 3)

            def exps(n, base, logit, prob, nmax, total, scale, slots):
                g = base + n
                act.wait_ge(negmax_ready, g + 1)
                if n >= slots:
                    act.wait_ge(transposed, g - slots + 1)
                for q, cols in ((0, slice(0, 128)), (1, slice(128, 384))):
                    nc.scalar.activation(prob[:, n % slots, cols], logit[:, n % 2, cols], ACT.Exp, bias=nmax[:, n % 2, q:q + 1],
                                         scale=scale, accum_out=total[:, n % slots, q:q + 1]).then_inc(probs_ready, 1)

            def copy_transposed(n, base, probT, slots):
                g = base + n
                act.wait_ge(transposed, g + 1)
                if n >= slots:
                    act.wait_ge(pv_done, g - slots + 1)
                nc.scalar.copy(probT[:, n % slots, :], trans[:, 0:384]).then_inc(probsT_ready, 1)

            nc.scalar.preload_act_table(ACT.Exp)
            for h in range(2):
                prep(h // 2, h % 2, first=True)
            act.wait_ge(vec_landed, 16)
            for k in range(KD):
                act.wait_ge(x_landed[k // 4], 16)
                round_tile(act_a[:, k, 0, :], x[:, k, :], gain("mix0", k))
            prep(1, 0, first=True)

            for j in range(2):
                prep(C0["FG"], j)
            root("mix0")
            act.wait_ge(gate_step, 1)
            nc.scalar.activation(f_exp[:], f_neg_abs[:], ACT.Exp).then_inc(gate_step, 1)
            act.wait_ge(gate_step, 2)
            nc.scalar.activation(f_ln[:], f_exp[:], ACT.Ln, bias=1.0).then_inc(gate_step, 1)
            for s in range(27):
                if s < 16:
                    prep(C0["FQK"] + s // 2, s % 2)
                if 18 <= s and s % 2 == 0 and s < 26:
                    g = (s - 18) // 2
                    act.wait_ge(half_done, 2 * (C0["FV"] + g) + 2)
                    for t in range(TT):
                        nc.scalar.activation(f_v[:, t, g * CW:(g + 1) * CW], bank_of("FV", 2 * g + t)[:, 0:CW], ACT.Copy,
                                             scale=rstd_of("mix0")[:, T + t:T + t + 1]).then_inc(act_evac, 1)
                if s >= 19:
                    act.wait_ge(pv_done, 2 * (s - 19) + 2)
                    round_tile(act_b[:, s - 19, 0, :], misc[:, 0:T])
                if 6 <= s < 22:
                    copy_transposed(s - 6, 0, f_probT, FOX_T)
                if 4 <= s < 20:
                    exps(s - 4, 0, f_logit, f_prob, neg_max, row_sum, FOX_SCALE, 3)
                if 16 <= s < 24:
                    prep(C0["FQK"] + s // 2, s % 2)
            residual("FO", "ffn0")
            up("U0")
            down("D0", [("kv", act_b), ("mix1", act_a)])

            for n in range(6):
                prep(C0["KVQ"] + n // 2, n % 2)
                if n == 0:
                    root("mix1")
                if n == 5:
                    root("kv_a")
                if n != 4:
                    m = n if n < 4 else n - 1
                    act.wait_ge(dve_evac, DE["KVQ"] + n + 1)
                    g = gain("kv_a", m) if m < 2 else gain("q_a", m - 2)
                    round_tile(m_act[:, m, 0, :], m_lat[:, m, :], g)
            for j in range(2):
                prep(C0["KB"], j)
            root("q_a")
            for j in range(2):
                prep(C0["QR"], j)
            for s in range(MLA_H + 5):
                if s < 6:
                    prep(C0["QA"] + s // 2, s % 2)
                if s >= 5:
                    h = s - 5
                    act.wait_ge(pv_done, FOX_H + h + 1)
                    round_tile(act_b[:, h, 0, :], misc[:, 0:T])
                if 3 <= s < MLA_H + 3:
                    copy_transposed(s - 3, FOX_H, m_probT, 2)
                if 1 <= s <= MLA_H:
                    exps(s - 1, FOX_H, m_logit, m_prob, m_nmax, m_sum, MLA_SCALE, 3)
                if s in (2, 3):
                    j = s - 2
                    act.wait_ge(half_done, 2 * C0["VB"] + j + 1)
                    act.wait_ge(rstd_ready, ROOTS.index("kv_a") + 1)
                    for t in range(TT):
                        nc.scalar.activation(m_v[:, t, 512 * j:512 * j + 512], bank_of("VB", 2 * j + t)[:], ACT.Copy,
                                             scale=rstd_of("kv_a")[:, T + t:T + t + 1]).then_inc(act_evac, 1)
            residual("MO", "ffn1")
            act.wait_ge(gains_ready, 2)
            up("U1")
            down("D1", [("x1", act_a)])

            for j in range(2):
                prep(C0["GA"], j)
            act_step = [0]

            def step(last):
                act_step[0] += 1
                last.then_inc(gla_act, 1)

            for n in range(8):
                prep(C0["GQK"] + n // 2, n % 2)
                if n == 0:
                    root("mix2")
                if n == 4:
                    act.wait_ge(gla_dve, 2)
                    step(nc.scalar.activation(g_e[:], g_e[:], ACT.Exp))
                    act.wait_ge(gla_act, 1)
                    step(nc.scalar.activation(g_e[:], g_e[:], ACT.Ln, bias=1.0))
            for g in range(2):
                act.wait_ge(gla_pe, 3 + g)
                hs = slice(2 * g, 2 * g + 2)
                v = score[g][:].rearrange("p (h t) -> p h t", h=2)
                step(nc.scalar.activation(g_eb[:, hs, :], v, ACT.Exp))
                step(nc.scalar.activation(g_ki[:, hs, :], v, ACT.Exp, scale=-1.0))
            for n in range(8):
                c = C0["GV"] + n // 2
                if n == 0:
                    act.wait_ge(rstd_ready, ROOTS.index("mix2") + 1)
                if n % 2:
                    act.wait_ge(half_done, 2 * c + 2)
                    for t in range(TT):
                        nc.scalar.activation(g_v[:, t, (n // 2) * CW:(n // 2 + 1) * CW], bank_of("GV", n - 1 + t)[:, 0:CW], ACT.Copy,
                                             scale=rstd_of("mix2")[:, T + t:T + t + 1]).then_inc(act_evac, 1)
                prep(c, n % 2)
                if n == 1:
                    act.wait_ge(gla_dve, 6)
                    step(nc.scalar.activation(g_kd[:], g_kd[:], ACT.Exp))
                if n == 2:
                    act.wait_ge(rstd_ready, ROOTS.index("final1"))
                    root("final1")
                if n == 6:
                    act.wait_ge(gla_pe, 7)
                    step(nc.scalar.copy(g_kdT[:, 0, :], trans[:]))
            for n in range(8):
                if n == 0:
                    act.wait_ge(gla_pe, 8)
                    step(nc.scalar.copy(g_kdT[:, 1, :], trans[:]))
                prep(C0["GG"] + n // 2, n % 2)
                if n in (4, 5):
                    for m in range(4 * (n - 4), 4 * (n - 4) + 4):
                        act.wait_ge(gla_pe, 12 + m)
                        if m == 0:
                            act.wait_ge(gla_dve, 9)
                        step(nc.scalar.copy(g_o[:, m, :], gla_bank[m % 4][:, 0:T]))
                        step(nc.scalar.activation(tmp_of(m), gla_bank[m % 4][:, 0:T], ACT.Square))
                if n == 6:
                    act.wait_ge(gla_dve, 24)
                    step(nc.scalar.activation(g_std[:], g_var[:], ACT.Sqrt))
                if n == 7:
                    silus = range(KD - 1)
                    for m in silus:
                        act.wait_ge(dve_evac, DE["GG"] + m + 1)
                        nc.scalar.activation(g_g[:, m, :], g_g[:, m, :], ACT.Silu).then_inc(silu_ready, 1)
            for m in range(KD):
                if m == 1:
                    act.wait_ge(dve_evac, DE["GG"] + KD)
                    nc.scalar.activation(g_g[:, KD - 1, :], g_g[:, KD - 1, :], ACT.Silu).then_inc(silu_ready, 1)
                act.wait_ge(gated_ready, GT["gla"] + m + 1)
                round_tile(act_b[:, m, 0, :], g_o[:, m, :])
            residual("GO", "ffn2")

            conv_up("CU0", "conv0", "ffn2")
            conv_down("CD0", "mix3")
            for n in range(24):
                c, j = C0["SI"] + n // 2, n % 2
                prep(c, j)
                if n == 0:
                    root("mix3")
                g, part = n // 6, (n % 6) // 2
                m = 2 * g + j
                if part == 0:
                    act.wait_ge(half_done, 2 * c + j + 1)
                    if g:
                        act.wait_ge(dve_evac, DE["SI"] + 4 * (g - 1) + j + 1)
                    nc.scalar.copy(s_c[:, j, :], bank_of("SI", n)[:, 0:T]).then_inc(act_evac, 1)
                if part == 1:
                    act.wait_ge(sc_ready, m + 1)
                    nc.scalar.activation(tmp[:, j, :], tmp2[:, j, :], ACT.Copy,
                                         scale=gain("sc_conv", 3 * m + 2)).then_inc(tap_ready, 1)
                if part == 2:
                    act.wait_ge(dve_evac, DE["SI"] + 4 * g + 2 + j + 1)
                    round_tile(act_b[:, m, 0, :], tmp[:, 2 + j, :])
            residual("SO", "ffn3")
            conv_up("CU1", "conv1", "ffn3")
            conv_down("CD1", None)
            root("final2")

        @block.vector
        def _(dve):
            def prep(c, j, it=STRAIGHT, first=False):
                nxt = (c, j) if first else ahead(c, j)
                if nxt is None:
                    return
                nc_, nj = nxt
                dve.wait_ge(w_hi_ready, halves_before(nc_, nj, it) + 1)
                nc.vector.tensor_tensor(split_half(w_lo, nc_, nj), raw_half(nc_, nj), split_half(w_hi, nc_, nj).bitcast(F32),
                                        ALU.subtract).then_inc(w_lo_ready, 1)

            def low_tile(n, dst, src, hi, scale=None, extra=None):
                dve.wait_ge(act_hi_ready, n + 1)
                if scale is None:
                    nc.vector.tensor_tensor(dst, src, hi.bitcast(F32), ALU.subtract).then_inc(act_ready, 1)
                else:
                    nc.vector.scalar_tensor_tensor(out=dst, in0=src, scalar=scale, in1=hi.bitcast(F32), op0=ALU.mult,
                                                   op1=ALU.subtract).then_inc(act_ready, 1)

            def variance(name):
                n, _, _, tok, feats = NORMS[name]
                cols = T + TT if tok else T
                dve.wait_ge(stat_done, n + 1)
                if n and name in ROOTS:
                    dve.wait_ge(std_ready, ROOTS.index("mix2" if name == "final1" else name))
                nc.vector.tensor_scalar(var[:, 0:cols], misc[:, 0:cols], 1.0 / feats, EPS, ALU.mult,
                                        ALU.add).then_inc(var_ready, 1)

            def inverse_rms(name):
                n = ROOTS.index(name)
                cols = T + TT if NORMS[name][3] else T
                dve.wait_ge(std_ready, n + 1)
                nc.vector.reciprocal(rstd_of(name)[:, 0:cols], std[:, 0:cols]).then_inc(rstd_ready, 1)
                dve.wait_ge(rstd_ready, n + 1)

            def norm(name):
                variance(name)
                inverse_rms(name)

            def inverse_square(name):
                variance(name)
                dve.wait_ge(var_ready, NORMS[name][0] + 1)
                link(nc.vector.reciprocal(rstd_of(name)[:, 0:T], var[:, 0:T]))

            own_n = [0]

            def link(last):
                own_n[0] += 1
                last.then_inc(dve_own, 1)
                dve.wait_ge(dve_own, own_n[0])

            def residual(stage, name, at):
                for n in range(8):
                    c, j = C0[stage] + n // 2, n % 2
                    prep(c, j)
                    dve.wait_ge(half_done, 2 * c + j + 1)
                    nc.vector.tensor_tensor(x[:, n, :], bank_of(stage, n)[:, 0:T], x[:, n, :], ALU.add).then_inc(dve_evac, 1)
                    if name is not None:
                        low_tile(AT[at] + n, act_a[:, n, 1, :], x[:, n, :], act_a[:, n, 0, :], gain(name, n))

            def up(stage):
                with dve.Fori(0, 4) as i:
                    def low(n):
                        t = ds(8 * i + n, 1)
                        low_tile(AT[stage] + n + 8 * i, hid[:, t, 1, :], tmp2[:, n % 4, :], hid[:, t, 0, :])

                    for n in range(8):
                        prep(C0[stage] + n // 2, n % 2, (i, 4, 8))
                        if n:
                            low(n - 1)
                        dve.wait_ge(act_evac, AE[stage] + n + 1 + 8 * i)
                        nc.vector.tensor_tensor(tmp2[:, n % 4, :], tmp[:, n % 4, :], tmp[:, n % 4, :],
                                                ALU.mult).then_inc(sq_ready, 1)
                    low(7)

            def down(stage, norm_name, names, at):
                inverse_square(norm_name)
                with dve.Fori(0, 4) as i:
                    it = (i, 4, 2)
                    for cc in range(4):
                        for j in range(2):
                            c = C0[stage] + cc
                            prep(c, j, it)
                            if cc == 3:
                                dve.wait_ge(half_done, halves_before(c, j, it) + 1)
                                nc.vector.tensor_tensor(tmp[:, j, :], bank_of(stage, j)[:, 0:T], rstd_of(norm_name)[:, 0:T],
                                                        ALU.mult).then_inc(dve_evac, 1)
                                dve.wait_ge(dve_evac, DE[stage] + j + 1 + 2 * i)
                                t = ds(2 * i + j, 1)
                                nc.vector.tensor_tensor(x[:, t, :], x[:, t, :], tmp[:, j, :], ALU.add).then_inc(resid_ready, 1)
                    for m, (name, dst) in enumerate(names):
                        for j in range(2):
                            t = ds(2 * i + j, 1)
                            low_tile(AT[at] + 2 * m + j + 2 * len(names) * i, dst[:, t, 1, :], x[:, t, :],
                                     dst[:, t, 0, :], vec[:, ds(2 * i + VEC[name] + j, 1)])

            def conv_up(stage, conv, norm_name):
                def step(n, it, i):
                    c, j = C0[stage] + n // 2, n % 2
                    if n == 0:
                        prep(c, j, it)
                        norm(norm_name)
                    dve.wait_ge(half_done, halves_before(c, j, it) + 1)
                    if n >= 2:
                        dve.wait_ge(conv_done, CONV[stage] + n - 1 + 8 * i)
                    nc.vector.tensor_tensor(tmp2[:, 2 + n % 2, :], bank_of(stage, n)[:, 0:T], rstd_of(norm_name)[:, 0:T],
                                            ALU.mult).then_inc(dve_evac, 1)
                    if n:
                        taps(n - 1, i)
                        prep(c, j, it)

                def taps(n, i):
                    tile = 2 * (n // 4) + n % 2 + (NT2 if n % 4 >= 2 else 0)
                    col = VEC[conv] + 3 * tile
                    w0, w1 = (vec[:, col + k:col + k + 1] if isinstance(i, int) else vec[:, ds(col + k + 12 * i, 1)] for k in range(2))
                    y, u = tmp[:, n % 4, :], tmp2[:, 2 + n % 2, :]
                    dve.wait_ge(tap_ready, CV[stage] + n + 1 + 8 * i)
                    nc.vector.scalar_tensor_tensor(out=y[:, 1:T], in0=u[:, 0:T - 1], scalar=w1, in1=y[:, 1:T],
                                                   op0=ALU.mult, op1=ALU.add).then_inc(tap_mid, 1)
                    dve.wait_ge(tap_mid, CV[stage] + n + 1 + 8 * i)
                    nc.vector.scalar_tensor_tensor(out=y[:, 2:T], in0=u[:, 0:T - 2], scalar=w0, in1=y[:, 2:T],
                                                   op0=ALU.mult, op1=ALU.add).then_inc(conv_done, 1)

                for n in range(4):
                    step(n, STRAIGHT, 0)
                with dve.Fori(0, 5) as i:
                    for n in range(4, 12):
                        step(n, (i, 4, 8), i)
                taps(43, 0)

            def conv_down(stage, name, at):
                def body(cc, it, i):
                    c = C0[stage] + cc
                    for j in range(2):
                        prep(c, j, it)
                        if cc % 4 == 3:
                            dve.wait_ge(half_done, halves_before(c, j, it) + 1)
                            xt = x[:, ds(2 * i + j, 1), :] if it[1] else x[:, 6 + j, :]
                            ps = bank_of(stage, j)[:, 0:T]
                            nc.vector.tensor_tensor(xt, ps, xt, ALU.add).then_inc(dve_evac, 1)
                    if cc % 4 == 3 and name is not None:
                        for j in range(2):
                            if it[1]:
                                t = ds(2 * i + j, 1)
                                low_tile(AT[at] + j + 2 * i, act_a[:, t, 1, :], x[:, t, :], act_a[:, t, 0, :],
                                         vec[:, ds(2 * i + VEC[name] + j, 1)])
                            else:
                                low_tile(AT[at] + 6 + j, act_a[:, 6 + j, 1, :], x[:, 6 + j, :], act_a[:, 6 + j, 0, :],
                                         gain(name, 6 + j))

                with dve.Fori(0, 3) as i:
                    for cc in range(4):
                        body(cc, (i, 4, 2), i)
                for cc in range(12, 16):
                    body(cc, STRAIGHT, 3)

            def scaled(stage, n, half, dst, norm_name, rows=P):
                dve.wait_ge(half_done, half)
                nc.vector.tensor_tensor(dst, bank_of(stage, n)[0:rows, 0:T], rstd_of(norm_name)[0:rows, 0:T],
                                        ALU.mult).then_inc(dve_evac, 1)

            def maxima(n, base, logit, rmax, nmax, scale):
                g = base + n
                dve.wait_ge(scores_done, g + 1)
                s = score[n % 2]
                nc.vector.tensor_tensor_reduce(logit[:, n % 2, 0:128], s[:, 0:128], mask[:, 128:256], 1.0, -3.0e38, ALU.add,
                                               ALU.max, rmax[:, n % 2, 0:1]).then_inc(logits_ready, 1)
                nc.vector.tensor_tensor_reduce(logit[:, n % 2, 128:384], s[:, 128:384], mask, 1.0, -3.0e38, ALU.add,
                                               ALU.max, rmax[:, n % 2, 1:2]).then_inc(logits_ready, 1)
                dve.wait_ge(logits_ready, 2 * g + 2)
                nc.vector.tensor_scalar(nmax[:, n % 2, :], rmax[:, n % 2, :], -scale, None, ALU.mult).then_inc(negmax_ready, 1)

            def norm_probs(n, base, prob, total, inv, slots):
                g = base + n
                dve.wait_ge(probs_ready, 2 * g + 2)
                nc.vector.reciprocal(inv[:, n % slots, :], total[:, n % slots, :]).then_inc(invsum_ready, 1)
                dve.wait_ge(invsum_ready, g + 1)
                for q, cols in ((0, slice(0, 128)), (1, slice(128, 384))):
                    nc.vector.tensor_scalar(prob[:, n % slots, cols], prob[:, n % slots, cols], inv[:, n % slots, q:q + 1], None,
                                            ALU.mult).then_inc(probs_normed, 1)

            for h in range(2):
                prep(h // 2, h % 2, first=True)
            dve.wait_ge(vec_landed, 16)
            for k in range(KD):
                dve.wait_ge(x_landed[k // 4], 16)
                low_tile(AT["x"] + k, act_a[:, k, 1, :], x[:, k, :], act_a[:, k, 0, :], gain("mix0", k))
            prep(1, 0, first=True)
            first = vec[:, VEC["final1"]:VEC["final1"] + KD]
            nc.vector.tensor_tensor(vec[:, VEC["x1"]:VEC["x1"] + KD], first, vec[:, VEC["mix2"]:VEC["mix2"] + KD],
                                    ALU.mult).then_inc(gains_ready, 1)
            nc.vector.tensor_tensor(vec[:, VEC["final1_sq"]:VEC["final1_sq"] + KD], first, first, ALU.mult).then_inc(gains_ready, 1)

            for j in range(2):
                prep(C0["FG"], j)
            link(nc.vector.memset(f_cum[:].bitcast(F32), 0.0))
            norm("mix0")
            c = C0["FG"]
            dve.wait_ge(half_done, 2 * c + 2)
            dve.wait_ge(fox_small_landed, 16)
            for t in range(TT):
                nc.vector.scalar_tensor_tensor(out=f_z[:, t, :], in0=bank_of("FG", t)[:, 0:FOX_H],
                                               scalar=rstd_of("mix0")[:, T + t:T + t + 1], in1=f_bias[:], op0=ALU.mult,
                                               op1=ALU.add).then_inc(dve_evac, 1)
            dve.wait_ge(dve_evac, DE["FG"] + 2)
            nc.vector.scalar_tensor_tensor(out=f_neg_abs[:], in0=f_z[:], scalar=-1.0, in1=f_z[:], op0=ALU.mult,
                                           op1=ALU.min).then_inc(gate_step, 1)
            for s in range(27):
                if s < 16:
                    c, j = C0["FQK"] + s // 2, s % 2
                    dst = (f_q, f_k)[s // 2 % 2][:, 2 * (s // 4) + j, :]
                    scaled("FQK", s, 2 * c + j + 1, dst, "mix0")
                if s == 1:
                    dve.wait_ge(con_landed, 16)
                    nc.vector.tensor_copy(f_sel[:], pick.unsqueeze(2).broadcast_to([P, FOX_H, P])).then_inc(sel_ready, 1)
                    dve.wait_ge(gate_step, 3)
                    nc.vector.scalar_tensor_tensor(out=f_ls[:], in0=f_z[:], scalar=0.0, in1=f_ln[:], op0=ALU.min,
                                                   op1=ALU.subtract).then_inc(gate_step, 1)
                if s == 3:
                    dve.wait_ge(cum_done, 1)
                    for row in (0, 64):
                        nc.vector.tensor_copy(f_cum[row:row + 16, :], trans[0:16, 0:T]).then_inc(cum_ready, 1)
                    dve.wait_ge(cum_ready, 1)
                    for row in (32, 96):
                        nc.vector.tensor_tensor(f_cum[row:row + 16, :], trans[0:16, 0:T], f_cum[0:16, :].bitcast(F32),
                                                ALU.subtract).then_inc(cum_ready, 1)
                if 5 <= s < 21:
                    norm_probs(s - 5, 0, f_prob, row_sum, inv_sum, 3)
                if 4 <= s < 20:
                    maxima(s - 4, 0, f_logit, row_max, neg_max, FOX_SCALE)
                if s >= 19:
                    low_tile(AT["fctx"] + s - 19, act_b[:, s - 19, 1, :], misc[:, 0:T], act_b[:, s - 19, 0, :])
                if s < 24:
                    prep(C0["FQK"] + s // 2, s % 2)
            residual("FO", "ffn0", "FO")
            up("U0")
            down("D0", "ffn0", [("kv", act_b), ("mix1", act_a)], "D0")

            for n in range(6):
                c, j = C0["KVQ"] + n // 2, n % 2
                if n == 5:
                    norm("kv_a")
                prep(c, j)
                if n == 0:
                    norm("mix1")
                m = n if n < 4 else n - 1
                scaled("KVQ", n, 2 * c + j + 1, m_kr_raw[:] if n == 4 else m_lat[:, m, :], "mix1")
                if n != 4:
                    g = gain("kv_a", m) if m < 2 else gain("q_a", m - 2)
                    low_tile(AT["lat"] + m, m_act[:, m, 1, :], m_lat[:, m, :], m_act[:, m, 0, :], g)
            for j in range(2):
                prep(C0["KB"], j)
                for n in range(4 * j, 4 * j + 4):
                    scaled("KB", n, 2 * C0["KB"] + j + 1, m_k[:, n, :], "kv_a")

            def rope(n):
                dst = m_kr[:] if n == 0 else m_qr[:, n - 1, :]
                dve.wait_ge(rot_done, n + 1)
                nc.vector.tensor_tensor(dst, rot_place[n], sin_t, ALU.mult).then_inc(rope_step, 1)
                dve.wait_ge(rope_step, 2 * n + 1)
                dve.wait_ge(rope_cos, n + 1)
                nc.vector.tensor_tensor(dst, dst, m_lat[:, n, :], ALU.add).then_inc(rope_step, 1)

            for j in range(2):
                if j == 0:
                    norm("q_a")
                prep(C0["QR"], j)
                for n in range(2):
                    scaled("QR", 2 * j + n, 2 * C0["QR"] + j + 1, m_qr_raw[:, 2 * j + n, :], "q_a")
            for s in range(MLA_H + 5):
                if s == 0:
                    for n in range(3):
                        rope(n)
                if s < 2 or 4 <= s < 6:
                    stage, j = (("QA", s) if s < 2 else ("QN", s - 4))
                    for n in range(2):
                        scaled(stage, 2 * j + n, 2 * C0[stage] + j + 1, m_q[:, 2 * j + n + (0 if s < 2 else 4), :], "q_a")
                if s == 0:
                    rope(3)
                    rope(4)
                if 2 <= s < MLA_H + 2:
                    norm_probs(s - 2, FOX_H, m_prob, m_sum, m_inv, 3)
                if 1 <= s <= MLA_H:
                    maxima(s - 1, FOX_H, m_logit, m_max, m_nmax, MLA_SCALE)
                if s >= 5:
                    low_tile(AT["mctx"] + s - 5, act_b[:, s - 5, 1, :], misc[:, 0:T], act_b[:, s - 5, 0, :])
                if s < 6:
                    prep(C0["QA"] + s // 2, s % 2)
            residual("MO", "ffn1", "MO")
            dve.wait_ge(gains_ready, 2)
            up("U1")
            down("D1", "ffn1", [("x1", act_a)], "x1")

            for j in range(2):
                prep(C0["GA"], j)
            prep(C0["GQK"], 0)
            variance("final1")
            dve.wait_ge(var_ready, NORMS["final1"][0] + 1)
            link(nc.vector.tensor_scalar(var_x1[:], var[:], EPS, None, ALU.mult))
            dve.wait_ge(stat_done, NORMS["mix2"][0] + 1)
            nc.vector.scalar_tensor_tensor(out=var_x1[:], in0=trans[:, 0:T + TT], scalar=1.0 / D, in1=var_x1[:], op0=ALU.mult,
                                           op1=ALU.add).then_inc(var_ready, 1)
            inverse_rms("mix2")
            scaled("GA", 0, 2 * C0["GA"] + 2, g_aT[:], "mix2", rows=GATE_RANK)
            dve_step = [0]

            def step(last, wait=False):
                dve_step[0] += 1
                last.then_inc(gla_dve, 1)
                if wait:
                    dve.wait_ge(gla_dve, dve_step[0])

            def bcum(g):
                return score[g][:].rearrange("p (c s) -> p c s", s=GLA_C)

            for n in range(8):
                c, j = C0["GQK"] + n // 2, n % 2
                if n:
                    prep(c, j)
                scaled("GQK", n, 2 * c + j + 1, (g_q, g_k)[n // 4][:, n % 4, :], "mix2")
                if n == 3:
                    for t in range(TT):
                        dve.wait_ge(gla_pe, 1 + t)
                        dve.wait_ge(gla_small_landed, 32)
                        link(nc.vector.tensor_tensor(g_z[:, t, :], score[t][:], g_bias[:], ALU.add))
                        step(nc.vector.scalar_tensor_tensor(out=g_e[:, t, :], in0=g_z[:, t, :], scalar=-1.0, in1=g_z[:, t, :],
                                                            op0=ALU.mult, op1=ALU.min))
                if n == 5:
                    dve.wait_ge(gla_act, 2)
                    for t in range(TT):
                        step(nc.vector.scalar_tensor_tensor(out=g_z[:, t, :], in0=g_z[:, t, :], scalar=0.0, in1=g_e[:, t, :],
                                                            op0=ALU.min, op1=ALU.subtract))
            for n in range(8):
                prep(C0["GV"] + n // 2, n % 2)
                if n == 0:
                    for g in range(2):
                        dve.wait_ge(gla_act, 4 + 2 * g)
                        hs = slice(2 * g, 2 * g + 2)
                        cum = bcum(g)
                        link(nc.vector.tensor_copy(g_last[:, 8 * g:8 * g + 8], cum[:, :, GLA_C - 1:GLA_C].squeeze(2)))
                        step(nc.vector.tensor_tensor(
                            g_kd[:, hs, :].rearrange("p h (c s) -> p (h c) s", s=GLA_C),
                            g_last[:, 8 * g:8 * g + 8].unsqueeze(2).broadcast_to([P, 8, GLA_C]), cum, ALU.subtract))
                if n == 1:
                    dve.wait_ge(dve_evac, DE["GQK"] + 8)
                    step(nc.vector.tensor_tensor(g_ki[:], g_ki[:], g_k[:], ALU.mult))
                if n == 2:
                    step(nc.vector.scalar_tensor_tensor(out=g_qi[:], in0=g_q[:], scalar=GLA_SCALE, in1=g_eb[:],
                                                        op0=ALU.mult, op1=ALU.mult))
                if n == 3:
                    dve.wait_ge(gla_act, 7)
                    step(nc.vector.tensor_tensor(g_kd[:], g_kd[:], g_k[:], ALU.mult))
                if n == 4:
                    inverse_rms("final1")
                if n >= 5:
                    for k in ((0, 1, 2), (3, 4, 5), (6, 7))[n - 5]:
                        nc.vector.scalar_tensor_tensor(out=x[:, k, :], in0=x[:, k, :], scalar=gain("final1", k),
                                                       in1=rstd_of("final1")[:, 0:T], op0=ALU.mult,
                                                       op1=ALU.mult).then_inc(resid_ready, 1)
                if n == 6:
                    dve.wait_ge(gla_zeroed, 1)
                    for t in range(TT):
                        dve.wait_ge(gla_pe, 5 + t)
                        step(nc.vector.copy_predicated(
                            g_sT[:, t, :].rearrange("p (h s) -> p h s", h=GLA_H),
                            chunk_mask.unsqueeze(1).broadcast_to([P, GLA_H, P]),
                            score[t][:].rearrange("p (h s) -> p h s", h=GLA_H)))
            for n in range(8):
                c, j = C0["GG"] + n // 2, n % 2
                if n == 7:
                    for m in range(KD):
                        dve.wait_ge(gla_pe, 21 + m // 4)
                        nc.vector.scalar_tensor_tensor(out=g_o[:, m, :], in0=g_o[:, m, :], scalar=gain("head", m),
                                                       in1=score[m // 4][:, (m // 2 % 2) * T:(m // 2 % 2) * T + T], op0=ALU.mult,
                                                       op1=ALU.mult).then_inc(head_normed, 1)
                prep(c, j)
                if n in (1, 2, 3):
                    m = n - 1
                    dve.wait_ge(gla_pe, 9 + m)
                    if m:
                        dve.wait_ge(gla_dve, 11 + 4 * m)
                    for h in range(GLA_H):
                        kv = score[h // 2][:, (h % 2) * T:(h % 2) * T + T]
                        if m == 0:
                            step(nc.vector.tensor_copy(g_s[:, 0, h, :], kv))
                        else:
                            decay = g_eb[:, h, m * GLA_C + GLA_C - 1:m * GLA_C + GLA_C]
                            step(nc.vector.scalar_tensor_tensor(out=g_s[:, m, h, :], in0=g_s[:, m - 1, h, :], scalar=decay,
                                                                in1=kv, op0=ALU.mult, op1=ALU.add))
                scaled("GG", n, 2 * c + j + 1, g_g[:, n, :], "mix2")
                if n == 5:
                    dve.wait_ge(gla_pe, 20)
                    step(nc.vector.tensor_scalar(g_var[:], misc[:, 0:GLA_H * TT], 1.0 / GLA_DV, EPS, ALU.mult, ALU.add))
                    dve.wait_ge(gla_act, 26)
                    step(nc.vector.reciprocal(g_rec[:], g_std[:]))
            for m in range(KD):
                dve.wait_ge(head_normed, m + 1)
                dve.wait_ge(silu_ready, SL["GG"] + m + 1)
                nc.vector.tensor_tensor(g_o[:, m, :], g_o[:, m, :], g_g[:, m, :], ALU.mult).then_inc(gated_ready, 1)
                if m:
                    low_tile(AT["gla"] + m - 1, act_b[:, m - 1, 1, :], g_o[:, m - 1, :], act_b[:, m - 1, 0, :])
            low_tile(AT["gla"] + 7, act_b[:, 7, 1, :], g_o[:, 7, :], act_b[:, 7, 0, :])
            dve.wait_ge(resid_ready, RT["x1"] + KD)
            residual("GO", "ffn2", "GO")

            conv_up("CU0", "conv0", "ffn2")
            conv_down("CD0", "mix3", "CD0")
            for n in range(24):
                c, j = C0["SI"] + n // 2, n % 2
                prep(c, j)
                if n == 0:
                    norm("mix3")
                    link(nc.vector.tensor_tensor(rstd_sq[:], rstd_of("mix3")[:, 0:T], rstd_of("mix3")[:, 0:T], ALU.mult))
                g, part = n // 6, (n % 6) // 2
                m = 2 * g + j
                ps = bank_of("SI", n)[:, 0:T]
                if part == 1:
                    dve.wait_ge(act_evac, AE["SI"] + m + 1)
                    dve.wait_ge(half_done, 2 * c + j + 1)
                    nc.vector.tensor_tensor(tmp2[:, 2 + j, :], ps, s_c[:, j, :], ALU.mult).then_inc(dve_evac, 1)
                    dve.wait_ge(dve_evac, DE["SI"] + 4 * g + j + 1)
                    nc.vector.tensor_tensor(tmp2[:, j, :], tmp2[:, 2 + j, :], rstd_sq[:], ALU.mult).then_inc(sc_ready, 1)
                    y, v = tmp[:, j, :], tmp2[:, j, :]
                    dve.wait_ge(tap_ready, CV["SI"] + m + 1)
                    nc.vector.scalar_tensor_tensor(out=y[:, 1:T], in0=v[:, 0:T - 1], scalar=gain("sc_conv", 3 * m + 1),
                                                   in1=y[:, 1:T], op0=ALU.mult, op1=ALU.add).then_inc(tap_mid, 1)
                    dve.wait_ge(tap_mid, CV["SI"] + m + 1)
                    link(nc.vector.scalar_tensor_tensor(out=y[:, 2:T], in0=v[:, 0:T - 2], scalar=gain("sc_conv", 3 * m),
                                                        in1=y[:, 2:T], op0=ALU.mult, op1=ALU.add))
                    link(nc.vector.tensor_tensor(y, y, rstd_of("mix3")[:, 0:T], ALU.mult))
                if part == 2:
                    dve.wait_ge(half_done, 2 * c + j + 1)
                    if g:
                        dve.wait_ge(act_ready, AT["sc"] + m - 2 + 1)
                    nc.vector.tensor_tensor(tmp[:, 2 + j, :], ps, tmp[:, j, :], ALU.mult).then_inc(dve_evac, 1)
                    low_tile(AT["sc"] + m, act_b[:, m, 1, :], tmp[:, 2 + j, :], act_b[:, m, 0, :])
            residual("SO", "ffn3", "SO")
            conv_up("CU1", "conv1", "ffn3")
            conv_down("CD1", None, None)
            norm("final2")
            for k in range(KD):
                nc.vector.scalar_tensor_tensor(out=x[:, k, :], in0=x[:, k, :], scalar=gain("final2", k),
                                               in1=rstd_of("final2")[:, 0:T], op0=ALU.mult, op1=ALU.mult).then_inc(resid_ready, 1)


_WEIGHTS = ["fox_w_in", "fox_b_f", "fox_w_out", "mla_w_kv_a", "mla_w_kv_b", "mla_w_q_a", "mla_w_q_b", "mla_w_out",
            "ffn_w_up", "ffn_w_down", "gla_w_in_2", "gla_w_gate_up_2", "gla_b_gate_2", "gla_w_out_2", "sc_w_in_2",
            "sc_w_out_2", "ffn_w_up_2", "ffn_w_down_2"]


def kernel(**inputs):
    import concourse.bacc as bacc
    from concourse.bass_utils import run_bass_kernel_spmd

    a = {name: np.ascontiguousarray(v) for name, v in inputs.items()}
    tiles = lambda v: v.reshape(-1, P).T
    taps = lambda v: v.reshape(-1, P, 3).transpose(1, 0, 2).reshape(P, -1)
    vec = np.concatenate(
        [tiles(v) for v in (a["norm_mix_g"][0], a["norm_ffn_g"][0], a["kv_norm_g"], a["norm_mix_g"][1], a["norm_ffn_g"][1],
                            a["final_norm_g"], a["norm_mix_g_2"][0], a["norm_ffn_g_2"][0], a["norm_mix_g_2"][1],
                            a["norm_ffn_g_2"][1], a["final_norm_g_2"], a["mla_kv_a_norm_g"], a["mla_q_a_norm_g"][0],
                            a["gla_head_norm_g_2"][0])]
        + [taps(a["sc_conv_w_2"][0]), taps(a["ffn_conv_w_2"][0]), taps(a["ffn_conv_w_2"][1])], axis=1)
    arrays = {name: a[name] for name in _WEIGHTS}
    arrays.update(xT=np.ascontiguousarray(a["x"][0].T), vec=np.ascontiguousarray(vec), con=shape_constants())
    nc = bacc.Bacc("TRN2", target_bir_lowering=False, num_devices=1)
    io = {name: nc.dram_tensor(f"in_{name}", v.shape, mybir.dt.from_np(v.dtype), kind="ExternalInput").ap()
          for name, v in arrays.items()}
    io["out"] = nc.dram_tensor("outT", (D, T), F32, kind="ExternalOutput").ap()
    build(nc, io)
    r = run_bass_kernel_spmd(nc, [{f"in_{name}": v for name, v in arrays.items()}], core_ids=[0])
    return np.ascontiguousarray(r.results[0]["outT"].T).reshape(1, T, D)
```

```python
from contextlib import ExitStack

import numpy as np

import concourse.bass as bass
from concourse import mybir

F32 = mybir.dt.float32
F32R = mybir.dt.float32r
U32 = mybir.dt.uint32
ALU = mybir.AluOpType
ACT = mybir.ActivationFunctionType
ds = bass.ds

P = 128
T = 256
TT = T // P
D = 1024
KD = D // P
EPS = 1e-6
FOX_H, FOX_DH = 16, 64
MLA_H, NOPE, ROPE, VDIM = 8, 128, 64, 128
QLORA, KVLORA = 384, 256
DFF = 4 * D
DFF2 = 2816
NT2 = DFF2 // P
GLA_H, GLA_DK, GLA_DV, GLA_C = 4, 128, 256, 64
GATE_RANK, GATE_TAU = 16, 16.0
FOX_SCALE = FOX_DH ** -0.5
MLA_SCALE = (NOPE + ROPE) ** -0.5
GLA_SCALE = GLA_DK ** -0.5
MASKED = -1.0e30

CW = 256
CHUNK = KD * CW
RAW_SLOTS = 4
W_SLOTS = 2
AHEAD = 3
FOX_LAG = 8
FOX_T = 14
CD_K = (6, 6, 5, 5)

STAGES = [("FQA", 2), ("FG", 1), ("FQB", 6), ("FV", 4), ("FO", 4), ("U0", 16), ("D0", 16), ("KVQ", 3), ("KB", 1), ("QR", 1),
          ("QA", 1), ("VB", 1), ("QN", 1), ("MO", 4), ("U1", 16), ("D1", 16), ("GA", 1), ("GQK", 4), ("GV", 4), ("GG", 4), ("GO", 4),
          ("CU0", 22), ("CD0", 16), ("SI", 12), ("SO", 4), ("CU1", 22), ("CD1", 16)]
C0 = {}
N_CHUNKS = 0
for _name, _n in STAGES:
    C0[_name] = N_CHUNKS
    N_CHUNKS += _n

VEC = {}
N_VEC = 0
for _name, _n in [("mix0", 8), ("ffn0", 8), ("kv", 8), ("mix1", 8), ("ffn1", 8), ("final1", 8), ("mix2", 8),
                  ("ffn2", 8), ("mix3", 8), ("ffn3", 8), ("final2", 8), ("kv_a", 2), ("q_a", 3), ("head", 8),
                  ("sc_conv", 24), ("conv0", 132), ("conv1", 132)]:
    VEC[_name] = N_VEC
    N_VEC += _n

VEC["x1"] = N_VEC
VEC["final1_sq"] = N_VEC + KD

CON = {}
N_CON = 0
for _name, _n in [("ones", 128), ("ident", 128), ("mask", 256), ("tri", 512), ("tri_chunk", 128), ("cos", 256),
                  ("sin", 256), ("rot", 128), ("chunk_mask", 128), ("pick", FOX_H),
                  ("head_row", GLA_H * GLA_H)]:
    CON[_name] = N_CON
    N_CON += _n


def shape_constants():
    con = np.zeros((P, N_CON), np.float32)
    at = lambda name, n: con[:, CON[name]:CON[name] + n]
    i = np.arange(P)
    at("ones", 128)[:] = 1.0
    at("ident", 128)[:] = np.eye(P)
    at("mask", 256)[:, 128:] = np.where(i[None, :] <= i[:, None], 0.0, MASKED)
    tri = np.where(np.arange(T)[:, None] <= np.arange(T)[None, :], -1.0 / FOX_SCALE, 0.0)
    at("tri", 512)[:] = tri.reshape(TT, P, T).transpose(1, 0, 2).reshape(P, 512)
    same = (i[:, None] // GLA_C) == (i[None, :] // GLA_C)
    upto = same & (i[:, None] <= i[None, :])
    at("tri_chunk", 128)[:] = np.where(upto, 1.0 / GATE_TAU, 0.0)
    at("chunk_mask", 128)[:] = np.where(upto, 1.0, 0.0)
    inv = (1.0 / (np.float32(10000.0) ** (np.arange(0, ROPE, 2, dtype=np.float32) / np.float32(ROPE)))).astype(np.float32)
    ang = np.arange(T, dtype=np.float32)[:, None] * inv[None, :]
    at("cos", 256)[:] = np.tile(np.cos(ang).T, (4, 1))
    at("sin", 256)[:] = np.tile(np.sin(ang).T, (4, 1))
    half = ROPE // 2
    for m in range(P):
        if m % ROPE < half:
            at("rot", 128)[m + half, m] = -1.0
        else:
            at("rot", 128)[m - half, m] = 1.0
    for h in range(FOX_H):
        at("pick", FOX_H)[[64 * (h % 2) + h, 64 * (h % 2) + 32 + h], h] = 1.0
    for h in range(GLA_H):
        at("head_row", GLA_H * GLA_H)[:, h * GLA_H + h] = 1.0
    return con


def build(nc, io):
    ctx = ExitStack()
    with ctx:
        used = [16512]

        def sb(name, shape, dt=F32, at=None):
            n = int(np.prod(shape[1:])) * 4
            if at is None:
                at = used[0]
                used[0] += (n + 31) // 32 * 32
            return nc.alloc_sbuf_tensor_at(name, shape, dt, offset=at)

        def bank(name):
            return ctx.enter_context(nc.psum_tensor(name, [P, 512], F32))

        def sem(name):
            return ctx.enter_context(nc.semaphore(name))

        w_raw = sb("w_raw", [P, RAW_SLOTS, CHUNK])
        w_hi = sb("w_hi", [P, W_SLOTS, CHUNK], F32R)
        w_lo = sb("w_lo", [P, W_SLOTS, CHUNK], F32R)
        x = sb("x", [P, KD, T])
        act_a = sb("act_a", [P, KD, 2, T], F32R)
        act_b = sb("act_b", [P, KD, 2, T], F32R)
        vec = sb("vec", [P, N_VEC + 2 * KD])
        con = sb("con", [P, N_CON])
        ssq = sb("ssq", [P, T])
        sqt = sb("sqt", [P, T])
        ssq_x1 = sb("ssq_x1", [P, T])
        sqt_x1 = sb("sqt_x1", [P, T])
        var = sb("var", [P, T + TT])
        var_x1 = sb("var_x1", [P, T + TT])
        std = sb("std", [P, T + TT])
        rstd = sb("rstd", [P, 3, T + TT])
        tmp = sb("tmp", [P, 4, T])
        tmp2 = sb("tmp2", [P, 4, T])
        rstd_sq = sb("rstd_sq", [P, T])
        g_last = sb("g_last", [P, GLA_H * (T // GLA_C)])
        arena = used[0]

        def overlay():
            used[0] = arena

        overlay()
        hid = sb("hid", [P, DFF // P, 2, T], F32R)
        end_hid = used[0]
        overlay()
        f_q = sb("f_q", [P, KD, T])
        f_k = sb("f_k", [P, KD, T])
        f_v = sb("f_v", [P, TT, D])
        f_logit = sb("f_logit", [P, 2, 384])
        f_prob = sb("f_prob", [P, 3, 384])
        f_probT = sb("f_probT", [P, FOX_T, 384])
        f_sel = sb("f_sel", [P, FOX_H, P], F32R)
        f_cum = sb("f_cum", [P, T], F32R)
        f_bias = sb("f_bias", [FOX_H, 1])
        f_z = sb("f_z", [FOX_H, T])
        f_exp = sb("f_exp", [FOX_H, T])
        f_ls = sb("f_ls", [P, TT, FOX_H])
        row_max = sb("row_max", [P, 2, 2])
        neg_max = sb("neg_max", [P, 2, 2])
        row_sum = sb("row_sum", [P, 3, 2])
        inv_sum = sb("inv_sum", [P, 3, 2])
        assert used[0] <= end_hid
        overlay()
        m_q = sb("m_q", [P, MLA_H, T])
        m_k = sb("m_k", [P, MLA_H, T])
        m_v = sb("m_v", [P, TT, D])
        m_qr_raw = sb("m_qr_raw", [P, 4, T])
        m_qr = sb("m_qr", [P, 4, T])
        m_kr_raw = sb("m_kr_raw", [P, T])
        m_kr = sb("m_kr", [P, T])
        m_lat = sb("m_lat", [P, 5, T])
        m_act = sb("m_act", [P, 5, 2, T], F32R)
        m_logit = sb("m_logit", [P, 2, 384])
        m_prob = sb("m_prob", [P, 3, 384])
        m_probT = sb("m_probT", [P, 2, 384])
        m_max = sb("m_max", [P, 2, 2])
        m_nmax = sb("m_nmax", [P, 2, 2])
        m_sum = sb("m_sum", [P, 3, 2])
        m_inv = sb("m_inv", [P, 3, 2])
        assert used[0] <= end_hid
        overlay()
        g_q = sb("g_q", [P, GLA_H, T])
        g_k = sb("g_k", [P, GLA_H, T])
        g_v = sb("g_v", [P, TT, D])
        g_z = sb("g_z", [P, TT, 512])
        g_e = sb("g_e", [P, TT, 512])
        g_s = sb("g_s", [P, 3, GLA_H, GLA_DV])
        g_eb = sb("g_eb", [P, GLA_H, T])
        g_ki = sb("g_ki", [P, GLA_H, T])
        g_kd = sb("g_kd", [P, GLA_H, T])
        g_qi = sb("g_qi", [P, GLA_H, T])
        g_kdT = sb("g_kdT", [P, TT, 512])
        g_sT = sb("g_sT", [P, TT, 512])
        g_aT = sb("g_aT", [GATE_RANK, T])
        end_gla = used[0]
        g_var, g_std, g_rec = (g_ki[0:GLA_H, n, :] for n in range(3))
        g_o = nc.alloc_sbuf_tensor_at("g_o", [P, KD, T], F32, offset=arena)
        g_g = nc.alloc_sbuf_tensor_at("g_g", [P, KD, T], F32, offset=arena + 16384)
        overlay()
        used[0] = max(end_hid, end_gla)
        g_up = sb("g_up", [GATE_RANK, 512])
        g_bias = sb("g_bias", [P, 512])
        s_c = sb("s_c", [P, 2, T])
        assert used[0] <= nc.sbuf_usable_end, used[0]

        gemm = [bank(f"gemm{i}") for i in range(4)]
        score = [bank("score0"), bank("score1")]
        trans = bank("trans")
        misc = bank("misc")

        gla_bank = [trans, score[0], score[1], misc]

        def state_place(n, h):
            return ((trans, misc) if n == 1 else score)[h // 2][:, (h % 2) * T:(h % 2) * T + T]

        rot_place = [b[:, 0:T] for b in (trans, misc, score[1], trans, misc)]

        ones = con[:, CON["ones"]:CON["ones"] + 128]
        ident = con[:, CON["ident"]:CON["ident"] + 128]
        mask = con[:, CON["mask"]:CON["mask"] + 256]
        tri = con[:, CON["tri"]:CON["tri"] + 512].rearrange("p (t n) -> p t n", t=TT)
        tri_chunk = con[:, CON["tri_chunk"]:CON["tri_chunk"] + 128]
        cos_t = con[:, CON["cos"]:CON["cos"] + 256]
        sin_t = con[:, CON["sin"]:CON["sin"] + 256]
        pick = con[:, CON["pick"]:CON["pick"] + FOX_H]
        head_row = con[:, CON["head_row"]:CON["head_row"] + GLA_H * GLA_H]
        rot = con[:, CON["rot"]:CON["rot"] + 128]
        chunk_mask = con[:, CON["chunk_mask"]:CON["chunk_mask"] + 128].bitcast(U32)

        def gain(name, k):
            return vec[:, VEC[name] + k:VEC[name] + k + 1]

        x_landed = [sem("x_landed0"), sem("x_landed1")]
        vec_landed = sem("vec_landed")
        ones_landed = sem("ones_landed")
        con_landed = sem("con_landed")
        fox_small_landed = sem("fox_small_landed")
        gla_small_landed = sem("gla_small_landed")
        first_landed = sem("first_landed")
        raw_landed = [sem(f"raw_landed{s}") for s in range(RAW_SLOTS)]
        w_hi_ready = sem("w_hi_ready")
        w_lo_ready = sem("w_lo_ready")
        half_done = sem("half_done")
        act_evac = sem("act_evac")
        dve_evac = sem("dve_evac")
        resid_ready = sem("resid_ready")
        act_hi_ready = sem("act_hi_ready")
        act_ready = sem("act_ready")
        pool_sq = sem("pool_sq")
        gains_ready = sem("gains_ready")
        x1_scaled = sem("x1_scaled")
        x1_sum = sem("x1_sum")
        gla_zeroed = sem("gla_zeroed")
        pool_sum = sem("pool_sum")
        stat_done = sem("stat_done")
        var_ready = sem("var_ready")
        std_ready = sem("std_ready")
        spread_done = sem("spread_done")
        rstd_ready = sem("rstd_ready")
        sq_x = sem("sq_x")
        sq_ready = sem("sq_ready")
        tap_ready = sem("tap_ready")
        tap_mid = sem("tap_mid")
        conv_done = sem("conv_done")
        silu_ready = sem("silu_ready")
        gated_ready = sem("gated_ready")
        scores_done = sem("scores_done")
        logits_ready = sem("logits_ready")
        negmax_ready = sem("negmax_ready")
        probs_ready = sem("probs_ready")
        invsum_ready = sem("invsum_ready")
        probs_normed = sem("probs_normed")
        transposed = sem("transposed")
        probsT_ready = sem("probsT_ready")
        pv_done = sem("pv_done")
        gate_step = sem("gate_step")
        cum_done = sem("cum_done")
        key_done = sem("key_done")
        cum_ready = sem("cum_ready")
        rot_done = sem("rot_done")
        rope_step = sem("rope_step")
        rope_cos = sem("rope_cos")
        sel_ready = sem("sel_ready")
        gla_pe = sem("gla_pe")
        gla_act = sem("gla_act")
        gla_dve = sem("gla_dve")
        head_sq = sem("head_sq")
        head_gated = sem("head_gated")
        last_sq = sem("last_sq")
        out_gained = sem("out_gained")
        sc_ready = sem("sc_ready")
        dve_own = sem("dve_own")
        out_landed = sem("out_landed")

        STRAIGHT = (0, 0, 0)

        def halves_before(c, j, it=STRAIGHT):
            return 2 * c + j + 2 * it[1] * it[0]

        DE, AE = {}, {}
        n_d = n_a = 0
        for name, d, a in [("FQA", 4, 1), ("FG", 1, 0), ("FQB", 12, 0), ("FV", 0, 8), ("FO", 8, 0), ("U0", 0, 32), ("D0", 8, 0),
                           ("KVQ", 6, 0), ("KB", 8, 0), ("QR", 4, 0), ("QA", 4, 0), ("VB", 0, 4), ("QN", 4, 0), ("MO", 8, 0), ("U1", 0, 32),
                           ("D1", 8, 0), ("GA", 1, 0), ("GQK", 8, 0), ("GV", 0, 8), ("GG", 8, 0), ("GO", 8, 0),
                           ("CU0", 44, 0), ("CD0", 8, 0), ("SI", 16, 8), ("SO", 8, 0), ("CU1", 44, 0), ("CD1", 8, 0)]:
            DE[name], AE[name] = n_d, n_a
            n_d, n_a = n_d + d, n_a + a
        AT = {}
        n_t = 0
        for name, n in [("x", 8), ("fctx", 8), ("FO", 8), ("U0", 32), ("D0", 16), ("lat", 5), ("mctx", 8), ("MO", 8),
                        ("U1", 32), ("x1", 8), ("gla", 8), ("GO", 8), ("CU0", 22), ("CD0", 8), ("sc", 8), ("SO", 8),
                        ("CU1", 22)]:
            AT[name] = n_t
            n_t += n
        GT = {}
        n_t = 0
        for name, n in [("gla", 8), ("CU0", 22), ("CU1", 22)]:
            GT[name] = n_t
            n_t += n
        RT = {"D0": 0, "D1": 8, "x1": 16}
        SQ = {"U0": 0, "U1": 32}
        TURN = {}
        n_t = 0
        for name, n in [("FQA", 4), ("FG", 1), ("FQB", 12), ("FV", 8), ("FPV", 8), ("FO", 8), ("U0", 32), ("D0", 2), ("KVQ", 6), ("KB", 8),
                        ("QR", 4), ("QA", 4), ("VB", 4), ("QN", 4), ("MPV", 8), ("MO", 8), ("U1", 32), ("D1", 2), ("GA", 1), ("GQK", 8),
                        ("GV", 8),
                        ("GG", 8), ("GO", 8), ("CU0", 44), ("CD0", 2), ("SI", 24), ("SO", 8), ("CU1", 44), ("CD1", 2)]:
            TURN[name] = n_t
            n_t += n

        def bank_of(stage, n):
            return gemm[(TURN[stage] + n) % 4]

        def fox_qk(s):
            return ("FQA", s) if s < 4 else ("FQB", s - 4)

        def tmp_of(k):
            return (tmp, tmp2)[k // 4][:, k % 4, :]

        CV = {"CU0": 0, "SI": 44, "CU1": 52}
        CONV = {"CU0": 0, "CU1": 44}
        SL = {"GG": 0, "CU0": 8, "CU1": 30}
        NORMS = {}
        n_t = 0
        for n, (name, tiles, tok, feats) in enumerate(
                [("mix0", 8, True, D), ("ffn0", 8, False, D), ("mix1", 8, False, D), ("kv_a", 2, True, KVLORA),
                 ("q_a", 3, False, QLORA), ("ffn1", 8, False, D), ("final1", 8, True, D), ("mix2", 0, True, D),
                 ("ffn2", 8, False, D), ("mix3", 8, False, D), ("ffn3", 8, False, D), ("final2", 7, True, D)]):
            NORMS[name] = (n, tiles, n_t, tok, feats)
            n_t += tiles
        ROOTS = ["mix0", "mix1", "kv_a", "q_a", "mix2", "final1", "ffn2", "mix3", "ffn3", "final2"]

        def sums_before(name):
            n, _, tiles_before, _, _ = NORMS[name]
            return tiles_before + n - (n > NORMS["mix2"][0])

        def stat_cols(name):
            if name == "final2":
                return slice(T, T + TT)
            return slice(0, T + TT if NORMS[name][3] else T)

        def rstd_of(name):
            return rstd[:, NORMS[name][0] % 3, :]

        def chunk_view(t, slot, kind):
            k = {"full": 8, "narrow": 8, "lat": 3, "kvb": 2}[kind]
            n = {"full": 256, "narrow": 128, "lat": 512, "kvb": 1024}[kind]
            return t[:, slot, 0:k * n].rearrange("p (k n) -> p k n", k=k)

        def kind_of(c):
            if c == C0["FG"]:
                return "narrow", 8
            if c in (C0["QR"], C0["QA"], C0["QN"]):
                return "lat", 3
            if c in (C0["KB"], C0["VB"]):
                return "kvb", 2
            for s in ("CD0", "CD1"):
                if C0[s] <= c < C0[s] + 16:
                    return "full", CD_K[(c - C0[s]) % 4]
            return "full", 8

        HALF = {"full": 128, "narrow": 128, "lat": 256, "kvb": 512}

        def raw_half(c, j):
            kind, nk = kind_of(c)
            w = HALF[kind]
            if kind == "narrow" and j:
                return chunk_view(w_raw, c % RAW_SLOTS, kind)[:, 0:nk, 0:1]
            return chunk_view(w_raw, c % RAW_SLOTS, kind)[:, 0:nk, j * w:(j + 1) * w]

        def split_half(t, c, j):
            kind, nk = kind_of(c)
            w = 1 if kind == "narrow" and j else HALF[kind]
            at = j * (CHUNK // 2)
            return t[:, c % W_SLOTS, at:at + nk * w].rearrange("p (k n) -> p k n", k=nk)

        def ahead(c, j):
            h = 2 * c + j + AHEAD
            return (h // 2, h % 2) if h < 2 * N_CHUNKS else None

        block = ctx.enter_context(nc.Block())

        @block.sync
        def _(sp):
            def load(c, dst, src, it=STRAIGHT):
                if c >= RAW_SLOTS:
                    sp.wait_ge(w_lo_ready, halves_before(c - RAW_SLOTS + 1, 0, it))
                sp.dma_start(dst, src).then_inc(raw_landed[c % RAW_SLOTS], 16)

            def ktiles(w):
                return w.rearrange("(k p) n -> p k n", p=P)

            def full(c):
                return chunk_view(w_raw, c % RAW_SLOTS, "full")

            def plain(stage, w, cols):
                for j, col in enumerate(cols):
                    c = C0[stage] + j
                    load(c, full(c), ktiles(w)[:, :, col:col + CW])

            def up(stage, w):
                with sp.Fori(0, 4) as i:
                    for cc in range(4):
                        c = C0[stage] + cc
                        load(c, full(c), ktiles(w)[:, :, ds(i * (4 * CW) + cc * CW, CW)], (i, 4, 8))

            def down(stage, w):
                with sp.Fori(0, 4) as i:
                    for cc in range(4):
                        c = C0[stage] + cc
                        load(c, full(c), ktiles(w)[:, 8 * cc:8 * cc + 8, ds(i * CW, CW)], (i, 4, 2))

            def conv_up(stage, w):
                def body(i, cc, it):
                    c = C0[stage] + cc
                    col = (cc // 2) * CW + (cc % 2) * DFF2 + i * (2 * CW)
                    src = ktiles(w)[:, :, ds(col, CW)] if it[1] else ktiles(w)[:, :, col:col + CW]
                    load(c, full(c), src, it)

                for cc in range(2):
                    body(0, cc, STRAIGHT)
                with sp.Fori(0, 5) as i:
                    for cc in range(2, 6):
                        body(i, cc, (i, 4, 8))

            def conv_down(stage, w):
                def body(i, cc, it):
                    c = C0[stage] + cc
                    k0, nk = sum(CD_K[:cc % 4]), CD_K[cc % 4]
                    cols = ds(i * CW, CW) if it[1] else slice((cc // 4) * CW, (cc // 4 + 1) * CW)
                    load(c, full(c)[:, 0:nk, :], ktiles(w)[:, k0:k0 + nk, cols], it)

                with sp.Fori(0, 3) as i:
                    for cc in range(4):
                        body(i, cc, (i, 4, 2))
                for cc in range(12, 16):
                    body(0, cc, STRAIGHT)

            w = io["fox_w_in"][0]
            sp.dma_start(full(0)[:, :, 0:P], ktiles(w)[:, :, 0:P]).then_inc(first_landed, 16)
            for k in range(0, KD, 4):
                sp.dma_start(x[:, k:k + 4, :], ktiles(io["xT"])[:, k:k + 4, :]).then_inc(x_landed[k // 4], 16)
            load(0, full(0)[:, :, P:CW], ktiles(w)[:, :, P:CW])
            load(1, full(1), ktiles(w)[:, :, D:D + CW])
            sp.dma_start(ones, io["con"][:, 0:P]).then_inc(ones_landed, 16)
            gate_chunk = chunk_view(w_raw, C0["FG"] % RAW_SLOTS, "narrow")
            for dst, src in ((slice(0, FOX_H), slice(3 * D, 3 * D + FOX_H)), (slice(FOX_H, P), slice(0, P - FOX_H))):
                sp.dma_start(gate_chunk[:, :, dst], ktiles(w)[:, :, src]).then_inc(raw_landed[C0["FG"] % RAW_SLOTS], 16)
            sp.dma_start(f_bias[:], io["fox_b_f"][0].rearrange("(h o) -> h o", o=1)).then_inc(fox_small_landed, 16)
            load(C0["FQB"], full(C0["FQB"]), ktiles(w)[:, :, CW:2 * CW])
            sp.dma_start(con[:, P:N_CON], io["con"][:, P:N_CON]).then_inc(con_landed, 16)
            for j in range(3, 8):
                c = C0["FQB"] + j - 2
                col = CW * (j // 2) + D * (j % 2)
                load(c, full(c), ktiles(w)[:, :, col:col + CW])
            sp.dma_start(g_bias[:], io["gla_b_gate_2"][0:1, :].partition_broadcast(P)).then_inc(gla_small_landed, 16)
            sp.dma_start(g_up[:], io["gla_w_gate_up_2"][0]).then_inc(gla_small_landed, 16)
            plain("FV", w, [2 * D + CW * j for j in range(4)])
            plain("FO", io["fox_w_out"][0], [CW * j for j in range(4)])
            up("U0", io["ffn_w_up"][0])
            down("D0", io["ffn_w_down"][0])
            c = C0["KVQ"]
            wkv, wq = ktiles(io["mla_w_kv_a"]), ktiles(io["mla_w_q_a"][0])
            load(c, full(c), wkv[:, :, 0:KVLORA])
            load(c + 1, full(c + 1), wq[:, :, 0:256])
            sp.wait_ge(w_lo_ready, halves_before(c + 2 - RAW_SLOTS + 1, 0))
            for dst, src in [(full(c + 2)[:, :, 0:64], wkv[:, :, KVLORA:KVLORA + ROPE]),
                             (full(c + 2)[:, :, 64:128], wkv[:, :, KVLORA:KVLORA + ROPE]),
                             (full(c + 2)[:, :, 128:256], wq[:, :, 256:384])]:
                sp.dma_start(dst, src).then_inc(raw_landed[(c + 2) % RAW_SLOTS], 16)
            wkvb = io["mla_w_kv_b"].rearrange("(k p) (h n) -> p k h n", p=P, h=MLA_H)
            wqb = io["mla_w_q_b"][0].rearrange("(k p) (h n) -> p k h n", p=P, h=MLA_H)
            for stage, w, heads, cols in (("KB", wkvb, slice(0, 8), slice(0, NOPE)), ("QR", wqb, slice(0, 8), slice(NOPE, NOPE + ROPE)),
                                          ("QA", wqb, slice(0, 4), slice(0, NOPE)), ("VB", wkvb, slice(0, 8), slice(NOPE, NOPE + VDIM)),
                                          ("QN", wqb, slice(4, 8), slice(0, NOPE))):
                c = C0[stage]
                kind, nk = kind_of(c)
                sp.wait_ge(w_lo_ready, halves_before(c - RAW_SLOTS + 1, 0))
                for k in range(nk):
                    dst = chunk_view(w_raw, c % RAW_SLOTS, kind)[:, k, :].rearrange("p (h n) -> p h n", h=heads.stop - heads.start)
                    sp.dma_start(dst, w[:, k, heads, cols]).then_inc(raw_landed[c % RAW_SLOTS], 16)
            plain("MO", io["mla_w_out"][0], [CW * j for j in range(4)])
            up("U1", io["ffn_w_up"][1])
            down("D1", io["ffn_w_down"][1])
            w = io["gla_w_in_2"][0]
            c = C0["GA"]
            load(c, full(c)[:, :, 0:GATE_RANK], ktiles(w)[:, :, 3 * D:3 * D + GATE_RANK])
            plain("GQK", w, [CW * j for j in range(4)])
            plain("GV", w, [D + CW * j for j in range(4)])
            plain("GG", w, [2 * D + CW * j for j in range(4)])
            plain("GO", io["gla_w_out_2"][0], [CW * j for j in range(4)])
            conv_up("CU0", io["ffn_w_up_2"][0])
            conv_down("CD0", io["ffn_w_down_2"][0])
            plain("SI", io["sc_w_in_2"][0], [CW * (j // 3) + D * ((j % 3 + 1) % 3) for j in range(12)])
            plain("SO", io["sc_w_out_2"][0], [CW * j for j in range(4)])
            conv_up("CU1", io["ffn_w_up_2"][1])
            conv_down("CD1", io["ffn_w_down_2"][1])
            for k in range(0, KD, 2):
                sp.wait_ge(resid_ready, RT["x1"] + KD + k + 2)
                sp.dma_start(ktiles(io["out"])[:, k:k + 2, :], x[:, k:k + 2, :]).then_inc(out_landed, 16)
            sp.wait_ge(out_landed, 16 * KD // 2)

        @block.gpsimd
        def _(pool):
            zeroed = [0]

            def zero(name):
                n, tiles, before, _, _ = NORMS[name]
                if n:
                    pool.wait_ge(stat_done, n)
                nc.gpsimd.memset(ssq[:], 0.0).then_inc(pool_sum, 1)

            def add(name, m, tile, i=0, step=0):
                n, tiles, before, _, _ = NORMS[name]
                t = before + m + step * i - (4 if n else 0)
                pool.wait_ge(pool_sum, sums_before(name) + 1 + m + step * i)
                nc.gpsimd.tensor_tensor(sqt[:], tile, tile, ALU.mult).then_inc(pool_sq, 1)
                pool.wait_ge(pool_sq, t + 1)
                nc.gpsimd.tensor_tensor(ssq[:], ssq[:], sqt[:], ALU.add).then_inc(pool_sum, 1)

            def straight(name, sig, base):
                zero(name)
                for m in range(NORMS[name][1]):
                    pool.wait_ge(sig, base + m + 1)
                    add(name, m, x[:, m, :])

            def looped(name, sig, base):
                zero(name)
                with pool.Fori(0, 4) as i:
                    for j in range(2):
                        pool.wait_ge(sig, base + j + 1 + 2 * i)
                        add(name, j, x[:, ds(2 * i + j, 1), :], i, 2)

            def gate(stage):
                def product(t, i):
                    n = 4 * (t // 2) + 2 + t % 2
                    y = tmp[:, n % 4, :]
                    pool.wait_ge(conv_done, CONV[stage] + n + 1 + 8 * i)
                    pool.wait_ge(silu_ready, SL[stage] + t + 1 + 4 * i)
                    nc.gpsimd.tensor_tensor(y, y, tmp2[:, n % 2, :], ALU.mult).then_inc(gated_ready, 1)

                def low(t, i):
                    y = tmp[:, 2 + t % 2, :]
                    hi, lo = (hid[:, t, k, :] if isinstance(i, int) else hid[:, ds(4 * i + t, 1), k, :] for k in range(2))
                    pool.wait_ge(act_hi_ready, AT[stage] + t + 1 + 4 * i)
                    nc.gpsimd.tensor_tensor(lo, y, hi.bitcast(F32), ALU.subtract).then_inc(act_ready, 1)

                def pair(t, i):
                    for step in (product, low):
                        for k in range(2):
                            step(t + k, i)

                pair(0, 0)
                with pool.Fori(0, 5) as i:
                    for t in (2, 4):
                        pair(t, i)

            zero("mix0")
            pool.wait_ge(x_landed[0], 16)
            for m in range(4):
                add("mix0", m, x[:, m, :])
            for m in range(4):
                pool.wait_ge(sq_x, m + 1)
                pool.wait_ge(pool_sum, 5 + m)
                nc.gpsimd.tensor_tensor(ssq[:], ssq[:], tmp[:, m, :], ALU.add).then_inc(pool_sum, 1)
            straight("ffn0", dve_evac, DE["FO"])
            looped("mix1", resid_ready, RT["D0"])
            zero("kv_a")
            for m in range(2):
                pool.wait_ge(dve_evac, DE["KVQ"] + m + 1)
                add("kv_a", m, m_lat[:, m, :])
            zero("q_a")
            for m in range(3):
                pool.wait_ge(dve_evac, DE["KVQ"] + (3, 4, 6)[m])
                add("q_a", m, m_lat[:, 2 + m, :])
            for n in range(5):
                pool.wait_ge(dve_evac, DE["KVQ"] + 5 if n == 0 else DE["QR"] + n)
                if n == 0:
                    pool.wait_ge(act_ready, AT["lat"] + 5)
                nc.gpsimd.tensor_tensor(m_lat[:, n, :], m_kr_raw[:] if n == 0 else m_qr_raw[:, n - 1, :], cos_t,
                                        ALU.mult).then_inc(rope_cos, 1)
            straight("ffn1", dve_evac, DE["MO"])
            zero("final1")
            nc.gpsimd.memset(ssq_x1[:], 0.0).then_inc(x1_sum, 1)
            pool.wait_ge(gains_ready, 2)
            before, sums = NORMS["final1"][2] - 4, sums_before("final1")
            with pool.Fori(0, 4) as i:
                for j in range(2):
                    pool.wait_ge(resid_ready, RT["D1"] + j + 1 + 2 * i)
                    t = ds(2 * i + j, 1)
                    pool.wait_ge(pool_sum, sums + 1 + j + 2 * i)
                    nc.gpsimd.tensor_tensor(sqt[:], x[:, t, :], x[:, t, :], ALU.mult).then_inc(pool_sq, 1)
                    pool.wait_ge(pool_sq, before + j + 1 + 2 * i)
                    pool.wait_ge(x1_sum, 1 + j + 2 * i)
                    gain_sq = vec[:, ds(2 * i + VEC["final1_sq"] + j, 1)]
                    nc.gpsimd.tensor_tensor(sqt_x1[:], sqt[:], gain_sq.broadcast_to([P, T]), ALU.mult).then_inc(x1_scaled, 1)
                    pool.wait_ge(x1_scaled, 1 + j + 2 * i)
                    nc.gpsimd.tensor_tensor(ssq_x1[:], ssq_x1[:], sqt_x1[:], ALU.add).then_inc(x1_sum, 1)
                    nc.gpsimd.tensor_tensor(ssq[:], ssq[:], sqt[:], ALU.add).then_inc(pool_sum, 1)
            pool.wait_ge(dve_evac, DE["GQK"] + 1)
            nc.gpsimd.memset(g_sT[:], 0.0).then_inc(gla_zeroed, 1)
            for h in range(GLA_H):
                pool.wait_ge(gla_act, 13 + 4 * h)
                nc.gpsimd.tensor_tensor(tmp_of(2 * h), tmp_of(2 * h), tmp_of(2 * h + 1), ALU.add).then_inc(head_sq, 1)
            for m in range(KD - 1):
                pool.wait_ge(silu_ready, SL["GG"] + m + 1)
                nc.gpsimd.tensor_tensor(g_o[:, m, :], g_o[:, m, :], g_g[:, m, :], ALU.mult).then_inc(head_gated, 1)
            straight("ffn2", dve_evac, DE["GO"])
            gate("CU0")
            straight("mix3", dve_evac, DE["CD0"])
            straight("ffn3", dve_evac, DE["SO"])
            gate("CU1")
            straight("final2", dve_evac, DE["CD1"])

        @block.tensor
        def _(pe):
            freed = [None] * 4

            def take_bank(stage, n, done):
                b = (TURN[stage] + n) % 4
                if freed[b] is not None:
                    pe.wait_ge(*freed[b])
                freed[b] = done
                return gemm[b]

            def split_ready(c, j, it=STRAIGHT):
                pe.wait_ge(w_lo_ready, halves_before(c, j, it) + 1)

            def feature_block(ps, c, j, act, k0=0, col=0, start=True, stop=True, tiles=None):
                wh, wl = split_half(w_hi, c, j), split_half(w_lo, c, j)
                nk, cols = kind_of(c)[1], slice(col, col + P)
                last = None
                for k in range(nk):
                    if tiles is not None:
                        pe.wait_ge(act_ready, tiles[k] if isinstance(tiles, list) else tiles + k + 1)
                    nc.tensor.matmul(ps, wh[:, k, cols], act[:, k0 + k, 0, :], start=start and k == 0, stop=False)
                    nc.tensor.matmul(ps, wh[:, k, cols], act[:, k0 + k, 1, :], start=False, stop=False)
                    last = nc.tensor.matmul(ps, wl[:, k, cols], act[:, k0 + k, 0, :], start=False,
                                            stop=stop and k == nk - 1)
                return last

            def token_block(ps, wh, wl, t, act):
                tok = slice(t * P, (t + 1) * P)
                nk = act.shape[1]
                for k in range(nk):
                    nc.tensor.matmul(ps, act[:, k, 0, tok], wh(k), start=k == 0, stop=False)
                    nc.tensor.matmul(ps, act[:, k, 1, tok], wh(k), start=False, stop=False)
                    last = nc.tensor.matmul(ps, act[:, k, 0, tok], wl(k), start=False, stop=k == nk - 1)
                return last

            def stat(name):
                n, tiles, _, tok, _ = NORMS[name]
                if name == "mix2":
                    pe.wait_ge(x1_sum, 1 + KD)
                    pe.wait_ge(probsT_ready, FOX_H + MLA_H)
                    to, sums = trans, ssq_x1
                else:
                    pe.wait_ge(pool_sum, sums_before(name) + 1 + tiles)
                    if n:
                        pe.wait_ge(var_ready, n)
                    to, sums = misc, ssq
                if name == "final2":
                    pe.wait_ge(last_sq, 1)
                    for t in range(TT):
                        cols, col = slice(t * P, (t + 1) * P), slice(T + t, T + t + 1)
                        nc.tensor.matmul(to[:, col], sums[:, cols], ones[:, 0:1], start=True, stop=False)
                        last = nc.tensor.matmul(to[:, col], sqt_x1[:, cols], ones[:, 0:1], start=False, stop=True)
                    last.then_inc(stat_done, 1)
                    return
                last = nc.tensor.matmul(to[:, 0:T], ones, sums[:], start=True, stop=True)
                if tok:
                    for t in range(TT):
                        last = nc.tensor.matmul(to[:, T + t:T + t + 1], sums[:, t * P:(t + 1) * P], ones[:, 0:1],
                                                start=True, stop=True)
                last.then_inc(stat_done, 1)

            def plain(stage, act, tiles, evac, base, nch=4):
                for n in range(2 * nch):
                    c, j = C0[stage] + n // 2, n % 2
                    split_ready(c, j)
                    ps = take_bank(stage, n, (evac, base + n + 1))
                    feature_block(ps[:, 0:T], c, j, act, tiles=tiles if n == 0 else None).then_inc(half_done, 1)

            def token_half(stage, n, act, evac, base):
                c, t = C0[stage] + n // 2, n % 2
                split_ready(c, 1)

                def both_halves(w):
                    v = w[:, c % W_SLOTS, :].rearrange("p (j k n) -> p j k n", j=2, k=KD)
                    return lambda k: v[:, :, k, :]

                ps = take_bank(stage, n, (evac, base + n + 1))[:, 0:CW].rearrange("p (j n) -> p j n", j=2)
                last = token_block(ps, both_halves(w_hi), both_halves(w_lo), t, act)
                if t == 1:
                    last.then_inc(half_done, 2)

            def up(stage, tiles, norm):
                b0 = TURN[stage]
                before = list(freed)
                with pe.Fori(0, 4) as i:
                    it = (i, 4, 8)
                    for n in range(8):
                        c, j = C0[stage] + n // 2, n % 2
                        split_ready(c, j, it)
                        b = (b0 + n) % 4
                        if n < 4:
                            pe.wait_ge(*before[b])
                        pe.wait_ge(act_evac, AE[stage] + n - 3 + 8 * i)
                        feature_block(gemm[b][:, 0:T], c, j, act_a, tiles=tiles if n == 0 else None).then_inc(half_done, 1)
                for b in range(4):
                    freed[(b0 + b) % 4] = (act_evac, AE[stage] + 28 + b + 1)
                stat(norm)

            def down(stage, tiles):
                b0 = TURN[stage]
                before = list(freed)
                with pe.Fori(0, 4) as i:
                    it = (i, 4, 2)
                    for cc in range(4):
                        c = C0[stage] + cc
                        for j in range(2):
                            b = (b0 + j) % 4
                            split_ready(c, j, it)
                            if cc == 0:
                                pe.wait_ge(*before[b])
                                pe.wait_ge(dve_evac, DE[stage] + j - 1 + 2 * i)
                            feature_block(gemm[b][:, 0:T], c, j, hid, k0=8 * cc,
                                          start=cc == 0, stop=cc == 3,
                                          tiles=tiles + 8 * cc if j == 0 else None).then_inc(half_done, 1)
                for j in range(2):
                    freed[(b0 + j) % 4] = (dve_evac, DE[stage] + 6 + j + 1)

            def conv_up(stage, tiles, norm):
                b0 = TURN[stage]
                before = list(freed)

                def body(n, it, i):
                    c, j = C0[stage] + n // 2, n % 2
                    b = (b0 + n) % 4
                    split_ready(c, j, it)
                    if n < 4:
                        pe.wait_ge(*before[b])
                    else:
                        pe.wait_ge(dve_evac, DE[stage] + n - 3 + 8 * i)
                    feature_block(gemm[b][:, 0:T], c, j, act_a, tiles=tiles if n == 0 else None).then_inc(half_done, 1)

                for n in range(4):
                    body(n, STRAIGHT, 0)
                    if n == 0:
                        stat(norm)
                with pe.Fori(0, 5) as i:
                    for n in range(4, 12):
                        body(n, (i, 4, 8), i)
                for n in range(40, 44):
                    freed[(b0 + n) % 4] = (dve_evac, DE[stage] + n + 1)

            def conv_down(stage, tiles):
                b0 = TURN[stage]
                before = list(freed)

                def body(cc, it, i):
                    c = C0[stage] + cc
                    k0 = sum(CD_K[:cc % 4])
                    for j in range(2):
                        b = (b0 + j) % 4
                        split_ready(c, j, it)
                        if cc % 4 == 0:
                            pe.wait_ge(*before[b])
                            pe.wait_ge(dve_evac, DE[stage] + j - 1 + 2 * i)
                        feature_block(gemm[b][:, 0:T], c, j, hid, k0=k0,
                                      start=cc % 4 == 0, stop=cc % 4 == 3,
                                      tiles=tiles + k0 if j == 0 else None).then_inc(half_done, 1)

                with pe.Fori(0, 3) as i:
                    for cc in range(4):
                        body(cc, (i, 4, 2), i)
                for cc in range(12, 16):
                    body(cc, STRAIGHT, 3)
                for j in range(2):
                    freed[(b0 + j) % 4] = (dve_evac, DE[stage] + 6 + j + 1)

            def transposes(n, prob, base, slots):
                g = base + n
                pe.wait_ge(probs_normed, 2 * g + 2)
                if g:
                    pe.wait_ge(probsT_ready, g)
                nc.tensor.transpose(trans[:, 0:128], prob[:, n % slots, 0:128], ident)
                nc.tensor.transpose(trans[:, 128:256], prob[:, n % slots, 128:256], ident)
                nc.tensor.transpose(trans[:, 256:384], prob[:, n % slots, 256:384], ident).then_inc(transposed, 1)

            def fox_gates():
                c = C0["FG"]
                split_ready(c, 0)
                ps = take_bank("FG", 0, (dve_evac, DE["FG"] + 1))
                feature_block(ps[:, 0:T], c, 0, act_a).then_inc(half_done, 1)

            def fox_gates_transposed():
                pe.wait_ge(gate_step, 6)
                for t in range(TT):
                    last = nc.tensor.transpose(trans[:, t * FOX_H:(t + 1) * FOX_H], f_z[:, t * P:(t + 1) * P], ident[0:FOX_H, 0:FOX_H])
                last.then_inc(cum_done, 1)

            def fox_cum():
                pe.wait_ge(gate_step, 7)
                for t in range(TT):
                    last = nc.tensor.matmul(trans[0:FOX_H, 0:T], f_ls[:, t, :], tri[:, t, :], start=t == 0, stop=t == TT - 1)
                last.then_inc(cum_done, 1)

            def fox_scores(h):
                stage, n = fox_qk(4 * (h // 4) + 2 + h // 2 % 2)
                pe.wait_ge(dve_evac, DE[stage] + n + 1)
                if h == 0:
                    pe.wait_ge(cum_ready, 4)
                    pe.wait_ge(sel_ready, 1)
                else:
                    pe.wait_ge(logits_ready, 2 * (h - 1) + 2)
                for q, cols, keys in ((0, slice(0, 128), 128), (1, slice(128, 384), 256)):
                    for e in range(2):
                        r = slice(64 * e, 64 * e + 64)
                        nc.tensor.matmul(score[e][:, cols], f_q[r, h // 2, q * P:(q + 1) * P], f_k[r, h // 2, 0:keys],
                                         start=True, stop=False)
                    for e in range(2):
                        r = slice(64 * e, 64 * e + 64)
                        last = nc.tensor.matmul(score[e][:, cols], f_sel[r, h + e, :], f_cum[r, 0:keys], start=False, stop=True)
                        if q:
                            last.then_inc(scores_done, 1)

            def fox_pv(h):
                r = slice(64 * (h % 2), 64 * (h % 2) + 64)
                cols = slice(64 * h, 64 * h + 64)
                pe.wait_ge(probsT_ready, h + 1)
                if h % 4 == 0:
                    pe.wait_ge(act_evac, AE["FV"] + 2 * (h // 4) + 2)
                if h % 2 == 0:
                    take_bank("FPV", h // 2, (act_ready, AT["fctx"] + h // 2 + 1))
                ps = bank_of("FPV", h // 2)
                nc.tensor.matmul(ps[r, 0:T], f_v[:, 0, cols], f_probT[:, h % FOX_T, 0:256], start=True, stop=False)
                nc.tensor.matmul(ps[r, P:T], f_v[:, 1, cols], f_probT[:, h % FOX_T, 256:384], start=False,
                                 stop=True).then_inc(pv_done, 1)

            for s in range(26):
                if s < 16:
                    stage, n = fox_qk(s)
                    c, j = C0[stage] + n // 2, n % 2
                    split_ready(c, j)
                    ps = take_bank(stage, n, (dve_evac, DE[stage] + n + 1) if s else (act_evac, AE["FQA"] + 1))
                    last = feature_block(ps[:, 0:T], c, j, act_a, tiles=AT["x"] if s == 0 else None)
                    last.then_inc(half_done, 2 if s == 4 else 1)
                elif s < 24:
                    token_half("FV", s - 16, act_a, act_evac, AE["FV"])
                if s == 2:
                    pe.wait_ge(ones_landed, 16)
                    stat("mix0")
                if s == 3:
                    fox_gates()
                if s == 6:
                    pe.wait_ge(con_landed, 16)
                    fox_gates_transposed()
                if s == 7:
                    fox_cum()
                if FOX_LAG <= s < FOX_LAG + 16 and (s - FOX_LAG) % 2 == 0:
                    fox_scores(s - FOX_LAG)
                if FOX_LAG + 2 <= s < FOX_LAG + 18:
                    transposes(s - FOX_LAG - 2, f_prob, 0, 3)
                if s >= 18:
                    fox_pv(2 * (s - 18))
                    fox_pv(2 * (s - 18) + 1)
            plain("FO", act_b, AT["fctx"], dve_evac, DE["FO"])

            up("U0", AT["FO"], "ffn0")
            down("D0", AT["U0"])

            c = C0["KVQ"]
            for n, act in enumerate([act_b, act_b, act_a, act_a, act_b, act_a]):
                split_ready(c + n // 2, n % 2)
                ps = take_bank("KVQ", n, (dve_evac, DE["KVQ"] + n + 1))
                tiles = [AT["D0"] + 4 * (k // 2) + k % 2 + 1 + n for k in range(KD)] if n in (0, 2) else None
                feature_block(ps[:, 0:T], c + n // 2, n % 2, act, tiles=tiles).then_inc(half_done, 1)
                if n == 0:
                    stat("mix1")
                if n == 4:
                    stat("kv_a")
            pe.wait_ge(act_ready, AT["lat"] + 2)
            for j in range(2):
                split_ready(C0["KB"], j)
                for n in range(4 * j, 4 * j + 4):
                    ps = take_bank("KB", n, (dve_evac, DE["KB"] + n + 1))
                    last = feature_block(ps[:, 0:T], C0["KB"], j, m_act, col=(n % 4) * P)
                    last.then_inc(*((key_done, 1) if n % 4 < 3 else (half_done, 1)))
                    if n == 5:
                        stat("q_a")
            pe.wait_ge(act_ready, AT["lat"] + 5)

            def q_half(stage, j):
                c = C0[stage]
                split_ready(c, j)
                for n in range(2):
                    ps = take_bank(stage, 2 * j + n, (dve_evac, DE[stage] + 2 * j + n + 1))[:, 0:T]
                    last = feature_block(ps, c, j, m_act, k0=2, col=n * P)
                last.then_inc(half_done, 1)

            def v_half(j):
                split_ready(C0["VB"], j)
                wh, wl = split_half(w_hi, C0["VB"], j), split_half(w_lo, C0["VB"], j)
                for t in range(TT):
                    ps = take_bank("VB", 2 * j + t, (act_evac, AE["VB"] + 2 * j + t + 1))
                    last = token_block(ps[:], lambda k: wh[:, k, :], lambda k: wl[:, k, :], t, m_act[:, 0:2])
                last.then_inc(half_done, 1)

            def rotate(n):
                src = m_kr_raw[:] if n == 0 else m_qr_raw[:, n - 1, :]
                pe.wait_ge(dve_evac, DE["KVQ"] + 5 if n == 0 else DE["QR"] + n)
                if n == 0:
                    pe.wait_ge(probsT_ready, FOX_H)
                    pe.wait_ge(logits_ready, 2 * FOX_H)
                if n == 1:
                    pe.wait_ge(var_ready, NORMS["q_a"][0] + 1)
                if n >= 3:
                    pe.wait_ge(rope_step, 2 * (n - 3) + 1)
                nc.tensor.matmul(rot_place[n], rot, src, start=True, stop=True).then_inc(rot_done, 1)

            def mla_scores(h):
                pe.wait_ge(dve_evac, DE["QA"] + h + 2 if h < 4 else DE["QN"] + h - 4 + 2)
                pe.wait_ge(rope_step, 6 if h == 0 else 10)
                pe.wait_ge(logits_ready, 2 * (FOX_H + h))
                for q, cols, keys in ((0, slice(0, 128), 128), (1, slice(128, 384), 256)):
                    qs = slice(q * P, (q + 1) * P)
                    for e in range(2):
                        nc.tensor.matmul(score[e][:, cols], m_q[:, h + e, qs], m_k[:, h + e, 0:keys], start=True, stop=False)
                    for e in range(2):
                        r = slice(64 * e, 64 * e + 64)
                        last = nc.tensor.matmul(score[e][:, cols], m_qr[r, h // 2, qs], m_kr[r, 0:keys], start=False, stop=True)
                        if q:
                            last.then_inc(scores_done, 1)

            def mla_pv(h):
                cols = slice(VDIM * h, VDIM * h + VDIM)
                pe.wait_ge(probsT_ready, FOX_H + h + 1)
                if h == 0:
                    pe.wait_ge(act_evac, AE["VB"] + 4)
                ps = take_bank("MPV", h, (act_ready, AT["mctx"] + h + 1))
                nc.tensor.matmul(ps[:, 0:T], m_v[:, 0, cols], m_probT[:, h % 2, 0:256], start=True, stop=False)
                nc.tensor.matmul(ps[:, P:T], m_v[:, 1, cols], m_probT[:, h % 2, 256:384], start=False,
                                 stop=True).then_inc(pv_done, 1)

            q_half("QR", 0)
            rotate(0)
            q_half("QR", 1)
            rotate(1)
            rotate(2)
            for s in range(MLA_H + 4):
                if s < 6:
                    (q_half, q_half, v_half, v_half, q_half, q_half)[s](
                        *(("QA", 0), ("QA", 1), (0,), (1,), ("QN", 0), ("QN", 1))[s])
                if s == 0:
                    rotate(3)
                    rotate(4)
                if 1 <= s <= MLA_H and s % 2:
                    mla_scores(s - 1)
                if 3 <= s < MLA_H + 3:
                    transposes(s - 3, m_prob, FOX_H, 3)
                if s >= 4:
                    mla_pv(s - 4)
            plain("MO", act_b, AT["mctx"], dve_evac, DE["MO"])
            up("U1", AT["MO"], "ffn1")
            down("D1", AT["U1"])

            split_ready(C0["GA"], 1)
            ps = take_bank("GA", 0, (dve_evac, DE["GA"] + 1))
            feature_block(ps[:, 0:T], C0["GA"], 0, act_a, tiles=AT["x1"]).then_inc(half_done, 2)
            pe_step = [0]

            def step(last):
                pe_step[0] += 1
                last.then_inc(gla_pe, 1)

            def gla_gates():
                pe.wait_ge(dve_evac, DE["GA"] + 1)
                pe.wait_ge(gla_small_landed, 32)
                for t in range(TT):
                    step(nc.tensor.matmul(score[t][:, 0:512], g_aT[:, t * P:(t + 1) * P], g_up[:], start=True, stop=True))

            def gla_cum():
                pe.wait_ge(gla_dve, 4)
                for g in range(2):
                    for h in range(2 * g, 2 * g + 2):
                        for t in range(TT):
                            last = nc.tensor.matmul(score[g][:, (h % 2) * T + t * P:(h % 2) * T + (t + 1) * P],
                                                    g_z[:, t, h * P:(h + 1) * P], tri_chunk, start=True, stop=True)
                    step(last)

            for n in range(8):
                c, j = C0["GQK"] + n // 2, n % 2
                split_ready(c, j)
                ps = take_bank("GQK", n, (dve_evac, DE["GQK"] + n + 1))
                feature_block(ps[:, 0:T], c, j, act_a).then_inc(half_done, 1)
                if n == 0:
                    stat("final1")
                    stat("mix2")
                if n == 2:
                    gla_gates()

            def gla_scores(t):
                pe.wait_ge(gla_dve, 8)
                for h in range(GLA_H):
                    tok = slice(t * P, (t + 1) * P)
                    last = nc.tensor.matmul(score[t][:, h * P:(h + 1) * P], g_ki[:, h, tok], g_qi[:, h, tok], start=True,
                                            stop=True)
                step(last)

            def gla_transpose(t):
                pe.wait_ge(gla_dve, 9)
                if t:
                    pe.wait_ge(gla_act, 8)
                for h in range(GLA_H):
                    last = nc.tensor.transpose(trans[:, h * P:(h + 1) * P], g_kd[:, h, t * P:(t + 1) * P], ident)
                step(last)

            def gla_states(chunks):
                pe.wait_ge(gla_act, 9)
                pe.wait_ge(act_evac, AE["GV"] + 8)
                pe.wait_ge(gla_dve, 11 if chunks[0] == 0 else 15)
                for h in range(GLA_H):
                    for n in chunks:
                        t, r = n // 2, slice(GLA_C * (n % 2), GLA_C * (n % 2) + GLA_C)
                        last = nc.tensor.matmul(state_place(n, h), g_kdT[r, t, h * P:(h + 1) * P],
                                                g_v[r, t, h * GLA_DV:(h + 1) * GLA_DV], start=True, stop=True)
                        if h == GLA_H - 1:
                            step(last)

            def gla_out(n):
                h = n // 2
                e = slice(n * P, (n + 1) * P)
                s = slice((n % 2) * P, (n % 2) * P + P)
                bank_ = gla_bank[n % 4]
                if n == 0:
                    pe.wait_ge(gla_act, 9)
                    pe.wait_ge(gla_dve, 23)
                if n >= 4:
                    pe.wait_ge(gla_act, 9 + 2 * (n - 4) + 2)
                for t in range(TT):
                    nc.tensor.matmul(bank_[:, t * P:(t + 1) * P], g_v[:, t, e], g_sT[:, t, h * P:(h + 1) * P],
                                     start=t == 0, stop=False)
                for m in range(1, T // GLA_C):
                    tok = slice(m * GLA_C, (m + 1) * GLA_C)
                    last = nc.tensor.matmul(bank_[:, tok], g_s[:, m - 1, h, s], g_qi[:, h, tok], start=False,
                                            stop=m == T // GLA_C - 1)
                step(last)

            def gla_stat():
                pe.wait_ge(gla_act, 25)
                for h in range(GLA_H):
                    pe.wait_ge(head_sq, h + 1)
                    last = nc.tensor.matmul(misc[0:GLA_H, 0:T], head_row[:, h * GLA_H:(h + 1) * GLA_H], tmp_of(2 * h), start=h == 0,
                                            stop=h == GLA_H - 1)
                step(last)

            def gla_spread(g):
                pe.wait_ge(gla_dve, 25)
                for h in range(2 * g, 2 * g + 2):
                    last = nc.tensor.matmul(score[g][:, (h % 2) * T:(h % 2) * T + T], ident[0:GLA_H, h:h + 1].broadcast_to([GLA_H, P]),
                                            g_rec, start=True, stop=True)
                step(last)

            for n in range(8):
                token_half("GV", n, act_a, act_evac, AE["GV"])
                if n == 0:
                    gla_cum()
                if n == 5:
                    gla_scores(0)
                    gla_scores(1)
                    gla_transpose(0)
            gla_transpose(1)
            for n in range(8):
                c, j = C0["GG"] + n // 2, n % 2
                split_ready(c, j)
                ps = take_bank("GG", n, (dve_evac, DE["GG"] + n + 1))
                feature_block(ps[:, 0:T], c, j, act_a).then_inc(half_done, 1)
                if n < 2:
                    gla_states(((0, 1), (2,))[n])
                if n in (2, 3):
                    for m in range(4):
                        gla_out(4 * (n - 2) + m)
                if n == 4:
                    gla_stat()
                if n == 6:
                    gla_spread(0)
                    gla_spread(1)
            plain("GO", act_b, AT["gla"], dve_evac, DE["GO"])

            conv_up("CU0", AT["GO"], "ffn2")
            conv_down("CD0", AT["CU0"])
            for n in range(24):
                c, j = C0["SI"] + n // 2, n % 2
                split_ready(c, j)
                g, part = n // 6, (n % 6) // 2
                done = (act_evac, AE["SI"] + 2 * g + j + 1) if part == 0 else (dve_evac, DE["SI"] + 4 * g + 2 * (part - 1) + j + 1)
                ps = take_bank("SI", n, done)
                feature_block(ps[:, 0:T], c, j, act_a, tiles=AT["CD0"] if n == 0 else None).then_inc(half_done, 1)
                if n == 0:
                    stat("mix3")
            plain("SO", act_b, AT["sc"], dve_evac, DE["SO"])
            conv_up("CU1", AT["SO"], "ffn3")
            conv_down("CD1", AT["CU1"])
            stat("final2")
            pe.wait_ge(rstd_ready, len(ROOTS))
            for t in range(TT):
                r = rstd_of("final2")[:, T + t:T + t + 1].broadcast_to([P, P])
                last = nc.tensor.matmul(trans[:, t * P:(t + 1) * P], r, ident, start=True, stop=True)
            last.then_inc(spread_done, 1)

        @block.scalar
        def _(act):
            act.dma_start(vec[:, 0:N_VEC], io["vec"]).then_inc(vec_landed, 16)

            def prep(c, j, it=STRAIGHT, first=False, more=0):
                nxt = (c, j) if first else ahead(c + (j + more) // 2, (j + more) % 2)
                if nxt is None:
                    return
                nc_, nj = nxt
                h = halves_before(nc_, nj, it)
                if nc_ == 0:
                    act.wait_ge((first_landed, raw_landed[0])[nj], 16)
                elif nj == 0:
                    act.wait_ge(raw_landed[nc_ % RAW_SLOTS], raw_count(nc_, it))
                if 2 * nc_ + nj >= 2 * W_SLOTS:
                    act.wait_ge(half_done, h - 2 * W_SLOTS + 1)
                nc.scalar.copy(split_half(w_hi, nc_, nj), raw_half(nc_, nj)).then_inc(w_hi_ready, 1)

            def dmas(c):
                if c == C0["KVQ"] + 2:
                    return 3
                if c == C0["FG"]:
                    return 2
                return kind_of(c)[1] if kind_of(c)[0] in ("lat", "kvb") else 1

            def raw_count(c, it):
                return 16 * sum(dmas(k) for k in range(c % RAW_SLOTS, c + 1, RAW_SLOTS)) + 16 * (it[1] // RAW_SLOTS) * it[0]

            def round_tile(dst, src, scale=None):
                if scale is None:
                    nc.scalar.copy(dst, src).then_inc(act_hi_ready, 1)
                else:
                    nc.scalar.activation(dst, src, ACT.Copy, scale=scale).then_inc(act_hi_ready, 1)

            def root(name):
                act.wait_ge(var_ready, NORMS[name][0] + 1)
                cols = stat_cols(name)
                nc.scalar.activation(std[:, cols], (var_x1 if name == "mix2" else var)[:, cols], ACT.Sqrt).then_inc(std_ready, 1)

            def plain_preps(stage, nch=4):
                for n in range(2 * nch):
                    prep(C0[stage] + n // 2, n % 2)
                    yield n

            def residual(stage, name, sig=None):
                for n in plain_preps(stage):
                    if n == 0:
                        nc.scalar.preload_act_table(ACT.Sqrt)
                    if name is not None:
                        act.wait_ge(dve_evac, DE[stage] + n + 1)
                        round_tile(act_a[:, n, 0, :], x[:, n, :], gain(name, n))

            def up(stage):
                nc.scalar.preload_act_table(ACT.Sqrt)
                with act.Fori(0, 4) as i:
                    def rounded(n):
                        act.wait_ge(sq_ready, SQ[stage] + n + 1 + 8 * i)
                        round_tile(hid[:, ds(8 * i + n, 1), 0, :], tmp2[:, n % 4, :])

                    for n in range(8):
                        c, j = C0[stage] + n // 2, n % 2
                        prep(c, j, (i, 4, 8))
                        if n:
                            rounded(n - 1)
                        act.wait_ge(half_done, halves_before(c, j, (i, 4, 8)) + 1)
                        nc.scalar.activation(tmp[:, n % 4, :], bank_of(stage, n)[:, 0:T], ACT.Relu).then_inc(act_evac, 1)
                    rounded(7)

            def down(stage, names):
                nc.scalar.preload_act_table(ACT.Sqrt)
                with act.Fori(0, 4) as i:
                    for cc in range(4):
                        for j in range(2):
                            prep(C0[stage] + cc, j, (i, 4, 2))
                    for name, dst in names:
                        for j in range(2):
                            act.wait_ge(resid_ready, RT[stage] + j + 1 + 2 * i)
                            g = vec[:, ds(2 * i + VEC[name] + j, 1)]
                            round_tile(dst[:, ds(2 * i + j, 1), 0, :], x[:, ds(2 * i + j, 1), :], g)

            def conv_up(stage, down, conv, norm):
                def step(n, it, i):
                    c, j = C0[stage] + n // 2, n % 2
                    prep(c, j, it)
                    if n == 0:
                        root(norm)
                        nc.scalar.preload_act_table(ACT.Silu)
                    if n >= 3:
                        rounded(n - 3, i)
                    if n >= 2:
                        silu(n - 2, i)
                    tile = 2 * (n // 4) + n % 2 + (NT2 if n % 4 >= 2 else 0)
                    col = VEC[conv] + 3 * tile + 2
                    w = vec[:, ds(col + 12 * i, 1)] if it[1] else vec[:, col:col + 1]
                    act.wait_ge(dve_evac, DE[stage] + n + 1 + 8 * i)
                    if n % 4 >= 2 and n >= 4:
                        act.wait_ge(act_ready, AT[stage] + 2 * (n // 4) + n % 2 - 1 + 4 * i)
                    nc.scalar.activation(tmp[:, n % 4, :], tmp2[:, 2 + n % 2, :], ACT.Copy, scale=w).then_inc(tap_ready, 1)

                def silu(n, i):
                    if n % 4 < 2:
                        act.wait_ge(conv_done, CONV[stage] + n + 1 + 8 * i)
                        nc.scalar.activation(tmp2[:, n % 2, :], tmp[:, n % 4, :], ACT.Silu).then_inc(silu_ready, 1)

                def rounded(n, i):
                    if n % 4 >= 2:
                        t = 2 * (n // 4) + n % 2
                        act.wait_ge(gated_ready, GT[stage] + t + 1 + 4 * i)
                        dst = hid[:, t, 0, :] if isinstance(i, int) else hid[:, ds(4 * i + t, 1), 0, :]
                        round_tile(dst, tmp[:, n % 4, :])

                for n in range(4):
                    step(n, STRAIGHT, 0)
                with act.Fori(0, 5) as i:
                    for n in range(4, 12):
                        step(n, (i, 4, 8), i)
                rounded(42, 0)
                prep(C0[down], 0)
                rounded(43, 0)

            def conv_down(stage, name):
                def rounded(j, it, i):
                    act.wait_ge(dve_evac, DE[stage] + j + 1 + 2 * i)
                    if it[1]:
                        round_tile(act_a[:, ds(2 * i + j, 1), 0, :], x[:, ds(2 * i + j, 1), :],
                                   vec[:, ds(2 * i + VEC[name] + j, 1)])
                    else:
                        round_tile(act_a[:, 6 + j, 0, :], x[:, 6 + j, :], gain(name, 6 + j))

                def body(cc, it, i):
                    last = cc % 4 == 3 and name is not None
                    prep(C0[stage] + cc, 0, it, more=1)
                    if last:
                        rounded(0, it, i)
                        rounded(1, it, i)
                    prep(C0[stage] + cc, 1, it, more=1)

                with act.Fori(0, 3) as i:
                    for cc in range(4):
                        body(cc, (i, 4, 2), i)
                for cc in range(12, 16):
                    if cc == 13:
                        nc.scalar.preload_act_table(ACT.Sqrt)
                    body(cc, STRAIGHT, 3)

            def exps(n, base, logit, prob, nmax, total, scale, slots):
                g = base + n
                act.wait_ge(negmax_ready, g + 1)
                if n >= slots:
                    act.wait_ge(transposed, g - slots + 1)
                for q, cols in ((0, slice(0, 128)), (1, slice(128, 384))):
                    nc.scalar.activation(prob[:, n % slots, cols], logit[:, n % 2, cols], ACT.Exp, bias=nmax[:, n % 2, q:q + 1],
                                         scale=scale, accum_out=total[:, n % slots, q:q + 1]).then_inc(probs_ready, 1)

            def copy_transposed(n, base, probT, slots):
                g = base + n
                act.wait_ge(transposed, g + 1)
                if n >= slots:
                    act.wait_ge(pv_done, g - slots + 1)
                nc.scalar.copy(probT[:, n % slots, :], trans[:, 0:384]).then_inc(probsT_ready, 1)

            nc.scalar.preload_act_table(ACT.Sqrt)
            prep(0, 0, first=True)
            act.wait_ge(vec_landed, 16)
            for k in range(KD):
                if k % 4 == 0:
                    act.wait_ge(x_landed[k // 4], 16)
                round_tile(act_a[:, k, 0, :], x[:, k, :], gain("mix0", k))
            prep(0, 1, first=True)
            prep(1, 0, first=True)
            for k in range(4):
                nc.scalar.activation(tmp[:, k, :], x[:, 4 + k, :], ACT.Square).then_inc(sq_x, 1)

            for s in range(27):
                if s < 16 and s != 1:
                    stage, n = fox_qk(s)
                    prep(C0[stage] + n // 2, n % 2)
                if s == 0:
                    prep(0, 1)
                    act.wait_ge(half_done, 1)
                    nc.scalar.copy(f_q[:, 0, :], bank_of("FQA", 0)[:, 0:T]).then_inc(act_evac, 1)
                    root("mix0")
                if s == 3:
                    for j in range(2):
                        prep(C0["FG"], j)
                if s == 4:
                    act.wait_ge(gate_step, 3)
                    nc.scalar.activation(f_exp[:], f_exp[:], ACT.Exp).then_inc(gate_step, 1)
                    act.wait_ge(gate_step, 4)
                    nc.scalar.activation(f_exp[:], f_exp[:], ACT.Ln, bias=1.0).then_inc(gate_step, 1)
                if s >= 19:
                    act.wait_ge(pv_done, 2 * (s - 19) + 2)
                    round_tile(act_b[:, s - 19, 0, :], bank_of("FPV", s - 19)[:, 0:T])
                if FOX_LAG + 2 <= s < FOX_LAG + 18:
                    copy_transposed(s - FOX_LAG - 2, 0, f_probT, FOX_T)
                if 17 <= s < 24 and s % 2:
                    g = (s - 17) // 2
                    act.wait_ge(half_done, 2 * (C0["FV"] + g) + 2)
                    for t in range(TT):
                        nc.scalar.activation(f_v[:, t, g * CW:(g + 1) * CW], bank_of("FV", 2 * g + t)[:, 0:CW], ACT.Copy,
                                             scale=rstd_of("mix0")[:, T + t:T + t + 1]).then_inc(act_evac, 1)
                if 16 <= s < 23:
                    prep(C0["FV"] + (s - 16) // 2, s % 2)
                elif s == 24:
                    prep(C0["FV"] + 3, 1)
                if FOX_LAG <= s < FOX_LAG + 16:
                    exps(s - FOX_LAG, 0, f_logit, f_prob, neg_max, row_sum, FOX_SCALE, 3)
            residual("FO", "ffn0")
            up("U0")
            down("D0", [("kv", act_b), ("mix1", act_a)])

            for n in range(6):
                prep(C0["KVQ"] + n // 2, n % 2)
                if n == 0:
                    root("mix1")
                if n == 5:
                    root("kv_a")
                if n != 4:
                    m = n if n < 4 else n - 1
                    act.wait_ge(dve_evac, DE["KVQ"] + n + 1)
                    g = gain("kv_a", m) if m < 2 else gain("q_a", m - 2)
                    round_tile(m_act[:, m, 0, :], m_lat[:, m, :], g)
            prep(C0["KB"], 0)
            root("q_a")
            prep(C0["KB"], 1)
            for j in range(2):
                prep(C0["QR"], j)
            for s in range(MLA_H + 5):
                if s < 6:
                    prep(C0["QA"] + s // 2, s % 2)
                if s >= 5:
                    h = s - 5
                    act.wait_ge(pv_done, FOX_H + h + 1)
                    round_tile(act_b[:, h, 0, :], bank_of("MPV", h)[:, 0:T])
                if 3 <= s < MLA_H + 3:
                    copy_transposed(s - 3, FOX_H, m_probT, 2)
                if 1 <= s <= MLA_H:
                    exps(s - 1, FOX_H, m_logit, m_prob, m_nmax, m_sum, MLA_SCALE, 3)
                if s in (2, 3):
                    j = s - 2
                    act.wait_ge(half_done, 2 * C0["VB"] + j + 1)
                    act.wait_ge(rstd_ready, ROOTS.index("kv_a") + 1)
                    for t in range(TT):
                        nc.scalar.activation(m_v[:, t, 512 * j:512 * j + 512], bank_of("VB", 2 * j + t)[:], ACT.Copy,
                                             scale=rstd_of("kv_a")[:, T + t:T + t + 1]).then_inc(act_evac, 1)
            residual("MO", "ffn1")
            act.wait_ge(gains_ready, 2)
            up("U1")
            down("D1", [("x1", act_a)])

            for j in range(2):
                prep(C0["GA"], j)
            act_step = [0]

            def step(last):
                act_step[0] += 1
                last.then_inc(gla_act, 1)

            for n in range(8):
                prep(C0["GQK"] + n // 2, n % 2)
                if n == 0:
                    root("mix2")
                if n == 4:
                    act.wait_ge(gla_dve, 2)
                    step(nc.scalar.activation(g_e[:], g_e[:], ACT.Exp))
                    act.wait_ge(gla_act, 1)
                    step(nc.scalar.activation(g_e[:], g_e[:], ACT.Ln, bias=1.0))
            prep(C0["GV"], 0)
            for g in range(2):
                act.wait_ge(gla_pe, 3 + g)
                hs = slice(2 * g, 2 * g + 2)
                v = score[g][:].rearrange("p (h t) -> p h t", h=2)
                step(nc.scalar.activation(g_eb[:, hs, :], v, ACT.Exp))
                step(nc.scalar.activation(g_ki[:, hs, :], v, ACT.Exp, scale=-1.0))
            for n in range(8):
                c = C0["GV"] + n // 2
                if n == 0:
                    act.wait_ge(rstd_ready, ROOTS.index("mix2") + 1)
                if n % 2:
                    act.wait_ge(half_done, 2 * c + 2)
                    for t in range(TT):
                        nc.scalar.activation(g_v[:, t, (n // 2) * CW:(n // 2 + 1) * CW], bank_of("GV", n - 1 + t)[:, 0:CW], ACT.Copy,
                                             scale=rstd_of("mix2")[:, T + t:T + t + 1]).then_inc(act_evac, 1)
                if n:
                    prep(c, n % 2)
                if n == 1:
                    act.wait_ge(gla_dve, 6)
                    step(nc.scalar.activation(g_kd[:], g_kd[:], ACT.Exp))
                if n == 2:
                    act.wait_ge(rstd_ready, ROOTS.index("final1"))
                    root("final1")
                if n == 6:
                    act.wait_ge(gla_pe, 7)
                    step(nc.scalar.copy(g_kdT[:, 0, :], trans[:]))
            def gate_silu(m):
                act.wait_ge(dve_evac, DE["GG"] + m + 1)
                nc.scalar.activation(g_g[:, m, :], g_g[:, m, :], ACT.Silu).then_inc(silu_ready, 1)

            for n in range(8):
                if n == 0:
                    act.wait_ge(gla_pe, 8)
                    step(nc.scalar.copy(g_kdT[:, 1, :], trans[:]))
                if n < 7:
                    prep(C0["GG"] + n // 2, n % 2)
                if n in (3, 4):
                    for m in range(4 * (n - 3), 4 * (n - 3) + 4):
                        act.wait_ge(gla_pe, 12 + m)
                        if m == 0:
                            act.wait_ge(gla_dve, 9)
                        step(nc.scalar.activation(g_o[:, m, :], gla_bank[m % 4][:, 0:T], ACT.Copy, scale=gain("head", m)))
                        step(nc.scalar.activation(tmp_of(m), gla_bank[m % 4][:, 0:T], ACT.Square))
                if n == 5:
                    act.wait_ge(gla_dve, 24)
                    step(nc.scalar.activation(g_std, g_var, ACT.Sqrt))
                for m in ((0, 1, 2, 3) if n == 5 else (4, 5) if n == 6 else (6,) if n == 7 else ()):
                    gate_silu(m)
                if n == 7:
                    prep(C0["GG"] + 3, 1)
            for m in range(KD):
                if m == 5:
                    gate_silu(7)
                act.wait_ge(gated_ready, GT["gla"] + m + 1)
                round_tile(act_b[:, m, 0, :], g_o[:, m, :])
            residual("GO", "ffn2")

            conv_up("CU0", "CD0", "conv0", "ffn2")
            conv_down("CD0", "mix3")
            for n in range(24):
                c, j = C0["SI"] + n // 2, n % 2
                if n:
                    prep(c, j)
                if n == 0:
                    root("mix3")
                g, part = n // 6, (n % 6) // 2
                m = 2 * g + j
                if part == 0:
                    act.wait_ge(half_done, 2 * c + j + 1)
                    if g:
                        act.wait_ge(dve_evac, DE["SI"] + 4 * (g - 1) + j + 1)
                    nc.scalar.copy(s_c[:, j, :], bank_of("SI", n)[:, 0:T]).then_inc(act_evac, 1)
                if part == 1:
                    act.wait_ge(sc_ready, m + 1)
                    nc.scalar.activation(tmp[:, j, :], tmp2[:, j, :], ACT.Copy,
                                         scale=gain("sc_conv", 3 * m + 2)).then_inc(tap_ready, 1)
                if part == 2:
                    act.wait_ge(dve_evac, DE["SI"] + 4 * g + 2 + j + 1)
                    round_tile(act_b[:, m, 0, :], tmp[:, 2 + j, :])
            residual("SO", "ffn3")
            conv_up("CU1", "CD1", "conv1", "ffn3")
            conv_down("CD1", None)
            for k in range(KD):
                act.wait_ge(dve_evac, DE["CD1"] + k + 1)
                if k == KD - 1:
                    nc.scalar.activation(sqt_x1[:], x[:, k, :], ACT.Square).then_inc(last_sq, 1)
                nc.scalar.activation(tmp_of(k), x[:, k, :], ACT.Copy, scale=gain("final2", k)).then_inc(out_gained, 1)
            root("final2")

        @block.vector
        def _(dve):
            def prep(c, j, it=STRAIGHT, first=False):
                nxt = (c, j) if first else ahead(c, j)
                if nxt is None:
                    return
                nc_, nj = nxt
                dve.wait_ge(w_hi_ready, halves_before(nc_, nj, it) + 1)
                nc.vector.tensor_tensor(split_half(w_lo, nc_, nj), raw_half(nc_, nj), split_half(w_hi, nc_, nj).bitcast(F32),
                                        ALU.subtract).then_inc(w_lo_ready, 1)

            def low_tile(n, dst, src, hi, scale=None, extra=None):
                dve.wait_ge(act_hi_ready, n + 1)
                if scale is None:
                    nc.vector.tensor_tensor(dst, src, hi.bitcast(F32), ALU.subtract).then_inc(act_ready, 1)
                else:
                    nc.vector.scalar_tensor_tensor(out=dst, in0=src, scalar=scale, in1=hi.bitcast(F32), op0=ALU.mult,
                                                   op1=ALU.subtract).then_inc(act_ready, 1)

            def variance(name):
                n, _, _, tok, feats = NORMS[name]
                cols = stat_cols(name)
                dve.wait_ge(stat_done, n + 1)
                if n and name in ROOTS:
                    dve.wait_ge(std_ready, ROOTS.index("mix2" if name == "final1" else name))
                nc.vector.tensor_scalar(var[:, cols], misc[:, cols], 1.0 / feats, EPS, ALU.mult,
                                        ALU.add).then_inc(var_ready, 1)

            def inverse_rms(name):
                n = ROOTS.index(name)
                cols = stat_cols(name)
                dve.wait_ge(std_ready, n + 1)
                nc.vector.reciprocal(rstd_of(name)[:, cols], std[:, cols]).then_inc(rstd_ready, 1)
                dve.wait_ge(rstd_ready, n + 1)

            def norm(name):
                variance(name)
                inverse_rms(name)

            def inverse_square(name):
                variance(name)
                dve.wait_ge(var_ready, NORMS[name][0] + 1)
                link(nc.vector.reciprocal(rstd_of(name)[:, 0:T], var[:, 0:T]))

            own_n = [0]

            def link(last):
                own_n[0] += 1
                last.then_inc(dve_own, 1)
                dve.wait_ge(dve_own, own_n[0])

            def residual(stage, name, at):
                for n in range(8):
                    c, j = C0[stage] + n // 2, n % 2
                    dve.wait_ge(half_done, 2 * c + j + 1)
                    nc.vector.tensor_tensor(x[:, n, :], bank_of(stage, n)[:, 0:T], x[:, n, :], ALU.add).then_inc(dve_evac, 1)
                    prep(c, j)
                    if name is not None:
                        low_tile(AT[at] + n, act_a[:, n, 1, :], x[:, n, :], act_a[:, n, 0, :], gain(name, n))

            def up(stage):
                with dve.Fori(0, 4) as i:
                    def low(n):
                        t = ds(8 * i + n, 1)
                        low_tile(AT[stage] + n + 8 * i, hid[:, t, 1, :], tmp2[:, n % 4, :], hid[:, t, 0, :])

                    for n in range(8):
                        prep(C0[stage] + n // 2, n % 2, (i, 4, 8))
                        if n:
                            low(n - 1)
                        dve.wait_ge(act_evac, AE[stage] + n + 1 + 8 * i)
                        nc.vector.tensor_tensor(tmp2[:, n % 4, :], tmp[:, n % 4, :], tmp[:, n % 4, :],
                                                ALU.mult).then_inc(sq_ready, 1)
                    low(7)

            def down(stage, norm_name, names, at):
                inverse_square(norm_name)
                with dve.Fori(0, 4) as i:
                    it = (i, 4, 2)
                    for cc in range(4):
                        for j in range(2):
                            c = C0[stage] + cc
                            prep(c, j, it)
                            if cc == 3:
                                dve.wait_ge(half_done, halves_before(c, j, it) + 1)
                                nc.vector.tensor_tensor(tmp[:, j, :], bank_of(stage, j)[:, 0:T], rstd_of(norm_name)[:, 0:T],
                                                        ALU.mult).then_inc(dve_evac, 1)
                                dve.wait_ge(dve_evac, DE[stage] + j + 1 + 2 * i)
                                t = ds(2 * i + j, 1)
                                nc.vector.tensor_tensor(x[:, t, :], x[:, t, :], tmp[:, j, :], ALU.add).then_inc(resid_ready, 1)
                    for m, (name, dst) in enumerate(names):
                        for j in range(2):
                            t = ds(2 * i + j, 1)
                            low_tile(AT[at] + 2 * m + j + 2 * len(names) * i, dst[:, t, 1, :], x[:, t, :],
                                     dst[:, t, 0, :], vec[:, ds(2 * i + VEC[name] + j, 1)])

            def conv_up(stage, conv, norm_name):
                def step(n, it, i):
                    c, j = C0[stage] + n // 2, n % 2
                    if n == 0:
                        prep(c, j, it)
                        norm(norm_name)
                    dve.wait_ge(half_done, halves_before(c, j, it) + 1)
                    if n >= 2:
                        dve.wait_ge(conv_done, CONV[stage] + n - 1 + 8 * i)
                    nc.vector.tensor_tensor(tmp2[:, 2 + n % 2, :], bank_of(stage, n)[:, 0:T], rstd_of(norm_name)[:, 0:T],
                                            ALU.mult).then_inc(dve_evac, 1)
                    if n:
                        taps(n - 1, i)
                        prep(c, j, it)

                def taps(n, i):
                    tile = 2 * (n // 4) + n % 2 + (NT2 if n % 4 >= 2 else 0)
                    col = VEC[conv] + 3 * tile
                    w0, w1 = (vec[:, col + k:col + k + 1] if isinstance(i, int) else vec[:, ds(col + k + 12 * i, 1)] for k in range(2))
                    y, u = tmp[:, n % 4, :], tmp2[:, 2 + n % 2, :]
                    dve.wait_ge(tap_ready, CV[stage] + n + 1 + 8 * i)
                    nc.vector.scalar_tensor_tensor(out=y[:, 1:T], in0=u[:, 0:T - 1], scalar=w1, in1=y[:, 1:T],
                                                   op0=ALU.mult, op1=ALU.add).then_inc(tap_mid, 1)
                    dve.wait_ge(tap_mid, CV[stage] + n + 1 + 8 * i)
                    nc.vector.scalar_tensor_tensor(out=y[:, 2:T], in0=u[:, 0:T - 2], scalar=w0, in1=y[:, 2:T],
                                                   op0=ALU.mult, op1=ALU.add).then_inc(conv_done, 1)

                for n in range(4):
                    step(n, STRAIGHT, 0)
                with dve.Fori(0, 5) as i:
                    for n in range(4, 12):
                        step(n, (i, 4, 8), i)
                taps(43, 0)

            def conv_down(stage, name, at):
                def body(cc, it, i):
                    c = C0[stage] + cc
                    for j in range(2):
                        prep(c, j, it)
                        if cc % 4 == 3:
                            dve.wait_ge(half_done, halves_before(c, j, it) + 1)
                            xt = x[:, ds(2 * i + j, 1), :] if it[1] else x[:, 6 + j, :]
                            ps = bank_of(stage, j)[:, 0:T]
                            nc.vector.tensor_tensor(xt, ps, xt, ALU.add).then_inc(dve_evac, 1)
                    if cc % 4 == 3 and name is not None:
                        for j in range(2):
                            if it[1]:
                                t = ds(2 * i + j, 1)
                                low_tile(AT[at] + j + 2 * i, act_a[:, t, 1, :], x[:, t, :], act_a[:, t, 0, :],
                                         vec[:, ds(2 * i + VEC[name] + j, 1)])
                            else:
                                low_tile(AT[at] + 6 + j, act_a[:, 6 + j, 1, :], x[:, 6 + j, :], act_a[:, 6 + j, 0, :],
                                         gain(name, 6 + j))

                with dve.Fori(0, 3) as i:
                    for cc in range(4):
                        body(cc, (i, 4, 2), i)
                for cc in range(12, 16):
                    body(cc, STRAIGHT, 3)

            def scaled(stage, n, half, dst, norm_name, rows=P):
                dve.wait_ge(half_done, half)
                nc.vector.tensor_tensor(dst, bank_of(stage, n)[0:rows, 0:T], rstd_of(norm_name)[0:rows, 0:T],
                                        ALU.mult).then_inc(dve_evac, 1)

            def maxima(n, base, logit, rmax, nmax, scale):
                g = base + n
                dve.wait_ge(scores_done, g + 1)
                s = score[n % 2]
                nc.vector.tensor_tensor_reduce(logit[:, n % 2, 0:128], s[:, 0:128], mask[:, 128:256], 1.0, -3.0e38, ALU.add,
                                               ALU.max, rmax[:, n % 2, 0:1]).then_inc(logits_ready, 1)
                nc.vector.tensor_tensor_reduce(logit[:, n % 2, 128:384], s[:, 128:384], mask, 1.0, -3.0e38, ALU.add,
                                               ALU.max, rmax[:, n % 2, 1:2]).then_inc(logits_ready, 1)
                dve.wait_ge(logits_ready, 2 * g + 2)
                nc.vector.tensor_scalar(nmax[:, n % 2, :], rmax[:, n % 2, :], -scale, None, ALU.mult).then_inc(negmax_ready, 1)

            def norm_probs(n, base, prob, total, inv, slots):
                g = base + n
                dve.wait_ge(probs_ready, 2 * g + 2)
                nc.vector.reciprocal(inv[:, n % slots, :], total[:, n % slots, :]).then_inc(invsum_ready, 1)
                dve.wait_ge(invsum_ready, g + 1)
                for q, cols in ((0, slice(0, 128)), (1, slice(128, 384))):
                    nc.vector.tensor_scalar(prob[:, n % slots, cols], prob[:, n % slots, cols], inv[:, n % slots, q:q + 1], None,
                                            ALU.mult).then_inc(probs_normed, 1)

            prep(0, 0, first=True)
            dve.wait_ge(vec_landed, 16)
            for k in range(KD):
                if k % 4 == 0:
                    dve.wait_ge(x_landed[k // 4], 16)
                low_tile(AT["x"] + k, act_a[:, k, 1, :], x[:, k, :], act_a[:, k, 0, :], gain("mix0", k))
            prep(0, 1, first=True)
            prep(1, 0, first=True)
            first = vec[:, VEC["final1"]:VEC["final1"] + KD]
            nc.vector.tensor_tensor(vec[:, VEC["x1"]:VEC["x1"] + KD], first, vec[:, VEC["mix2"]:VEC["mix2"] + KD],
                                    ALU.mult).then_inc(gains_ready, 1)
            nc.vector.tensor_tensor(vec[:, VEC["final1_sq"]:VEC["final1_sq"] + KD], first, first, ALU.mult).then_inc(gains_ready, 1)

            link(nc.vector.memset(f_cum[:].bitcast(F32), 0.0))
            for s in range(27):
                if s == 0:
                    prep(0, 0)
                    prep(0, 1)
                    norm("mix0")
                if s == 5:
                    dve.wait_ge(con_landed, 16)
                    nc.vector.tensor_copy(f_sel[:], pick.unsqueeze(2).broadcast_to([P, FOX_H, P])).then_inc(sel_ready, 1)
                if s == 4:
                    c = C0["FG"]
                    dve.wait_ge(half_done, 2 * c + 1)
                    dve.wait_ge(fox_small_landed, 16)
                    nc.vector.tensor_tensor(f_z[:], bank_of("FG", 0)[0:FOX_H, 0:T], rstd_of("mix0")[0:FOX_H, 0:T],
                                            ALU.mult).then_inc(dve_evac, 1)
                    dve.wait_ge(dve_evac, DE["FG"] + 1)
                    nc.vector.tensor_scalar(f_z[:], f_z[:], f_bias[:], None, ALU.add).then_inc(gate_step, 2)
                    dve.wait_ge(gate_step, 2)
                    nc.vector.scalar_tensor_tensor(out=f_exp[:], in0=f_z[:], scalar=-1.0, in1=f_z[:], op0=ALU.mult,
                                                   op1=ALU.min).then_inc(gate_step, 1)
                if s == 5:
                    dve.wait_ge(gate_step, 5)
                    nc.vector.scalar_tensor_tensor(out=f_z[:], in0=f_z[:], scalar=0.0, in1=f_exp[:], op0=ALU.min,
                                                   op1=ALU.subtract).then_inc(gate_step, 1)
                if s == 7:
                    dve.wait_ge(cum_done, 1)
                    nc.vector.tensor_copy(f_ls[:].rearrange("p t h -> p (t h)"), trans[:, 0:TT * FOX_H]).then_inc(gate_step, 1)
                if s == 8:
                    dve.wait_ge(cum_done, 2)
                    for row in (0, 64):
                        nc.vector.tensor_copy(f_cum[row:row + 16, :], trans[0:16, 0:T]).then_inc(cum_ready, 1)
                    dve.wait_ge(cum_ready, 1)
                    for row in (32, 96):
                        nc.vector.tensor_tensor(f_cum[row:row + 16, :], trans[0:16, 0:T], f_cum[0:16, :].bitcast(F32),
                                                ALU.subtract).then_inc(cum_ready, 1)
                if s < 16:
                    stage, n = fox_qk(s)
                    c, j = C0[stage] + n // 2, n % 2
                    dst = (f_q, f_k)[s // 2 % 2][:, 2 * (s // 4) + j, :]
                    if s == 0:
                        dve.wait_ge(act_evac, AE["FQA"] + 1)
                        nc.vector.tensor_tensor(dst, dst, rstd_of("mix0")[:, 0:T], ALU.mult).then_inc(dve_evac, 1)
                    else:
                        scaled(stage, n, 2 * c + j + 1, dst, "mix0")
                if s == 24:
                    norm_probs(15, 0, f_prob, row_sum, inv_sum, 3)
                if s >= 19:
                    low_tile(AT["fctx"] + s - 19, act_b[:, s - 19, 1, :], bank_of("FPV", s - 19)[:, 0:T], act_b[:, s - 19, 0, :])
                if FOX_LAG <= s < 24:
                    maxima(s - FOX_LAG, 0, f_logit, row_max, neg_max, FOX_SCALE)
                if FOX_LAG + 1 <= s < 24:
                    norm_probs(s - FOX_LAG - 1, 0, f_prob, row_sum, inv_sum, 3)
                if 1 < s < 16:
                    prep(c, j)
                elif 16 <= s < 23:
                    prep(C0["FV"] + (s - 16) // 2, s % 2)
                elif s == 24:
                    prep(C0["FV"] + 3, 1)
                if s == 3:
                    for j in range(2):
                        prep(C0["FG"], j)
            residual("FO", "ffn0", "FO")
            up("U0")
            down("D0", "ffn0", [("kv", act_b), ("mix1", act_a)], "D0")

            def key_scaled(n):
                if n % 4 < 3:
                    dve.wait_ge(key_done, 3 * (n // 4) + n % 4 + 1)
                scaled("KB", n, 2 * C0["KB"] + (n // 4 if n % 4 < 3 else n // 4 + 1), m_k[:, n, :], "kv_a")

            for n in range(6):
                c, j = C0["KVQ"] + n // 2, n % 2
                if n == 5:
                    norm("kv_a")
                if n == 0:
                    prep(c, j)
                    norm("mix1")
                m = n if n < 4 else n - 1
                scaled("KVQ", n, 2 * c + j + 1, m_kr_raw[:] if n == 4 else m_lat[:, m, :], "mix1")
                if n == 5:
                    for h in range(2):
                        key_scaled(h)
                if n:
                    prep(c, j)
                if n != 4:
                    g = gain("kv_a", m) if m < 2 else gain("q_a", m - 2)
                    low_tile(AT["lat"] + m, m_act[:, m, 1, :], m_lat[:, m, :], m_act[:, m, 0, :], g)
            for n in range(2, 8):
                if n == 4:
                    prep(C0["KB"], 0)
                    variance("q_a")
                key_scaled(n)
            inverse_rms("q_a")
            prep(C0["KB"], 1)

            def rope(n):
                dst = m_kr[:] if n == 0 else m_qr[:, n - 1, :]
                dve.wait_ge(rot_done, n + 1)
                nc.vector.tensor_tensor(dst, rot_place[n], sin_t, ALU.mult).then_inc(rope_step, 1)
                dve.wait_ge(rope_step, 2 * n + 1)
                dve.wait_ge(rope_cos, n + 1)
                nc.vector.tensor_tensor(dst, dst, m_lat[:, n, :], ALU.add).then_inc(rope_step, 1)

            for j in range(2):
                prep(C0["QR"], j)
                for n in range(2):
                    scaled("QR", 2 * j + n, 2 * C0["QR"] + j + 1, m_qr_raw[:, 2 * j + n, :], "q_a")
            for s in range(MLA_H + 5):
                if s == 0:
                    for n in range(3):
                        rope(n)
                if s < 2 or 4 <= s < 6:
                    stage, j = (("QA", s) if s < 2 else ("QN", s - 4))
                    for n in range(2):
                        scaled(stage, 2 * j + n, 2 * C0[stage] + j + 1, m_q[:, 2 * j + n + (0 if s < 2 else 4), :], "q_a")
                if s == 0:
                    rope(3)
                    rope(4)
                pair = s % 2 and s < MLA_H
                if pair:
                    maxima(s - 1, FOX_H, m_logit, m_max, m_nmax, MLA_SCALE)
                if 2 <= s < MLA_H + 2:
                    norm_probs(s - 2, FOX_H, m_prob, m_sum, m_inv, 3)
                if pair:
                    maxima(s, FOX_H, m_logit, m_max, m_nmax, MLA_SCALE)
                if s >= 5:
                    low_tile(AT["mctx"] + s - 5, act_b[:, s - 5, 1, :], bank_of("MPV", s - 5)[:, 0:T], act_b[:, s - 5, 0, :])
                if s < 6:
                    prep(C0["QA"] + s // 2, s % 2)
            residual("MO", "ffn1", "MO")
            dve.wait_ge(gains_ready, 2)
            up("U1")
            down("D1", "ffn1", [("x1", act_a)], "x1")

            for j in range(2):
                prep(C0["GA"], j)
            prep(C0["GQK"], 0)
            variance("final1")
            dve.wait_ge(var_ready, NORMS["final1"][0] + 1)
            link(nc.vector.tensor_scalar(var_x1[:], var[:], EPS, None, ALU.mult))
            dve.wait_ge(stat_done, NORMS["mix2"][0] + 1)
            nc.vector.scalar_tensor_tensor(out=var_x1[:], in0=trans[:, 0:T + TT], scalar=1.0 / D, in1=var_x1[:], op0=ALU.mult,
                                           op1=ALU.add).then_inc(var_ready, 1)
            inverse_rms("mix2")
            scaled("GA", 0, 2 * C0["GA"] + 2, g_aT[:], "mix2", rows=GATE_RANK)
            dve_step = [0]

            def step(last, wait=False):
                dve_step[0] += 1
                last.then_inc(gla_dve, 1)
                if wait:
                    dve.wait_ge(gla_dve, dve_step[0])

            def bcum(g):
                return score[g][:].rearrange("p (c s) -> p c s", s=GLA_C)

            for n in range(8):
                c, j = C0["GQK"] + n // 2, n % 2
                if n:
                    prep(c, j)
                scaled("GQK", n, 2 * c + j + 1, (g_q, g_k)[n // 4][:, n % 4, :], "mix2")
                if n == 3:
                    for t in range(TT):
                        dve.wait_ge(gla_pe, 1 + t)
                        dve.wait_ge(gla_small_landed, 32)
                        link(nc.vector.tensor_tensor(g_z[:, t, :], score[t][:], g_bias[:], ALU.add))
                        step(nc.vector.scalar_tensor_tensor(out=g_e[:, t, :], in0=g_z[:, t, :], scalar=-1.0, in1=g_z[:, t, :],
                                                            op0=ALU.mult, op1=ALU.min))
                if n == 6:
                    dve.wait_ge(gla_act, 2)
                    for t in range(TT):
                        step(nc.vector.scalar_tensor_tensor(out=g_z[:, t, :], in0=g_z[:, t, :], scalar=0.0, in1=g_e[:, t, :],
                                                            op0=ALU.min, op1=ALU.subtract))
            for n in range(8):
                prep(C0["GV"] + n // 2, n % 2)
                if n == 0:
                    for g in range(2):
                        dve.wait_ge(gla_act, 4 + 2 * g)
                        hs = slice(2 * g, 2 * g + 2)
                        cum = bcum(g)
                        link(nc.vector.tensor_copy(g_last[:, 8 * g:8 * g + 8], cum[:, :, GLA_C - 1:GLA_C].squeeze(2)))
                        step(nc.vector.tensor_tensor(
                            g_kd[:, hs, :].rearrange("p h (c s) -> p (h c) s", s=GLA_C),
                            g_last[:, 8 * g:8 * g + 8].unsqueeze(2).broadcast_to([P, 8, GLA_C]), cum, ALU.subtract))
                if n == 1:
                    dve.wait_ge(dve_evac, DE["GQK"] + 8)
                    step(nc.vector.tensor_tensor(g_ki[:], g_ki[:], g_k[:], ALU.mult))
                if n == 2:
                    step(nc.vector.scalar_tensor_tensor(out=g_qi[:], in0=g_q[:], scalar=GLA_SCALE, in1=g_eb[:],
                                                        op0=ALU.mult, op1=ALU.mult))
                if n == 3:
                    dve.wait_ge(gla_act, 7)
                    step(nc.vector.tensor_tensor(g_kd[:], g_kd[:], g_k[:], ALU.mult))
                if n == 4:
                    inverse_rms("final1")
                if n >= 5:
                    for k in ((0, 1, 2), (3, 4, 5), (6, 7))[n - 5]:
                        nc.vector.scalar_tensor_tensor(out=x[:, k, :], in0=x[:, k, :], scalar=gain("final1", k),
                                                       in1=rstd_of("final1")[:, 0:T], op0=ALU.mult,
                                                       op1=ALU.mult).then_inc(resid_ready, 1)
                if n == 6:
                    dve.wait_ge(gla_zeroed, 1)
                    for t in range(TT):
                        dve.wait_ge(gla_pe, 5 + t)
                        step(nc.vector.copy_predicated(
                            g_sT[:, t, :].rearrange("p (h s) -> p h s", h=GLA_H),
                            chunk_mask.unsqueeze(1).broadcast_to([P, GLA_H, P]),
                            score[t][:].rearrange("p (h s) -> p h s", h=GLA_H)))
            def head_norm(m):
                dve.wait_ge(gla_pe, 21 + m // 4)
                if m < KD - 1:
                    dve.wait_ge(head_gated, m + 1)
                nc.vector.tensor_tensor(g_o[:, m, :], g_o[:, m, :], score[m // 4][:, (m // 2 % 2) * T:(m // 2 % 2) * T + T],
                                        ALU.mult).then_inc(gated_ready, 1)

            def head_low(m):
                low_tile(AT["gla"] + m, act_b[:, m, 1, :], g_o[:, m, :], act_b[:, m, 0, :])

            for n in range(8):
                c, j = C0["GG"] + n // 2, n % 2
                for m in ((0, 1) if n == 1 else (2,) if n == 2 else ()):
                    dve.wait_ge(gla_pe, 9 + m)
                    if m:
                        dve.wait_ge(gla_dve, 11 + 4 * m)
                    for h in range(GLA_H):
                        if m == 0:
                            step(nc.vector.tensor_copy(g_s[:, 0, h, :], state_place(m, h)))
                        else:
                            decay = g_eb[:, h, m * GLA_C + GLA_C - 1:m * GLA_C + GLA_C]
                            step(nc.vector.scalar_tensor_tensor(out=g_s[:, m, h, :], in0=g_s[:, m - 1, h, :], scalar=decay,
                                                                in1=state_place(m, h), op0=ALU.mult, op1=ALU.add))
                if n < 7:
                    prep(c, j)
                if n == 5:
                    dve.wait_ge(gla_act, 26)
                    step(nc.vector.reciprocal(g_rec, g_std))
                if n == 7:
                    for m in range(5):
                        head_norm(m)
                        if m:
                            head_low(m - 1)
                scaled("GG", n, 2 * c + j + 1, g_g[:, n, :], "mix2")
                if n == 4:
                    dve.wait_ge(gla_pe, 20)
                    step(nc.vector.tensor_scalar(g_var, misc[0:GLA_H, 0:T], 1.0 / GLA_DV, EPS, ALU.mult, ALU.add))
            head_norm(5)
            head_low(4)
            head_norm(6)
            dve.wait_ge(silu_ready, SL["GG"] + KD)
            link(nc.vector.tensor_tensor(g_o[:, 7, :], g_o[:, 7, :], g_g[:, 7, :], ALU.mult))
            head_low(5)
            head_norm(7)
            head_low(6)
            head_low(7)
            prep(C0["GG"] + 3, 1)
            dve.wait_ge(resid_ready, RT["x1"] + KD)
            residual("GO", "ffn2", "GO")

            conv_up("CU0", "conv0", "ffn2")
            conv_down("CD0", "mix3", "CD0")
            for n in range(24):
                c, j = C0["SI"] + n // 2, n % 2
                if n // 2 % 3 == 0:
                    prep(c, j)
                if n == 0:
                    norm("mix3")
                    link(nc.vector.tensor_tensor(rstd_sq[:], rstd_of("mix3")[:, 0:T], rstd_of("mix3")[:, 0:T], ALU.mult))
                g, part = n // 6, (n % 6) // 2
                m = 2 * g + j
                ps = bank_of("SI", n)[:, 0:T]
                if part == 1:
                    dve.wait_ge(act_evac, AE["SI"] + m + 1)
                    dve.wait_ge(half_done, 2 * c + j + 1)
                    nc.vector.tensor_tensor(tmp2[:, 2 + j, :], ps, s_c[:, j, :], ALU.mult).then_inc(dve_evac, 1)
                    dve.wait_ge(dve_evac, DE["SI"] + 4 * g + j + 1)
                    nc.vector.tensor_tensor(tmp2[:, j, :], tmp2[:, 2 + j, :], rstd_sq[:], ALU.mult).then_inc(sc_ready, 1)
                    prep(c, j)
                    y, v = tmp[:, j, :], tmp2[:, j, :]
                    dve.wait_ge(tap_ready, CV["SI"] + m + 1)
                    nc.vector.scalar_tensor_tensor(out=y[:, 1:T], in0=v[:, 0:T - 1], scalar=gain("sc_conv", 3 * m + 1),
                                                   in1=y[:, 1:T], op0=ALU.mult, op1=ALU.add).then_inc(tap_mid, 1)
                    dve.wait_ge(tap_mid, CV["SI"] + m + 1)
                    link(nc.vector.scalar_tensor_tensor(out=y[:, 2:T], in0=v[:, 0:T - 2], scalar=gain("sc_conv", 3 * m),
                                                        in1=y[:, 2:T], op0=ALU.mult, op1=ALU.add))
                    link(nc.vector.tensor_tensor(y, y, rstd_of("mix3")[:, 0:T], ALU.mult))
                if part == 2:
                    dve.wait_ge(half_done, 2 * c + j + 1)
                    if g:
                        dve.wait_ge(act_ready, AT["sc"] + m - 2 + 1)
                    nc.vector.tensor_tensor(tmp[:, 2 + j, :], ps, tmp[:, j, :], ALU.mult).then_inc(dve_evac, 1)
                    if n < 23:
                        prep(c, j)
                    low_tile(AT["sc"] + m, act_b[:, m, 1, :], tmp[:, 2 + j, :], act_b[:, m, 0, :])
                    if n == 23:
                        prep(c, j)
            residual("SO", "ffn3", "SO")
            conv_up("CU1", "conv1", "ffn3")
            conv_down("CD1", None, None)
            norm("final2")
            dve.wait_ge(spread_done, 1)
            for k in range(0, KD, 2):
                dve.wait_ge(out_gained, k + 2)
                nc.vector.tensor_tensor(x[:, k:k + 2, :], (tmp, tmp2)[k // 4][:, k % 4:k % 4 + 2, :],
                                        trans[:, 0:T].unsqueeze(1).broadcast_to([P, 2, T]), ALU.mult).then_inc(resid_ready, 2)


_WEIGHTS = ["fox_w_in", "fox_b_f", "fox_w_out", "mla_w_kv_a", "mla_w_kv_b", "mla_w_q_a", "mla_w_q_b", "mla_w_out",
            "ffn_w_up", "ffn_w_down", "gla_w_in_2", "gla_w_gate_up_2", "gla_b_gate_2", "gla_w_out_2", "sc_w_in_2",
            "sc_w_out_2", "ffn_w_up_2", "ffn_w_down_2"]


def kernel(**inputs):
    import concourse.bacc as bacc
    from concourse.bass_utils import run_bass_kernel_spmd

    a = {name: np.ascontiguousarray(v) for name, v in inputs.items()}
    tiles = lambda v: v.reshape(-1, P).T
    taps = lambda v: v.reshape(-1, P, 3).transpose(1, 0, 2).reshape(P, -1)
    vec = np.concatenate(
        [tiles(v) for v in (a["norm_mix_g"][0], a["norm_ffn_g"][0], a["kv_norm_g"], a["norm_mix_g"][1], a["norm_ffn_g"][1],
                            a["final_norm_g"], a["norm_mix_g_2"][0], a["norm_ffn_g_2"][0], a["norm_mix_g_2"][1],
                            a["norm_ffn_g_2"][1], a["final_norm_g_2"], a["mla_kv_a_norm_g"], a["mla_q_a_norm_g"][0],
                            a["gla_head_norm_g_2"][0])]
        + [taps(a["sc_conv_w_2"][0]), taps(a["ffn_conv_w_2"][0]), taps(a["ffn_conv_w_2"][1])], axis=1)
    arrays = {name: a[name] for name in _WEIGHTS}
    arrays.update(xT=np.ascontiguousarray(a["x"][0].T), vec=np.ascontiguousarray(vec), con=shape_constants())
    nc = bacc.Bacc("TRN2", target_bir_lowering=False, num_devices=1)
    io = {name: nc.dram_tensor(f"in_{name}", v.shape, mybir.dt.from_np(v.dtype), kind="ExternalInput").ap()
          for name, v in arrays.items()}
    io["out"] = nc.dram_tensor("outT", (D, T), F32, kind="ExternalOutput").ap()
    build(nc, io)
    r = run_bass_kernel_spmd(nc, [{f"in_{name}": v for name, v in arrays.items()}], core_ids=[0])
    return np.ascontiguousarray(r.results[0]["outT"].T).reshape(1, T, D)
```
